# Optimizing a Trainium2 kernel written in Bass

```python
import math
import jax
import jax.numpy as jnp
from jax import lax
import numpy as np

D_MODEL = 1024
BATCH = 1
SEQ = 512
DEPTH = 1
DEC_BATCH = 8
DEC_SEQ = 1
PAST_LEN = 4096
PAGE_SIZE = 128

N_META = 16
D_S5 = D_MODEL // 2
S5_GROUP = 16
N_S5_GROUPS = D_S5 // S5_GROUP
S5_STATE = 64
D_RET = D_MODEL - D_S5
N_RET_HEADS = 8
RET_HEAD_DIM = D_RET // N_RET_HEADS
RET_CHUNK = 128
ROPE_BASE = 10000.0
D_IN = D_S5 + 4 * D_RET
N_EXPERTS = 64
TOP_K = 8
N_EXPERT_GROUPS = 8
TOPK_GROUPS = 4
D_EXPERT = D_MODEL // 4
ROUTED_SCALE = 2.5
EPS = 1e-6

kernel_name = 'hymba_s5_retnet_moe_step'

def rmsnorm(x, g):
    xf = x.astype(jnp.float32)
    y = xf * lax.rsqrt(jnp.mean(xf * xf, axis=-1, keepdims=True) + EPS)
    return (y * g.astype(jnp.float32)).astype(x.dtype)

def rotary(x, pos):
    half = x.shape[-1] // 2
    inv_freq = ROPE_BASE ** (-jnp.arange(half, dtype=jnp.float32) / half)
    ang = pos.astype(jnp.float32)[:, None] * inv_freq[None, :]
    cos = jnp.cos(ang)[None, :, None, :]
    sin = jnp.sin(ang)[None, :, None, :]
    xf = x.astype(jnp.float32)
    x1, x2 = xf[..., :half], xf[..., half:]
    return jnp.concatenate([x1 * cos - x2 * sin, x1 * sin + x2 * cos], axis=-1)

def retention_log_decay():
    return jnp.log1p(-jnp.exp2(-5.0 - jnp.arange(N_RET_HEADS, dtype=jnp.float32)))

def retention_chunk(q, k, v, state, log_g):
    c = q.shape[2]
    n = jnp.arange(c, dtype=jnp.float32)
    diff = n[:, None] - n[None, :]
    decay = jnp.where(diff[None] >= 0.0,
                      jnp.exp(log_g[:, None, None] * jnp.maximum(diff, 0.0)[None]), 0.0)
    scores = jnp.einsum('bhnd,bhmd->bhnm', q, k) * decay[None]
    inner = jnp.einsum('bhnm,bhmv->bhnv', scores, v)
    q_dec = q * jnp.exp(log_g[:, None] * (n + 1.0)[None])[None, :, :, None]
    cross = jnp.einsum('bhnd,bhdv->bhnv', q_dec, state)
    k_dec = k * jnp.exp(log_g[:, None] * (c - 1.0 - n)[None])[None, :, :, None]
    new_state = (jnp.exp(log_g * c)[None, :, None, None] * state
                 + jnp.einsum('bhmd,bhmv->bhdv', k_dec, v))
    return inner + cross, new_state

def retention(q, k, v, state, lead):
    log_g = retention_log_decay()
    o0, state = retention_chunk(q[:, :, :lead], k[:, :, :lead], v[:, :, :lead], state, log_g)
    b, h, length, dk = q.shape
    if length == lead:
        return o0, state
    dv = v.shape[-1]
    nc = (length - lead) // RET_CHUNK

    def to_chunks(t):
        return jnp.moveaxis(t[:, :, lead:].reshape(b, h, nc, RET_CHUNK, t.shape[-1]), 2, 0)

    def step(s, qkv):
        qc, kc, vc = qkv
        o, s = retention_chunk(qc, kc, vc, s, log_g)
        return s, o

    state, oc = lax.scan(step, state, (to_chunks(q), to_chunks(k), to_chunks(v)))
    oc = jnp.moveaxis(oc, 0, 2).reshape(b, h, nc * RET_CHUNK, dv)
    return jnp.concatenate([o0, oc], axis=2), state

def _complex_affine_combine(e1, e2):
    a1r, a1i, b1r, b1i = e1
    a2r, a2i, b2r, b2i = e2
    return (a2r * a1r - a2i * a1i,
            a2r * a1i + a2i * a1r,
            a2r * b1r - a2i * b1i + b2r,
            a2r * b1i + a2i * b1r + b2i)

def s5_scan(u, lam_re, lam_im, log_dt, b_re, b_im, c_re, c_im, d_skip, x0_re, x0_im):
    f32 = jnp.float32
    lam_re, lam_im = lam_re.astype(f32), lam_im.astype(f32)
    dt = jnp.exp(log_dt.astype(f32))[:, None]
    mag = jnp.exp(lam_re * dt)
    abar_re, abar_im = mag * jnp.cos(lam_im * dt), mag * jnp.sin(lam_im * dt)
    num_re, num_im = abar_re - 1.0, abar_im
    den = lam_re * lam_re + lam_im * lam_im
    f_re = (num_re * lam_re + num_im * lam_im) / den
    f_im = (num_im * lam_re - num_re * lam_im) / den
    b_re, b_im = b_re.astype(f32), b_im.astype(f32)
    bbar_re = f_re[..., None] * b_re - f_im[..., None] * b_im
    bbar_im = f_re[..., None] * b_im + f_im[..., None] * b_re
    bu_re = jnp.einsum('blgh,gph->blgp', u, bbar_re)
    bu_im = jnp.einsum('blgh,gph->blgp', u, bbar_im)
    a_re = jnp.broadcast_to(abar_re, bu_re.shape)
    a_im = jnp.broadcast_to(abar_im, bu_re.shape)
    acum_re, acum_im, h_re, h_im = lax.associative_scan(
        _complex_affine_combine, (a_re, a_im, bu_re, bu_im), axis=1)
    x0_re, x0_im = x0_re.astype(f32)[:, None], x0_im.astype(f32)[:, None]
    xs_re = acum_re * x0_re - acum_im * x0_im + h_re
    xs_im = acum_re * x0_im + acum_im * x0_re + h_im
    y = (jnp.einsum('gnp,blgp->blgn', c_re.astype(f32), xs_re)
         - jnp.einsum('gnp,blgp->blgn', c_im.astype(f32), xs_im)
         + d_skip.astype(f32)[None, None] * u)
    return y, xs_re[:, -1], xs_im[:, -1]

def moe(h, w_router, router_bias, w_gate_e, w_up_e, w_down_e, w_gate_sh, w_up_sh, w_down_sh):
    t = h.shape[0]
    scores = jax.nn.sigmoid((h @ w_router).astype(jnp.float32))
    sel = scores + router_bias.astype(jnp.float32)[None]
    grp = sel.reshape(t, N_EXPERT_GROUPS, N_EXPERTS // N_EXPERT_GROUPS)
    group_score = jnp.sum(lax.top_k(grp, 2)[0], axis=-1)
    _, gidx = lax.top_k(group_score, TOPK_GROUPS)
    gmask = jnp.sum(jax.nn.one_hot(gidx, N_EXPERT_GROUPS, dtype=jnp.float32), axis=1) > 0.0
    emask = jnp.repeat(gmask, N_EXPERTS // N_EXPERT_GROUPS, axis=1)
    _, eidx = lax.top_k(jnp.where(emask, sel, -jnp.inf), TOP_K)
    w = jnp.take_along_axis(scores, eidx, axis=1)
    w = w / jnp.sum(w, axis=-1, keepdims=True) * ROUTED_SCALE
    gates = jnp.einsum('tk,tke->te', w, jax.nn.one_hot(eidx, N_EXPERTS, dtype=jnp.float32)).astype(h.dtype)
    hg = jnp.einsum('td,edf->tef', h, w_gate_e)
    hu = jnp.einsum('td,edf->tef', h, w_up_e)
    act = jax.nn.silu(hg) * hu * gates[..., None]
    routed = jnp.einsum('tef,efd->td', act, w_down_e)
    shared = (jax.nn.silu(h @ w_gate_sh) * (h @ w_up_sh)) @ w_down_sh
    return routed + shared

def decoder_layer(x, pos, lead, s5_x0_re, s5_x0_im, ret_s0, map_rows,
                  norm1, w_in, s5_lam_re, s5_lam_im, s5_log_dt, s5_b_re, s5_b_im,
                  s5_c_re, s5_c_im, s5_d, s5_w_glu, s5_norm, ret_norm, w_out, norm2,
                  w_router, router_bias, w_gate_e, w_up_e, w_down_e, w_gate_sh, w_up_sh, w_down_sh):
    b, length, _ = x.shape
    h = rmsnorm(x, norm1)
    proj = h @ w_in
    u, q, k, v, g = jnp.split(proj, [D_S5, D_S5 + D_RET, D_S5 + 2 * D_RET, D_S5 + 3 * D_RET], axis=-1)
    y_s5, s5_re, s5_im = s5_scan(u.reshape(b, length, N_S5_GROUPS, S5_GROUP).astype(jnp.float32),
                                 s5_lam_re, s5_lam_im, s5_log_dt, s5_b_re, s5_b_im,
                                 s5_c_re, s5_c_im, s5_d, s5_x0_re, s5_x0_im)
    y_s5 = jax.nn.gelu(y_s5.reshape(b, length, D_S5))
    y_s5 = y_s5 * jax.nn.sigmoid(y_s5 @ s5_w_glu.astype(jnp.float32))
    y_s5 = rmsnorm(y_s5, s5_norm)
    qh = rotary(q.reshape(b, length, N_RET_HEADS, RET_HEAD_DIM), pos)
    kh = rotary(k.reshape(b, length, N_RET_HEADS, RET_HEAD_DIM), pos) * (RET_HEAD_DIM ** -0.5)
    vh = v.reshape(b, length, N_RET_HEADS, RET_HEAD_DIM).astype(jnp.float32)
    o, ret_state = retention(qh.transpose(0, 2, 1, 3), kh.transpose(0, 2, 1, 3),
                             vh.transpose(0, 2, 1, 3), ret_s0.astype(jnp.float32), lead)
    o = o.transpose(0, 2, 1, 3)
    mu = jnp.mean(o, axis=-1, keepdims=True)
    var = jnp.mean(jnp.square(o - mu), axis=-1, keepdims=True)
    o = ((o - mu) * lax.rsqrt(var + EPS)).reshape(b, length, D_RET) * ret_norm.astype(jnp.float32)
    y_ret = jax.nn.silu(g.astype(jnp.float32)) * o
    x = x + jnp.concatenate([y_s5, y_ret], axis=-1).astype(x.dtype) @ w_out
    h2 = rmsnorm(x, norm2)

    def moe_fn(tok):
        return moe(tok, w_router, router_bias, w_gate_e, w_up_e, w_down_e, w_gate_sh, w_up_sh, w_down_sh)

    if map_rows:
        f = lax.map(moe_fn, h2)
    else:
        f = moe_fn(h2.reshape(b * length, D_MODEL)).reshape(b, length, D_MODEL)
    return x + f, s5_re, s5_im, ret_state

def setup_inputs(seed: int = 0) -> dict:
    key = jax.random.key(seed)
    ks = jax.random.split(key, 32)
    nrm = jax.random.normal
    f32 = jnp.float32
    lam_im_base = math.pi * jnp.arange(S5_STATE, dtype=f32)
    return {
        'x_prompt': nrm(ks[0], (BATCH, SEQ, D_MODEL), f32),
        'x_sample': nrm(ks[1], (DEC_BATCH, DEC_SEQ, D_MODEL), f32),
        'state_s5_re': 0.1 * nrm(ks[2], (DEPTH, DEC_BATCH, N_S5_GROUPS, S5_STATE), f32),
        'state_s5_im': 0.1 * nrm(ks[3], (DEPTH, DEC_BATCH, N_S5_GROUPS, S5_STATE), f32),
        'state_ret': nrm(ks[4], (DEPTH, DEC_BATCH, N_RET_HEADS, RET_HEAD_DIM, RET_HEAD_DIM), f32),
        'meta_tokens': nrm(ks[5], (N_META, D_MODEL), f32),
        'norm1': 1.0 + 0.02 * nrm(ks[6], (DEPTH, D_MODEL), f32),
        'w_in': nrm(ks[7], (DEPTH, D_MODEL, D_IN), f32) * D_MODEL ** -0.5,
        's5_lam_re': -0.5 + 0.01 * nrm(ks[8], (DEPTH, N_S5_GROUPS, S5_STATE), f32),
        's5_lam_im': lam_im_base + 0.01 * nrm(ks[9], (DEPTH, N_S5_GROUPS, S5_STATE), f32),
        's5_log_dt': jax.random.uniform(ks[10], (DEPTH, N_S5_GROUPS), f32, math.log(1e-3), math.log(1e-1)),
        's5_b_re': nrm(ks[11], (DEPTH, N_S5_GROUPS, S5_STATE, S5_GROUP), f32) * (2 * S5_GROUP) ** -0.5,
        's5_b_im': nrm(ks[12], (DEPTH, N_S5_GROUPS, S5_STATE, S5_GROUP), f32) * (2 * S5_GROUP) ** -0.5,
        's5_c_re': nrm(ks[13], (DEPTH, N_S5_GROUPS, S5_GROUP, S5_STATE), f32) * S5_STATE ** -0.5,
        's5_c_im': nrm(ks[14], (DEPTH, N_S5_GROUPS, S5_GROUP, S5_STATE), f32) * S5_STATE ** -0.5,
        's5_d': nrm(ks[15], (DEPTH, N_S5_GROUPS, S5_GROUP), f32),
        's5_w_glu': nrm(ks[16], (DEPTH, D_S5, D_S5), f32) * D_S5 ** -0.5,
        's5_norm': 1.0 + 0.02 * nrm(ks[17], (DEPTH, D_S5), f32),
        'ret_norm': 1.0 + 0.02 * nrm(ks[18], (DEPTH, D_RET), f32),
        'w_out': nrm(ks[19], (DEPTH, D_MODEL, D_MODEL), f32) * D_MODEL ** -0.5,
        'norm2': 1.0 + 0.02 * nrm(ks[20], (DEPTH, D_MODEL), f32),
        'w_router': nrm(ks[21], (DEPTH, D_MODEL, N_EXPERTS), f32) * D_MODEL ** -0.5,
        'router_bias': 0.01 * nrm(ks[22], (DEPTH, N_EXPERTS), f32),
        'w_gate_e': nrm(ks[23], (DEPTH, N_EXPERTS, D_MODEL, D_EXPERT), f32) * D_MODEL ** -0.5,
        'w_up_e': nrm(ks[24], (DEPTH, N_EXPERTS, D_MODEL, D_EXPERT), f32) * D_MODEL ** -0.5,
        'w_down_e': nrm(ks[25], (DEPTH, N_EXPERTS, D_EXPERT, D_MODEL), f32) * D_EXPERT ** -0.5,
        'w_gate_sh': nrm(ks[26], (DEPTH, D_MODEL, D_EXPERT), f32) * D_MODEL ** -0.5,
        'w_up_sh': nrm(ks[27], (DEPTH, D_MODEL, D_EXPERT), f32) * D_MODEL ** -0.5,
        'w_down_sh': nrm(ks[28], (DEPTH, D_EXPERT, D_MODEL), f32) * D_EXPERT ** -0.5,
        'final_norm': 1.0 + 0.02 * nrm(ks[29], (D_MODEL,), f32),
    }

def reference(x_prompt, x_sample, state_s5_re, state_s5_im, state_ret, meta_tokens, norm1, w_in,
              s5_lam_re, s5_lam_im, s5_log_dt, s5_b_re, s5_b_im, s5_c_re, s5_c_im, s5_d, s5_w_glu,
              s5_norm, ret_norm, w_out, norm2, w_router, router_bias, w_gate_e, w_up_e, w_down_e,
              w_gate_sh, w_up_sh, w_down_sh, final_norm):
    bp = x_prompt.shape[0]
    meta = jnp.broadcast_to(meta_tokens.astype(x_prompt.dtype)[None], (bp, N_META, D_MODEL))
    xp = jnp.concatenate([meta, x_prompt], axis=1)
    xs = x_sample
    pos_p = jnp.arange(xp.shape[1], dtype=jnp.int32)
    pos_s = PAST_LEN + jnp.arange(xs.shape[1], dtype=jnp.int32)
    zero_s5 = jnp.zeros((bp, N_S5_GROUPS, S5_STATE), jnp.float32)
    zero_ret = jnp.zeros((bp, N_RET_HEADS, RET_HEAD_DIM, RET_HEAD_DIM), jnp.float32)
    p_re, p_im, p_ret, s_re, s_im, s_ret = [], [], [], [], [], []
    for l in range(DEPTH):
        lp = (norm1[l], w_in[l], s5_lam_re[l], s5_lam_im[l], s5_log_dt[l], s5_b_re[l], s5_b_im[l],
              s5_c_re[l], s5_c_im[l], s5_d[l], s5_w_glu[l], s5_norm[l], ret_norm[l], w_out[l], norm2[l],
              w_router[l], router_bias[l], w_gate_e[l], w_up_e[l], w_down_e[l],
              w_gate_sh[l], w_up_sh[l], w_down_sh[l])
        xp, a_re, a_im, a_ret = decoder_layer(xp, pos_p, N_META, zero_s5, zero_s5, zero_ret, True, *lp)
        xs, c_re, c_im, c_ret = decoder_layer(xs, pos_s, xs.shape[1], state_s5_re[l], state_s5_im[l],
                                              state_ret[l], False, *lp)
        p_re.append(a_re)
        p_im.append(a_im)
        p_ret.append(a_ret)
        s_re.append(c_re)
        s_im.append(c_im)
        s_ret.append(c_ret)
    y_prompt = rmsnorm(xp, final_norm)[:, N_META:]
    y_sample = rmsnorm(xs, final_norm)
    s5_re_prompt = jnp.stack(p_re)
    s5_im_prompt = jnp.stack(p_im)
    ret_prompt = jnp.stack(p_ret)
    s5_re_sample = jnp.stack(s_re)
    s5_im_sample = jnp.stack(s_im)
    ret_sample = jnp.stack(s_ret)
    return (y_prompt, y_sample, s5_re_prompt, s5_im_prompt, ret_prompt, s5_re_sample, s5_im_sample, ret_sample)


_drawn_inputs = setup_inputs


def setup_inputs(seed=0):
    import zlib

    import numpy as np

    out = dict(_drawn_inputs(seed))
    spreads = {}
    factors = {}
    for name, (base, spread) in spreads.items():
        noise = np.random.default_rng([zlib.crc32(name.encode()), seed]).standard_normal(out[name].shape)
        drawn = base * np.exp(spread * noise) if base else spread * noise
        out[name] = jnp.asarray(drawn.astype(out[name].dtype))
    for name, factor in factors.items():
        out[name] = (out[name] * factor).astype(out[name].dtype)
    return out
```

```python
from contextlib import ExitStack

import numpy as np

import concourse.bass as bass
from concourse import mybir

ALU = mybir.AluOpType
ACT = mybir.ActivationFunctionType
AX = mybir.AxisListType
F32 = mybir.dt.float32
BF16 = mybir.dt.bfloat16
I32 = mybir.dt.int32
U32 = mybir.dt.uint32
U16 = mybir.dt.uint16

P = 128
D = 1024
KD = D // P
SEQ = 512
NMETA = 16
NS = 8
PAST = 4096
DS5 = 512
NG = 32
NST = 64
H = 8
HD = 64
NE = 64
NGRP = 8
TOPG = 4
TOPK = 8
FE = 256
SCALE_ROUTED = 2.5
EPS = 1e-6

L = 4
GP = NG // 2
HG = GP // 2
NC_META = NMETA // L
NC_ALL = (NMETA + SEQ) // L
NCS = NC_ALL + NS
TE = 4
XM = 32
XR = XM + NMETA
TC = SEQ + XR
TT = SEQ + NS
NT = 5
SLOTS = 128
MORE = -(-TT // SLOTS) - 1
JOBS = TT * TOPK // SLOTS // 4 * 4
MAGIC = 12582912.0
C1, C2 = 6.28125, 0.0019350051879882812
C3 = float(2 * np.pi - C1 - C2)


def kernel_program(nc, ins, outs):
    ctx = ExitStack()
    with ctx:
        arena = ctx.enter_context(nc.sbuf_tensor("arena", [P, 49920], F32))

        def at(off, n):
            return arena[:, off:off + n]

        def sb(name, shape, dt=F32):
            return ctx.enter_context(nc.sbuf_tensor(name, shape, dt))

        def sem(name):
            return ctx.enter_context(nc.semaphore(name))

        bank = [ctx.enter_context(nc.psum_tensor(f"bank{i}", [P, 512], F32)) for i in range(8)]

        HC = HG * NCS
        phase_re, phase_im = at(0, HC), at(1120, HC)
        rot_re, rot_im = at(2240, HC), at(3360, HC)
        st_re, st_im = at(4480, HC), at(5600, HC)
        vt_re, vt_im = at(4480, 1024), at(5600, 1024)
        wt_re, wt_im = at(6720, 1024), at(7744, 1024)
        m_mat = at(8768, 1024)
        v_re, v_im = at(9792, 1024), at(10816, 1024)
        u_chunk = at(11840, GP * NCS).rearrange("p (g c) -> p g c", g=GP)
        x_tiles = at(14080, NT * D).rearrange("p (t d) -> p t d", t=NT)
        xn_bufs = at(19200, 2 * D).rearrange("p (b d) -> p b d", b=2)
        gain1 = at(26880, D)
        v_tok = at(14080, NT * 512).rearrange("p (t f) -> p t f", t=NT)
        gate_tok = at(16640, NT * 512).rearrange("p (t f) -> p t f", t=NT)
        kT = at(19200, 4 * 512).rearrange("p (a t) -> p a t", a=4)
        qT = at(21248, 2 * 512).rearrange("p (b a t) -> p b a t", b=2, a=4)
        kdec = at(22272, 2 * 512).rearrange("p (b f) -> p b f", b=2)
        rt1, rt2 = at(23296, 512), at(23808, 512)
        rotd = [at(24320, 512), at(26880, 512)]
        probs = at(24832, 2 * 512).rearrange("p (b f) -> p b f", b=2)
        on1, on2, on3 = at(25856, 512), at(26368, 512), at(27904, 512)
        state_bd = at(28416, 4 * 512).rearrange("p (c a v) -> p c a v", c=4, a=4)
        state_new = at(30464, 512).rearrange("p (b a v) -> p b a v", b=2, a=4)
        u_feat = at(30976, 4 * 536).rearrange("p (f t) -> p f t", f=4)
        y_feat = at(30976, 4 * TT).rearrange("p (f t) -> p f t", f=4)
        yr_feat = at(33120, 4 * TT).rearrange("p (f t) -> p f t", f=4)
        wbuf = at(35200, 8192)
        w_glu = at(8704, 2048).rearrange("p (k n) -> p k n", k=4)
        hT = at(45440, KD * TC).rearrange("p (k t) -> p k t", k=KD)
        SR = NS * H
        sm_qkv = arena[0:SR, 0:192].rearrange("p (c d) -> p c d", c=3)
        sm_st = [arena[0:SR, 256 + D * b:256 + D * b + D] for b in range(4)]
        sm_kv = [arena[0:SR, 4352 + D * b:4352 + D * b + D] for b in range(4)]
        sm_o = arena[0:SR, 8448:8448 + 256].rearrange("p (c v) -> p c v", c=4)
        sm_x = arena[0:SR, 10752:10752 + 256].rearrange("p (c v) -> p c v", c=4)
        o_ex = arena[0:NS, 11008:11520]
        WSLOT = 6144
        wexp = [at(WSLOT * s, WSLOT) for s in range(4)]
        acc = at(24576, NT * D).rearrange("p (t d) -> p t d", t=NT)
        h2p = at(22272, 2 * D).rearrange("p (b d) -> p b d", b=2)
        glu_t = at(14080, 4 * TT).rearrange("p (f t) -> p f t", f=4)
        glu_sq = at(16160, 4 * TT).rearrange("p (f t) -> p f t", f=4)
        xg = [at(29696 + D * b, D) for b in range(2)]
        xgT = [at(31744 + D * b, D).rearrange("p (k t) -> p k t", k=KD) for b in range(2)]
        ys = [at(33792 + D * b, D) for b in range(2)]
        sil = [at(35840 + 256 * b, 256) for b in range(2)]
        actg = [at(36352 + 256 * b, 256) for b in range(2)]
        actT = [at(36864 + 256 * b, 256).rearrange("p (k t) -> p k t", k=2) for b in range(2)]
        TB = 37376
        small = [at(TB + 320 * i, 320).rearrange("p (t e) -> p t e", t=NT) for i in range(12)]
        hot = [at(TB + 3840 + 320 * b, 320).bitcast(BF16).rearrange("p (t s) -> p t s", t=NT) for b in range(2)]
        info_v = at(TB + 4480, 1280).bitcast(BF16).rearrange("p (t e c) -> p t e c", t=NT, c=8)
        h2T = at(45440, KD * TT).rearrange("p (k t) -> p k t", k=KD)
        gain2 = at(19200, D)

        ident = sb("ident", [P, P])
        identb_tri = sb("tri_ones", [P, 2, P], BF16)
        ones_col = sb("ones_col", [P, 2])
        cosin = sb("cosin", [P, 2, NT, HD // 2])
        mask_dec = at(43392, 1024)
        mask_m = sb("mask_m", [P, P])
        dec_cols = sb("dec_cols", [P, 4, H])
        gam_pair = sb("gam_pair", [P, 4])
        lam = sb("lam", [P, 3, GP])
        pb = at(44416, 1024).rearrange("p (a g h) -> p a g h", a=4, g=GP)
        bb = sb("bb", [P, 2, GP, 16])
        bt = at(4480, 512).rearrange("p (a g h) -> p a g h", a=2, g=GP)
        ncim = sb("ncim", [P, GP, 16])
        dskip = sb("dskip", [P, GP])
        pw = sb("pw", [P, 4, GP, L])
        prm = sb("prm", [P, 34, GP])
        xs0 = sb("xs0", [P, 2, GP, NS])
        fin_s5 = sb("fin_s5", [P, 2, GP, 1 + NS])
        stat = sb("stat", [P, 12, 8])
        norms = sb("norms", [P, 3, 4])
        hst = sb("hst", [P, 4, H])
        w_rt = at(20224, KD * NE).rearrange("p (k n) -> p k n", k=KD)
        bias_b = at(43136, NE)
        rconst = sb("rconst", [P, 16])
        iota_b = sb("iota_b", [P, P], BF16)
        tri8 = at(43200, NE)
        idx_all = at(43264, NE).bitcast(I32)
        gate_all = at(43328, NE)
        idx_buf = sb("idx_buf", [P, 4], I32)
        gate_buf = sb("gate_buf", [P, 4])
        over = sb("over", [P, 6])
        job_e, job_shift = small[0][:, 0, 0:JOBS], small[0][:, 0, JOBS:2 * JOBS]
        job_ei = small[0][:, 1, 0:JOBS].bitcast(I32)
        n_more_i = small[0][0:1, 2, 0:1].bitcast(I32)
        idx_more, gate_more = small[0][:, 3, 0:JOBS].bitcast(I32), small[0][:, 3, JOBS:2 * JOBS]
        done_mark, info_mark = over[:, 2:3], over[:, 3:4]
        INFO_OPS = 7

        h2_dram = nc.dram_tensor("h2_rows", [TT, D], F32, kind="Internal").ap()
        sum_dram = nc.dram_tensor("sum_rows", [TT + SLOTS, D], F32, kind="Internal").ap()
        qkv_dram = nc.dram_tensor("qkv_samples", [3, NS, 512], F32, kind="Internal").ap()
        o_dram = nc.dram_tensor("o_samples", [NS * H, HD], F32, kind="Internal").ap()

        S = {}

        def s(name):
            if name not in S:
                S[name] = sem(name)
            return S[name]

        XT = "x_tiles"
        block = ctx.enter_context(nc.Block())
        TILES = (TE, 0, 1, 2, 3)

        def bc(ap, shape):
            return ap.to_broadcast(shape)

        def h2t_evac(n_):
            i_ = TILES[n_]
            r_ = NS if i_ == TE else P
            for hf in range(2):
                nc.scalar.wait_ge(s("pe_h2t"), 2 * n_ + hf + 1)
                nc.scalar.copy(h2T[:, 4 * hf:4 * hf + 4, P * i_:P * i_ + r_],
                               bank[4 * (n_ % 2) + hf][:, :].rearrange("p (k t) -> p k t", k=4)[:, :, 0:r_]
                               ).then_inc(s("a_h2t"), 1)

        def weights(slot, kind):
            return wexp[slot][:, 2048 * kind:2048 * (kind + 1)]

        def load_expert(sp, q, j, e, first):
            if not first:
                sp.wait_ge(s("pe_down"), 4 * q + j - 3)
            for kind, nm in enumerate(("w_gate_e", "w_up_e")):
                if not first and kind == 1:
                    sp.wait_ge(s("pe_half"), 4 * q + j - 1)
                sp.dma_start(weights(j, kind), ins[nm][0, bass.ds(e, 1)].rearrange("a (p k) f -> p (a k f)", p=P)
                             ).then_inc(s(f"w_slot{j}"), 16)
            if not first:
                sp.wait_ge(s("pe_gu"), 4 * q + j - 1)
            sp.dma_start(weights(j, 2), ins["w_down_e"][0, bass.ds(e, 1)].rearrange("a (p k) d -> p (a k d)", p=P)
                         ).then_inc(s(f"w_slot{j}"), 16)

        def moe_sync(sp):
            sp.wait_ge(s("pe_ss"), 1)
            for kind, nm in enumerate(("w_gate_sh", "w_up_sh")):
                sp.dma_start(weights(2, kind), ins[nm][0].rearrange("(p k) f -> p (k f)", p=P)).then_inc(s("w_shared"), 16)
            sp.dma_start(weights(2, 2), ins["w_down_sh"][0].rearrange("(p k) d -> p (k d)", p=P)).then_inc(s("w_shared"), 16)
            for j in range(2):
                load_expert(sp, 0, j, j, True)
            sp.wait_ge(s("pe_rt"), NT)
            load_expert(sp, 0, 3, 3, True)
            sp.wait_ge(s("pe_shared"), NT)
            load_expert(sp, 0, 2, 2, True)
            for n_, i in enumerate(TILES):
                r_ = NS if i == TE else P
                sp.wait_ge(s("d_sh"), n_ + 1)
                sp.dma_start(sum_dram[P * i:P * i + r_, :], acc[0:r_, i, :]).then_inc(s("st_sum"), 16)
            with sp.Fori(1, NE // 4) as q:
                for j in range(4):
                    load_expert(sp, q, j, 4 * q + j, False)
            overflow(sp, sync_more)
            sp.wait_ge(s("all_added"), 1)
            for n_, i in enumerate(TILES):
                r_ = NS if i == TE else P
                sp.dma_start(acc[0:r_, i, :], sum_dram[P * i:P * i + r_, :]).then_inc(s(f"ld_tok{i}"), 16)
            sp.dma_start(gain2, ins["final_norm"].partition_broadcast(P)).then_inc(s("ld_gain"), 16)
            for n_, i in enumerate(TILES):
                sp.wait_ge(s("d_out"), n_ + 1)
                if i == TE:
                    sp.dma_start(outs["y_sample"][:, 0, :], acc[0:NS, TE, :]).then_inc(s("st_fin"), 16)
                else:
                    sp.dma_start(outs["y_prompt"][0, P * i:P * (i + 1), :], acc[:, i, :]).then_inc(s("st_fin"), 16)
            sp.wait_ge(s("st_fin"), 16 * 5)

        def sync_more(sp, k):
            for j in range(4):
                e = sp.value_load(job_ei[0:1, bass.ds(4 * k + j, 1)], min_val=0, max_val=NE - 1)
                load_expert(sp, NE // 4 + k, j, e, False)

        def overflow(eng, body):
            eng.wait_ge(s("jobs_ready"), 1)
            n_more = eng.value_load(n_more_i, min_val=0, max_val=JOBS)
            with eng.Fori(0, JOBS // 4) as k:
                with eng.If(n_more > 4 * k):
                    body(eng, k)

        def settle(pool, kind, n):
            if not isinstance(n, int) or n:
                pool.wait_ge(s(f"settled{kind}"), n)
            mark = over[0:1, kind:kind + 1]
            pool.tensor_tensor(mark, mark, mark, ALU.mult).then_inc(s(f"settled{kind}"), 1)

        def pool_step(pool, q, j, gate, idx):
            first = isinstance(q, int) and q == 0
            if not first:
                pool.wait_ge(s("scattered"), 16 * (4 * q + j - 3))
                pool.wait_ge(s("act_done"), 4 * q + j - 3)
            pool.tensor_copy(gate_buf[:, j:j + 1], gate).then_inc(s("gate_copied"), 1)
            pool.tensor_copy(idx_buf[:, j:j + 1], idx).then_inc(s("idx_copied"), 1)
            pool.wait_ge(s("idx_copied"), 4 * q + j + 1)
            if not first or j >= 2:
                pool.wait_ge(s("pe_xgt"), 4 * q + j - 1)
            settle(pool, 0, 4 * q + j)
            pool.indirect_dma_start(xg[j % 2], None, h2_dram, bass.IndirectOffsetOnAxis(idx_buf[:, j:j + 1].bitcast(U32), axis=0),
                                    bounds_check=TT - 1, oob_is_err=False).then_inc(s(f"gathered{j % 2}"), 16)

        def pool_scatter(pool, q, j):
            first = isinstance(q, int) and q == 0
            pool.wait_ge(s("a_ys"), 4 * q + j + 1)
            pool.wait_ge(s("d_ys"), 4 * q + j + 1)
            if not first or j >= 1:
                pool.wait_ge(s("scattered"), 16 * (4 * q + j))
            settle(pool, 1, 4 * q + j)
            pool.indirect_dma_start(sum_dram, bass.IndirectOffsetOnAxis(idx_buf[:, j:j + 1].bitcast(U32), axis=0),
                                    ys[j % 2], None, bounds_check=TT + SLOTS - 1, compute_op=ALU.add
                                    ).then_inc(s("scattered"), 16)

        def pool_first(pool):
            for j in range(4):
                pool_step(pool, 0, j, gate_all[:, j:j + 1], idx_all[:, j:j + 1])
                if j == 3:
                    pool.wait_ge(s("st_sum"), 16 * NT)
                    pool.wait_ge(s("st_dump"), 16)
                    pool_scatter(pool, 0, 0)
            with pool.Fori(1, NE // 4) as q:
                pool.wait_ge(s("info_ready"), q)
                for j in range(4):
                    e = bass.ds(4 * q + j, 1)
                    pool_step(pool, q, j, gate_all[:, e], idx_all[:, e])
                    pool_scatter(pool, q + ((j + 1) // 4 - 1), (j + 1) % 4)
            for j in (1, 2, 3):
                pool_scatter(pool, NE // 4 - 1, j)

        def pool_more(pool, k):
            q = NE // 4 + k
            pool.wait_ge(s("info_ready"), NE // 4 + k)
            for j in range(4):
                n_ = bass.ds(4 * k + j, 1)
                pool_step(pool, q, j, gate_more[:, n_], idx_more[:, n_])
                if j >= 2:
                    pool_scatter(pool, q, j - 2)
            for j in (2, 3):
                pool_scatter(pool, q, j)
            pool.wait_ge(s("scattered"), 16 * (4 * q + 4))
            mark = over[0:1, 2:3]
            pool.wait_ge(s("group_done"), k + 1)
            pool.tensor_tensor(mark, mark, mark, ALU.mult).then_inc(s("group_done"), 1)

        def moe_pool(pool):
            pool.wait_ge(s("info_ready"), 1)
            pool.wait_ge(s("st_h2_0"), 16 * 3)
            pool.wait_ge(s("st_h2_1"), 16 * 2)
            pool.wait_ge(s("xg_zero"), 1)
            pool.memset(over[:, 5:6], 0.0).then_inc(s("group_done"), 1)
            pool_first(pool)
            pool.wait_ge(s("scattered"), 16 * NE)
            overflow(pool, pool_more)
            pool.memset(over[:, 4:5], 0.0).then_inc(s("all_added"), 1)

        def act_rows(act, q, j):
            first = isinstance(q, int) and q == 0
            n = 4 * q + j
            act.wait_ge(s("pe_xgt"), n + 1)
            if not first or j >= 2:
                act.wait_ge(s("pe_gu"), n - 1)
            nc.scalar.copy(xgT[j % 2][:, 0:4, :], bank[0][:, :].rearrange("p (k t) -> p k t", k=4)).then_inc(s("a_xgt"), 1)

        def act_step(act, q, j, last=False, alone=False):
            first = isinstance(q, int) and q == 0
            n = 4 * q + j
            act.wait_ge(s("pe_gu"), n + 1)
            if not first or j >= 2:
                act.wait_ge(s("act_done"), n - 1)
            nc.scalar.activation(sil[j % 2], bank[(2, 6)[j % 2]][:, 0:FE], ACT.Silu).then_inc(s("silu_done"), 1)
            if not last:
                act_rows(act, q + (j + 1) // 4, (j + 1) % 4)
            if (not first or j >= 1) and not (alone and j == 0):
                act_down(act, q if j else q - 1, (j - 1) % 4)

        def act_down(act, q, j):
            first = isinstance(q, int) and q == 0
            n = 4 * q + j
            act.wait_ge(s("pe_down"), n + 1)
            if not first or j >= 2:
                act.wait_ge(s("scattered"), 16 * (n - 1))
            nc.scalar.copy(ys[j % 2][:, 0:512], bank[4][:, :]).then_inc(s("a_ys"), 1)

        def act_first(act):
            act_rows(act, 0, 0)
            for j in range(4):
                act_step(act, 0, j)
            with act.Fori(1, NE // 4 - 1) as q:
                for j in range(4):
                    act_step(act, q, j)
            for j in range(4):
                act_step(act, NE // 4 - 1, j, last=j == 3)
            act_down(act, NE // 4 - 1, 3)

        def act_more(act, k):
            act_rows(act, NE // 4 + k, 0)
            for j in range(4):
                act_step(act, NE // 4 + k, j, j == 3, True)
            act_down(act, NE // 4 + k, 3)

        def moe_act(act):
            def a(out, in_, f, **kw):
                return nc.scalar.activation(out, in_, f, **kw)
            act.wait_ge(s("pe_rt"), NT)
            act.wait_ge(s("lg_zero"), 1)
            a(small[0][:, 0:4, :], bank[0][:, 0:4 * NE].rearrange("p (t e) -> p t e", e=NE), ACT.Tanh, scale=0.5
              ).then_inc(s("a_lg"), 1)
            a(small[0][0:NS, TE, :], bank[0][0:NS, TE * NE:NT * NE], ACT.Tanh, scale=0.5).then_inc(s("a_lg"), 1)
            for n_, i in enumerate(TILES):
                r_ = NS if i == TE else P
                act.wait_ge(s("pe_shgu"), n_ + 1)
                if n_ >= 2:
                    act.wait_ge(s("d_shact"), n_ - 1)
                a(sil[n_ % 2][0:r_, :], bank[(2, 6)[n_ % 2]][0:r_, 0:FE], ACT.Silu).then_inc(s("a_shsil"), 1)
            act_first(act)
            overflow(act, act_more)
            for n_, i in enumerate(TILES):
                r_ = NS if i == TE else P
                act.wait_ge(s(f"ld_tok{i}"), 64 if i == TE else 48)
                a(h2p[0:r_, n_ % 2, :], acc[0:r_, i, :], ACT.Square, accum_out=stat[0:r_, 8, i:i + 1]).then_inc(s("a_ss2"), 1)
                act.wait_ge(s("a_ss2"), NT + n_ + 1)
                a(stat[0:r_, 9, i:i + 1], stat[0:r_, 8, i:i + 1], ACT.Sqrt, scale=1.0 / D,
                  bias=stat[0:r_, 7, 0:1]).then_inc(s("a_rt2"), 1)

        def dve_rows(dve, q, j):
            first = isinstance(q, int) and q == 0
            n = 4 * q + j
            dve.wait_ge(s("pe_xgt"), n + 1)
            if not first or j >= 2:
                dve.wait_ge(s("pe_gu"), n - 1)
            nc.vector.tensor_copy(xgT[j % 2][:, 4:8, :], bank[1][:, :].rearrange("p (k t) -> p k t", k=4)
                                  ).then_inc(s("d_xgt"), 1)

        def dve_step(dve, q, j, last=False, alone=False):
            first = isinstance(q, int) and q == 0
            n = 4 * q + j
            v = nc.vector
            dve.wait_ge(s("silu_done"), n + 1)
            dve.wait_ge(s("gate_copied"), n + 1)
            if not first or j >= 2:
                dve.wait_ge(s("pe_at"), n - 1)
            v.scalar_tensor_tensor(actg[j % 2].rearrange("t (k p) -> t p k", k=2), sil[j % 2].rearrange("t (p k) -> t p k", k=2),
                                   gate_buf[:, j:j + 1], bank[(2, 6)[j % 2]][:, FE:].rearrange("t (p k) -> t p k", k=2),
                                   ALU.mult, ALU.mult).then_inc(s("act_done"), 1)
            if not last:
                dve_rows(dve, q + (j + 1) // 4, (j + 1) % 4)
            if (not first or j >= 1) and not (alone and j == 0):
                dve_down(dve, q if j else q - 1, (j - 1) % 4)
            dve.wait_ge(s("pe_at"), n + 1)
            if not first or j >= 2:
                dve.wait_ge(s("pe_down"), n - 1)
            v.tensor_copy(actT[j % 2], bank[3][:, 0:256].rearrange("p (k t) -> p k t", k=2)).then_inc(s("d_at"), 1)

        def dve_down(dve, q, j):
            first = isinstance(q, int) and q == 0
            n = 4 * q + j
            dve.wait_ge(s("pe_down"), n + 1)
            if not first or j >= 2:
                dve.wait_ge(s("scattered"), 16 * (n - 1))
            nc.vector.tensor_copy(ys[j % 2][:, 512:1024], bank[5][:, :]).then_inc(s("d_ys"), 1)

        def hot_rows(dve, half, ranks):
            for i in range(NT):
                last = nc.vector.tensor_scalar(hot[half][:, i, :], iota_b[:], ranks(i), None, ALU.is_equal)
            last.then_inc(s("hot_ready"), 1)

        def dve_info(dve):
            for e in range(2 * 4):
                if e >= 2:
                    dve.wait_ge(s("pe_info"), e - 1)
                hot_rows(dve, e % 2, lambda i: small[1][:, i, e:e + 1])
            dve.wait_ge(s("pe_info"), 8)
            slot_info(dve, 8, 0, idx_all[:, 0:8], gate_all[:, 0:8])

        def dve_ahead(dve, q, j):
            for j2 in {0: (0,), 1: (1,), 2: (2, 3), 3: ()}[j]:
                n = 4 * (q + 2) + j2
                dve.wait_ge(s("pe_info"), n - 1)
                hot_rows(dve, j2 % 2, lambda i: small[1][:, i, bass.ds(n, 1)])
            if j == 3:
                g = bass.ds(4 * (q + 2), 4)
                dve.wait_ge(s("pe_info"), 4 * (q + 2) + 4)
                slot_info(dve, 4, INFO_OPS * (q + 1), idx_all[:, g], gate_all[:, g])

        def slot_info(dve, ne, base, idx, gate):
            v = nc.vector
            ps = bank[7][:, 0:8 * ne].rearrange("p (e c) -> p e c", c=8)
            flat = small[3].rearrange("p t e -> p (t e)")
            col = lambda c: flat[:, ne * c:ne * (c + 1)]
            t0, t1 = small[2][:, 0, 0:ne], small[2][:, 1, 0:ne]
            v.tensor_copy(flat[:, 0:4 * ne].rearrange("p (c e) -> p e c", c=4), ps[:, :, 0:4]).then_inc(s("d_info"), 1)
            dve.wait_ge(s("d_info"), base + 1)
            v.scalar_tensor_tensor(t0, col(0), float(P), col(1), ALU.mult, ALU.add).then_inc(s("d_info"), 1)
            v.tensor_scalar(t1, col(2), -1.0, 1.0, ALU.mult, ALU.add).then_inc(s("d_info"), 1)
            dve.wait_ge(s("d_info"), base + 3)
            v.scalar_tensor_tensor(t0, t1, rconst[:, 0:1], t0, ALU.mult, ALU.add).then_inc(s("d_info"), 1)
            dve.wait_ge(s("d_info"), base + 4)
            v.tensor_tensor(t1, col(3), ps[:, :, 4], ALU.add).then_inc(s("d_info"), 1)
            dve.wait_ge(s("d_info"), base + 5)
            v.tensor_copy(idx, t0).then_inc(s("d_info"), 1)
            v.tensor_tensor(gate, t1, ps[:, :, 5], ALU.add).then_inc(s("d_info"), 1)
            dve.wait_ge(s("d_info"), base + INFO_OPS)
            v.memset(info_mark, 0.0).then_inc(s("info_ready"), 1)

        def dve_first(dve, seq):
            dve_rows(dve, 0, 0)
            for j in range(4):
                dve_step(dve, 0, j)
                dve_ahead(dve, 0, j)
                job_table(seq, j)
            with dve.Fori(1, NE // 4 - 2) as q:
                for j in range(4):
                    dve_step(dve, q, j)
                    dve_ahead(dve, q, j)
            for q in (NE // 4 - 2, NE // 4 - 1):
                for j in range(4):
                    dve_step(dve, q, j, last=q == NE // 4 - 1 and j == 3)
            dve_down(dve, NE // 4 - 1, 3)

        def job_table(seq, part):
            v = nc.vector
            cnt, xb, cum, js = (small[11][:, i_, :] for i_ in range(4))
            js, inval = js[:, 0:JOBS], small[11][:, 4, 0:JOBS]
            cmp = at(TB + 4 * 320, JOBS * NE).rearrange("p (j e) -> p j e", e=NE)
            sh = [P, JOBS, NE]
            if part == 0:
                v.tensor_copy(js, iota_b[:, 0:JOBS])
                seq(v.tensor_scalar(xb, cnt, float(SLOTS), None, ALU.is_gt))
                for m in range(2, MORE + 1):
                    seq(v.scalar_tensor_tensor(xb, cnt, float(SLOTS * m), xb, ALU.is_gt, ALU.add))
                seq(v.tensor_tensor_scan(cum, xb, bc(ones_col[:, 0:1], [P, NE]), 0.0, ALU.add, ALU.mult))
                seq(v.tensor_tensor(cmp, bc(cum.unsqueeze(1), sh), bc(js.unsqueeze(2), sh), ALU.is_le))
            elif part == 1:
                seq(v.tensor_reduce(job_e, cmp, AX.X, ALU.add))
                seq(v.tensor_tensor(cmp, cmp, bc(xb.unsqueeze(1), sh), ALU.mult))
            elif part == 2:
                seq(v.tensor_reduce(job_shift, cmp, AX.X, ALU.add))
                seq(v.tensor_tensor(job_shift, js, job_shift, ALU.subtract))
                seq(v.tensor_scalar(inval, js, cum[:, NE - 1:NE], float(TT), ALU.is_ge, ALU.mult))
                seq(v.tensor_tensor(job_shift, job_shift, inval, ALU.add))
                seq(v.tensor_scalar(job_shift, job_shift, 1.0, float(SLOTS), ALU.add, ALU.mult))
            else:
                seq(v.tensor_scalar(job_e, job_e, float(NE - 1), None, ALU.min))
                seq(v.tensor_copy(job_ei, job_e))
                seq(v.tensor_copy(n_more_i, cum[0:1, NE - 1:NE]))
                v.memset(done_mark, 0.0).then_inc(s("jobs_ready"), 1)

        def dve_more(dve, k):
            v = nc.vector
            n0 = NE + 4 * k
            for j in range(4):
                e = dve.value_load(job_ei[0:1, bass.ds(4 * k + j, 1)], min_val=0, max_val=NE - 1)
                v.tensor_tensor(small[2][:, :, j:j + 1], small[1][:, :, bass.ds(e, 1)],
                                bc(job_shift[:, bass.ds(4 * k + j, 1)].unsqueeze(1), [P, NT, 1]), ALU.subtract
                                ).then_inc(s("rank_shift"), 1)
                dve.wait_ge(s("rank_shift"), 4 * k + j + 1)
                dve.wait_ge(s("pe_info"), n0 + j - 1)
                hot_rows(dve, j % 2, lambda i: small[2][:, i, j:j + 1])
            dve.wait_ge(s("pe_info"), n0 + 4)
            slot_info(dve, 4, INFO_OPS * (NE // 4 - 1 + k), idx_more[:, bass.ds(4 * k, 4)], gate_more[:, bass.ds(4 * k, 4)])
            dve_rows(dve, NE // 4 + k, 0)
            for j in range(4):
                dve_step(dve, NE // 4 + k, j, j == 3, True)
            dve_down(dve, NE // 4 + k, 3)

        def moe_dve(dve):
            v = nc.vector
            n = [0]

            def seq(i):
                n[0] += 1
                i.then_inc(s("moe_seq"), 1)
                dve.wait_ge(s("moe_seq"), n[0])

            def tt(o, a_, b_, op):
                return v.tensor_tensor(o, a_, b_, op)

            dve.wait_ge(s("ld_bt"), 32)
            seq(v.memset(small[0], 0.0))
            for b in range(2):
                seq(v.memset(xg[b], 0.0))
            v.memset(ys[0], 0.0).then_inc(s("xg_zero"), 1)
            dve.wait_ge(s("xg_zero"), 1)
            v.memset(done_mark, 0.0).then_inc(s("lg_zero"), 1)
            dve.wait_ge(s("lg_zero"), 1)
            dve.wait_ge(s("a_lg"), 2)
            sc, sel = small[2], small[3]
            t4, t5, t6, t7 = small[4], small[5], small[6], small[7]
            seq(v.tensor_scalar(sc, small[0], 0.5, 0.5, ALU.mult, ALU.add))
            seq(tt(sel, sc, bc(bias_b.unsqueeze(1), [P, NT, NE]), ALU.add))
            g8 = lambda w: w.rearrange("p t (g m) -> p (t g) m", m=8)
            for k in (1, 2, 3, 4):
                o = t4 if k == 1 else t5
                seq(tt(g8(o)[:, :, 0:8 - k], g8(sel)[:, :, 0:8 - k], g8(sel)[:, :, k:8], ALU.add))
                seq(tt(g8(o)[:, :, 8 - k:8], g8(sel)[:, :, 8 - k:8], g8(sel)[:, :, 0:k], ALU.add))
                if k > 1:
                    seq(tt(t4, t4, t5, ALU.max))
            gs = t5.rearrange("p t e -> p (t e)")[:, 0:NT * 8].rearrange("p (t g) -> p t g", g=8)
            seq(v.tensor_reduce(gs, g8(t4).rearrange("p (t g) m -> p t g m", g=8), AX.X, ALU.max))
            a4 = lambda w: w.rearrange("p t (i j) -> p t i j", j=8)
            for i in range(NT):
                gi = bc(gs[:, i, :].unsqueeze(2), [P, 8, 8])
                gj = bc(gs[:, i, :].unsqueeze(1), [P, 8, 8])
                seq(tt(a4(t6)[:, i], gj, gi, ALU.is_gt))
                seq(tt(a4(t7)[:, i], gj, gi, ALU.is_equal))
            seq(tt(t7, t7, bc(tri8.unsqueeze(1), [P, NT, 64]), ALU.mult))
            seq(tt(t6, t6, t7, ALU.add))
            rk = t4.rearrange("p t e -> p (t e)")[:, 0:NT * 8]
            seq(v.tensor_reduce(rk, t6.rearrange("p t (i j) -> p (t i) j", j=8), AX.X, ALU.add))
            seq(v.tensor_scalar(rk, rk, float(TOPG) - 0.5, None, ALU.is_lt))
            gm = bc(rk.unsqueeze(2), [P, NT * 8, 8])
            seq(v.tensor_scalar(t5.rearrange("p t e -> p (t e)")[:, 0:NT * 8], rk, -1.0, 1e30, ALU.add, ALU.mult))
            lo = bc(t5.rearrange("p t e -> p (t e)")[:, 0:NT * 8].unsqueeze(2), [P, NT * 8, 8])
            seq(tt(g8(t6), g8(sel), gm, ALU.mult))
            seq(tt(g8(t6), g8(t6), lo, ALU.add))
            best = stat[:, 11, :]
            for i in range(NT):
                seq(v.max(best, t6[:, i, :]))
                seq(v.match_replace(t7[:, i, :], best, t6[:, i, :], -3e38))
            seq(tt(t4, t6, t7, ALU.not_equal))
            seq(tt(t4, t4, bc(rconst[:, 1:6].unsqueeze(2), [P, NT, NE]), ALU.mult))
            seq(tt(t5, sc, t4, ALU.mult))
            sm = stat[:, 6, 0:NT]
            seq(v.tensor_reduce(sm, t5, AX.X, ALU.add))
            seq(v.tensor_scalar(sm, sm, 1e-37, None, ALU.max))
            seq(v.reciprocal(sm, sm))
            seq(tt(t5, t5, bc(sm.unsqueeze(2), [P, NT, NE]), ALU.mult))
            seq(v.tensor_scalar(t5, t5, SCALE_ROUTED, None, ALU.mult))
            seq(v.tensor_copy(small[8].rearrange("p t e -> p (t e)").bitcast(BF16)[:, 0:NT * NE], t4.rearrange("p t e -> p (t e)")))
            v.memset(info_v.rearrange("p t e c -> p (t e c)"), 0.0).then_inc(s("mask_ready"), 1)
            dve.wait_ge(s("mask_ready"), 1)
            for i in range(NT):
                seq(v.memset(info_v[:, i, :, 0], float(i)))
            seq(v.tensor_copy(info_v[:, :, :, 1], bc(rconst[:, 6:7].unsqueeze(2), [P, NT, NE])))
            seq(v.memset(info_v[:, :, :, 2], 1.0))
            seq(v.tensor_copy(info_v[:, :, :, 3], t5))
            seq(tt(t6, t5, info_v[:, :, :, 3], ALU.subtract))
            seq(v.tensor_copy(info_v[:, :, :, 4], t6))
            seq(tt(t6, t6, info_v[:, :, :, 4], ALU.subtract))
            seq(v.tensor_copy(info_v[:, :, :, 5], t6))
            dve.wait_ge(s("pe_rank"), 1)
            ps = bank[1][:, 0:NT * NE].rearrange("p (t e) -> p t e", e=NE)
            seq(v.tensor_scalar(t6, ps, 1.0, None, ALU.add))
            seq(tt(t6, t6, t4, ALU.mult))
            seq(v.tensor_scalar(small[1], t6, -1.0, None, ALU.add))
            seq(v.tensor_copy(small[11][:, 0, :], bank[1][:, 384:448]))
            dve_info(dve)
            for n_, i in enumerate(TILES):
                r_ = NS if i == TE else P
                dve.wait_ge(s("a_shsil"), n_ + 1)
                if n_ >= 2:
                    dve.wait_ge(s("pe_shat"), n_ - 1)
                tt(actg[n_ % 2][0:r_].rearrange("t (k p) -> t p k", k=2), sil[n_ % 2][0:r_].rearrange("t (p k) -> t p k", k=2),
                   bank[(2, 6)[n_ % 2]][0:r_, FE:].rearrange("t (p k) -> t p k", k=2), ALU.mult).then_inc(s("d_shact"), 1)
                dve.wait_ge(s("pe_shat"), n_ + 1)
                v.tensor_copy(actT[n_ % 2][:, :, 0:r_], bank[3][:, 0:256].rearrange("p (k t) -> p k t", k=2)[:, :, 0:r_]
                              ).then_inc(s("d_shat"), 1)
                dve.wait_ge(s("pe_shared"), n_ + 1)
                for hf in range(2):
                    last = tt(acc[0:r_, i, 512 * hf:512 * hf + 512], acc[0:r_, i, 512 * hf:512 * hf + 512],
                              bank[4 + hf][0:r_, :], ALU.add)
                last.then_inc(s("d_sh"), 1)
            dve_first(dve, seq)
            overflow(dve, dve_more)
            dve.wait_ge(s("ld_gain"), 48)
            for n_, i in enumerate(TILES):
                r_ = NS if i == TE else P
                dve.wait_ge(s("a_rt2"), NT + n_ + 1)
                seq(v.reciprocal(stat[0:r_, 10, i:i + 1], stat[0:r_, 9, i:i + 1]))
                v.scalar_tensor_tensor(acc[0:r_, i, :], acc[0:r_, i, :], stat[0:r_, 10, i:i + 1], gain2[0:r_, :],
                                       ALU.mult, ALU.mult).then_inc(s("d_out"), 1)

        def mmul(o, l, r, start, stop):
            return nc.tensor.matmul(o, l, r, start=start, stop=stop, skip_group_check=True)

        def w_gu(slot):
            return wexp[slot][:, 0:4096].rearrange("p (a k f) -> p k a f", a=2, k=KD)

        def pe_rows(pe, q, j):
            first = isinstance(q, int) and q == 0
            n = 4 * q + j
            pe.wait_ge(s(f"gathered{j % 2}"), 16 * (2 * q + j // 2 + 1))
            if not first or j >= 1:
                pe.wait_ge(s("a_xgt"), n)
                pe.wait_ge(s("d_xgt"), n)
            for k in range(KD):
                t = nc.tensor.transpose(bank[k // 4][:, P * (k % 4):P * (k % 4) + P], xg[j % 2][:, P * k:P * k + P], ident[:])
            t.then_inc(s("pe_xgt"), 1)

        def pe_up(pe, q, j):
            first = isinstance(q, int) and q == 0
            n = 4 * q + j
            pe.wait_ge(s(f"w_slot{j}"), 48 * (q + 1))
            pe.wait_ge(s("a_xgt"), n + 1)
            pe.wait_ge(s("d_xgt"), n + 1)
            if not first or j >= 2:
                pe.wait_ge(s("act_done"), n - 1)
            for k in range(KD):
                t = mmul(bank[(2, 6)[j % 2]][:, :].rearrange("p (a f) -> p a f", a=2), xgT[j % 2][:, k, :],
                         w_gu(j)[:, k], k == 0, k == KD - 1)
                if k == KD // 2 - 1:
                    t.then_inc(s("pe_half"), 1)
            t.then_inc(s("pe_gu"), 1)

        def pe_act(pe, q, j):
            first = isinstance(q, int) and q == 0
            n = 4 * q + j
            pe.wait_ge(s("act_done"), n + 1)
            if not first or j >= 1:
                pe.wait_ge(s("d_at"), n)
            for k in range(2):
                t = nc.tensor.transpose(bank[3][:, P * k:P * k + P], actg[j % 2][:, P * k:P * k + P], ident[:])
            t.then_inc(s("pe_at"), 1)

        def pe_down(pe, q, j):
            first = isinstance(q, int) and q == 0
            n = 4 * q + j
            pe.wait_ge(s("d_at"), n + 1)
            if not first or j >= 1:
                pe.wait_ge(s("a_ys"), n)
                pe.wait_ge(s("d_ys"), n)
            wd = weights(j, 2).rearrange("p (k d) -> p k d", k=2)
            for hf in range(2):
                for k in range(2):
                    t = mmul(bank[4 + hf][:, :], actT[j % 2][:, k, :], wd[:, k, 512 * hf:512 * hf + 512], k == 0, k == 1)
            t.then_inc(s("pe_down"), 1)

        def pe_step(pe, q, j, last=False, ahead=False):
            pe_up(pe, q, j)
            if ahead:
                pe_ahead(pe, q, j)
            if not last:
                pe_rows(pe, q + (j + 1) // 4, (j + 1) % 4)
            if not (isinstance(q, int) and q == 0 and j == 0):
                pe_down(pe, q if j else q - 1, (j - 1) % 4)
            pe_act(pe, q, j)

        def pe_info(pe):
            for e in range(2 * 4):
                info_block(pe, e % 2, e, e, e)

        def pe_ahead(pe, q, j):
            if j == 0:
                pe.wait_ge(s("info_ready"), q + 1)
            for j2 in {0: (), 1: (0,), 2: (1,), 3: (2, 3)}[j]:
                info_block(pe, j2 % 2, j2, 4 * (q + 2) + j2, 4 * (q + 2) + j2)

        def info_block(pe, half, col, e, n):
            pe.wait_ge(s("hot_ready"), n + 1)
            for i in range(NT):
                t = mmul(bank[7][:, bass.ds(8 * col, 8)], hot[half][:, i, :], info_v[:, i, bass.ds(e, 1), :],
                         i == 0, i == NT - 1)
            t.then_inc(s("pe_info"), 1)

        def pe_first(pe):
            pe_rows(pe, 0, 0)
            for j in range(4):
                pe_step(pe, 0, j, ahead=True)
            with pe.Fori(1, NE // 4 - 2) as q:
                for j in range(4):
                    pe_step(pe, q, j, ahead=True)
            for q in (NE // 4 - 2, NE // 4 - 1):
                for j in range(4):
                    pe_step(pe, q, j, last=q == NE // 4 - 1 and j == 3)
            pe_down(pe, NE // 4 - 1, 3)

        def pe_more(pe, k):
            q = NE // 4 + k
            pe.wait_ge(s("info_ready"), NE // 4 - 1 + k)
            for j in range(4):
                e = pe.value_load(job_ei[0:1, bass.ds(4 * k + j, 1)], min_val=0, max_val=NE - 1)
                info_block(pe, j % 2, j, e, 4 * q + j)
            pe_rows(pe, q, 0)
            for j in range(4):
                pe_up(pe, q, j)
                if j < 3:
                    pe_rows(pe, q, j + 1)
                if j > 0:
                    pe_down(pe, q, j - 1)
                pe_act(pe, q, j)
            pe_down(pe, q, 3)

        def moe_pe(pe):
            pe.wait_ge(s("a_h2t"), 10)
            pe.wait_ge(s("ld_rt"), 16)
            for n_, i in enumerate(TILES):
                r_ = NS if i == TE else P
                for k in range(KD):
                    t = mmul(bank[0][0:r_, NE * i:NE * (i + 1)], h2T[:, k, P * i:P * i + r_], w_rt[:, k, :], k == 0, k == KD - 1)
                t.then_inc(s("pe_rt"), 1)
            pe.wait_ge(s("w_shared"), 48)
            wd = weights(2, 2).rearrange("p (k d) -> p k d", k=2)

            def sh_up(n_):
                i = TILES[n_]
                r_ = NS if i == TE else P
                if n_ >= 2:
                    pe.wait_ge(s("d_shact"), n_ - 1)
                for k in range(KD):
                    t = mmul(bank[(2, 6)[n_ % 2]][0:r_, :].rearrange("p (a f) -> p a f", a=2), h2T[:, k, P * i:P * i + r_],
                             w_gu(2)[:, k], k == 0, k == KD - 1)
                t.then_inc(s("pe_shgu"), 1)

            sh_up(0)
            pe.wait_ge(s("mask_ready"), 1)
            mb = small[8].rearrange("p t e -> p (t e)").bitcast(BF16)[:, 0:NT * NE].rearrange("p (t e) -> p t e", e=NE)
            for i in range(NT):
                for i2 in range(i + 1):
                    t = mmul(bank[1][:, NE * i:NE * (i + 1)], identb_tri[:, 0 if i2 == i else 1, :], mb[:, i2, :], i2 == 0, i2 == i)
            for i in range(NT):
                t = mmul(bank[1][:, 384:448], identb_tri[:, 1, :], mb[:, i, :], i == 0, i == NT - 1)
            t.then_inc(s("pe_rank"), 1)
            sh_up(1)
            pe_info(pe)
            for n_, i in enumerate(TILES):
                r_ = NS if i == TE else P
                if 1 <= n_ < NT - 1:
                    sh_up(n_ + 1)
                pe.wait_ge(s("d_shact"), n_ + 1)
                if n_ >= 1:
                    pe.wait_ge(s("d_shat"), n_)
                for k in range(2):
                    t = nc.tensor.transpose(bank[3][:, P * k:P * k + r_], actg[n_ % 2][0:r_, P * k:P * k + P], ident[0:r_, 0:r_])
                t.then_inc(s("pe_shat"), 1)
                pe.wait_ge(s("d_shat"), n_ + 1)
                if n_ >= 1:
                    pe.wait_ge(s("d_sh"), n_)
                for hf in range(2):
                    for k in range(2):
                        t = mmul(bank[4 + hf][0:r_, :], actT[n_ % 2][:, k, 0:r_], wd[:, k, 512 * hf:512 * hf + 512], k == 0, k == 1)
                t.then_inc(s("pe_shared"), 1)
            pe.wait_ge(s("d_sh"), NT)
            pe_first(pe)
            overflow(pe, pe_more)

        def u_shuffle(copy, odd, done):
            uf = u_feat.rearrange("p f (c l) -> p f c l", l=L)
            for a_ in range(4):
                for t in range(4):
                    if (t % 2) != odd:
                        continue
                    dst = u_chunk[32 * t:32 * t + 32, :, 0:NC_ALL].rearrange("p (f a) c -> p f a c", a=4)[:, :, a_, :]
                    src = uf[32 * a_:32 * a_ + 32, :, 0:NC_ALL, t]
                    i = copy(dst, src)
                if odd:
                    dst = u_chunk[96:128, :, NC_ALL:].rearrange("p (f a) c -> p f a c", a=4)[:, :, a_, :]
                    i = copy(dst, u_feat[32 * a_:32 * a_ + 32, :, NMETA + SEQ:])
            i.then_inc(done, 1)

        def y_shuffle(copy, half, odd, done):
            ysb = st_re.rearrange("p (f a c) -> p f a c", f=2, a=4)
            yf = y_feat[:, 2 * half:2 * half + 2, 0:SEQ].rearrange("p f (c l) -> p f c l", l=L)
            for a_ in range(4):
                for t in range(4):
                    if (t % 2) != odd:
                        continue
                    i = copy(yf[32 * a_:32 * a_ + 32, :, :, t], ysb[32 * t:32 * t + 32, :, a_, NC_META:NC_ALL])
                if odd:
                    i = copy(y_feat[32 * a_:32 * a_ + 32, 2 * half:2 * half + 2, SEQ:],
                             ysb[96:128, :, a_, NC_ALL:])
            i.then_inc(done, 1)

        @block.sync
        def _(sp):
            def load(dst, src, name):
                sp.dma_start(dst, src).then_inc(s(name), 16)

            load(lam[:], ins["lam"], "ld_lam")
            load(x_tiles[:, 0, :], ins["x_prompt"][0, 0:P, :], "ld_tok0")
            sp.wait_ge(s("x4_zero"), 1)
            load(x_tiles[0:NS, TE, :], ins["x_sample"][:, 0, :], "ld_tok4")
            load(x_tiles[XM:XR, TE, :], ins["meta_tokens"], "ld_tok4")
            for i in range(1, 4):
                load(x_tiles[:, i, :], ins["x_prompt"][0, i * P:(i + 1) * P, :], f"ld_tok{i}")
            load(gain1, ins["norm1"].rearrange("a d -> (a d)").partition_broadcast(P), "ld_gain")
            load(ident[:], ins["c_ident"], "ld_id")
            w_in = ins["w_in"][0].rearrange("(k p) n -> p k n", p=P)

            def wblock(b, buf):
                dst = wbuf[:, 4096 * buf:4096 * (buf + 1)].rearrange("p (k n) -> p k n", k=KD)
                load(dst, w_in[:, :, 512 * b:512 * (b + 1)], f"ld_wbuf{buf}")

            wblock(0, 0)
            load(pb[:], ins["bc"], "ld_bc")
            load(mask_m[:], ins["c_mask_m"], "ld_mm")
            load(dskip[:], ins["dskip"], "ld_mm")
            wblock(3, 1)
            load(xs0[:], ins["xs0"], "ld_xs0")
            load(cosin[:], ins["c_cosin"], "ld_cos")
            load(mask_dec, ins["c_mask_dec"], "ld_cos")
            load(dec_cols[:], ins["c_dec"], "ld_cos")
            load(gam_pair[:], ins["c_gam"], "ld_cos")
            load(identb_tri[:].bitcast(U16), ins["c_tri"], "ld_tri")
            load(rconst[:], ins["c_route"], "ld_tri")
            load(iota_b[:].bitcast(U16), ins["c_iota"], "ld_tri")
            load(norms[:], ins["norms"], "ld_tri")
            sp.wait_ge(s("pe_u"), 4)
            wblock(2, 0)
            sp.wait_ge(s("pe_v"), NT)
            wblock(4, 1)
            for c, nm in ((2, "v"), (1, "k")):
                sp.wait_ge(s("a_v2" if nm == "v" else "d_k"), 1)
                src = v_tok[0:NS, TE, :] if nm == "v" else rotd[0][0:NS, :]
                sp.dma_start(qkv_dram[c], src).then_inc(s("st_kv4"), 16)
            sp.wait_ge(s("pe_k"), NT)
            wblock(1, 0)
            w_out = ins["w_out"][0].rearrange("(k p) n -> p k n", p=P)
            sp.wait_ge(s("pe_g"), NT)
            load(wbuf[:, 4096:].rearrange("p (k n) -> p k n", k=4), w_out[:, 0:4, :], "ld_wbuf1")
            sp.wait_ge(s("s5_state_ready"), 1)
            sp.dma_start(outs["s5_states"], fin_s5[:]).then_inc(s("st_out"), 16)
            sp.wait_ge(s("ret_state_ready"), 1)
            for g in range(2):
                sp.dma_start(outs["ret_prompt"][g], state_new[HD * g:HD * (g + 1), 0, :, :]).then_inc(s("st_out"), 16)
            sp.wait_ge(s("a_y"), 2)
            sp.wait_ge(s("a_yf"), 2)
            sp.wait_ge(s("d_yf"), 2)
            load(w_glu, ins["s5_w_glu"][0].rearrange("(k p) n -> p k n", p=P), "ld_glu")
            st_in = ins["state_ret"].rearrange("a b h d v -> (a b h) (d v)")
            for c in range(4):
                load(sm_st[c], st_in[:, D * c:D * (c + 1)], "ld_smst")
            sp.wait_ge(s("d_q"), 1)
            sp.dma_start(qkv_dram[0], rotd[0][0:NS, :]).then_inc(s("st_q4"), 16)
            sp.wait_ge(s("st_kv4"), 32)
            sp.wait_ge(s("st_q4"), 16)
            load(sm_qkv, qkv_dram.rearrange("c b (h d) -> (b h) c d", h=H), "ld_smq")
            sp.wait_ge(s("pe_q"), NT)
            load(wbuf[:, 0:4096].rearrange("p (k n) -> p k n", k=4), w_out[:, 4:8, :], "ld_wbuf0")
            for c in range(4):
                sp.wait_ge(s("sm_new"), c + 1)
                sp.dma_start(outs["ret_sample"][:, D * c:D * (c + 1)], sm_st[c]).then_inc(s("st_out"), 16)
            sp.wait_ge(s("sm_on"), 1)
            sp.dma_start(o_dram, sm_x[:, 0, :]).then_inc(s("st_o"), 16)
            sp.wait_ge(s("st_o"), 16)
            load(o_ex, o_dram.rearrange("(b h) d -> b (h d)", h=H), "ld_oex")
            sp.wait_ge(s("a_yr"), NT)
            sp.wait_ge(s("d_y2"), NT)
            load(gain2, ins["norm2"].rearrange("a d -> (a d)").partition_broadcast(P), "ld_gain")
            load(w_rt, ins["w_router"][0].rearrange("(p k) n -> p k n", k=KD), "ld_rt")
            load(acc[0:NS, TE, :], ins["x_sample"][:, 0, :], "ld_tok4")
            for i in range(4):
                load(acc[:, i, :], ins["x_prompt"][0, i * P:(i + 1) * P, :], f"ld_tok{i}")
            for n_, i in enumerate(TILES):
                r_ = NS if i == TE else P
                sp.wait_ge(s("d_h2"), n_ + 1)
                if n_ == NT - 1:
                    load(bias_b, ins["router_bias"].rearrange("a d -> (a d)").partition_broadcast(P), "ld_bt")
                    load(tri8, ins["c_tri8"], "ld_bt")
                sp.dma_start(h2_dram[P * i:P * i + r_, :], h2p[0:r_, n_ % 2, :]).then_inc(s(f"st_h2_{n_ % 2}"), 16)
            sp.wait_ge(s("xg_zero"), 1)
            sp.dma_start(sum_dram[TT:TT + SLOTS, :], ys[0]).then_inc(s("st_dump"), 16)
            sp.wait_ge(s("st_out"), 16 * 7)
            moe_sync(sp)

        @block.gpsimd
        def _(pool):
            n = [0]

            def seq(i):
                n[0] += 1
                i.then_inc(s("pool_seq"), 1)
                pool.wait_ge(s("pool_seq"), n[0])

            for half in range(2):
                gs = slice(HG * half, HG * (half + 1))
                er = phase_re.rearrange("p (g c) -> p g c", g=HG)
                ei = phase_im.rearrange("p (g c) -> p g c", g=HG)
                if half == 0:
                    pool.wait_ge(s("prm_ready"), 1)
                else:
                    pool.wait_ge(s("z_ready"), 1)
                    pool.wait_ge(s("pe_y"), 3)
                sc = prm[:, 29:33, gs]
                seq(pool.tensor_copy(sc[:, 0, :], prm[:, 20, gs]))
                seq(pool.tensor_copy(sc[:, 1, :], prm[:, 21, gs]))
                seq(pool.memset(er[:, :, 0:1], 1.0))
                seq(pool.memset(ei[:, :, 0:1], 0.0))
                w = 1
                while w < NCS:
                    m = min(w, NCS - w)
                    cr = bc(sc[:, 0, :].unsqueeze(2), [P, HG, m])
                    ci = bc(sc[:, 1, :].unsqueeze(2), [P, HG, m])
                    t1 = rot_im[:, 0:HG * m].rearrange("p (g c) -> p g c", g=HG)
                    t2 = rot_im[:, 512:512 + HG * m].rearrange("p (g c) -> p g c", g=HG)
                    pool.tensor_tensor(t1, er[:, :, 0:m], cr, ALU.mult)
                    seq(pool.tensor_tensor(t2, ei[:, :, 0:m], ci, ALU.mult))
                    seq(pool.tensor_tensor(er[:, :, w:w + m], t1, t2, ALU.subtract))
                    pool.tensor_tensor(t1, er[:, :, 0:m], ci, ALU.mult)
                    seq(pool.tensor_tensor(t2, ei[:, :, 0:m], cr, ALU.mult))
                    seq(pool.tensor_tensor(ei[:, :, w:w + m], t1, t2, ALU.add))
                    w *= 2
                    if w < NCS:
                        pool.tensor_tensor(sc[:, 2, :], sc[:, 0, :], sc[:, 1, :], ALU.mult)
                        seq(pool.tensor_tensor(sc[:, 3, :], sc[:, 1, :], sc[:, 1, :], ALU.mult))
                        pool.tensor_scalar(sc[:, 0, :], sc[:, 3, :], -2.0, 1.0, ALU.mult, ALU.add)
                        seq(pool.tensor_scalar(sc[:, 1, :], sc[:, 2, :], 2.0, None, ALU.mult))
                pool.memset(rot_im[:, 0:1], 0.0).then_inc(s("phase_ready"), 1)

            pool.wait_ge(s("ld_smq"), 16)
            seq(pool.tensor_scalar(sm_x[:, 0, :], sm_qkv[:, 1, :], float(HD ** -0.5), None, ALU.mult))
            part = lambda w: w.rearrange("p (d v) -> p d v", v=HD)
            for c in range(4):
                pool.tensor_tensor(part(sm_kv[c]), bc(sm_x[:, 0, 16 * c:16 * c + 16].unsqueeze(2), [SR, 16, HD]),
                                   bc(sm_qkv[:, 2, :].unsqueeze(1), [SR, 16, HD]), ALU.mult).then_inc(s("sm_kv"), 1)
            for c in range(4):
                pool.wait_ge(s("sm_new"), c + 1)
                pool.tensor_tensor(part(sm_kv[c]), part(sm_st[c]),
                                   bc(sm_qkv[:, 0, 16 * c:16 * c + 16].unsqueeze(2), [SR, 16, HD]),
                                   ALU.mult).then_inc(s("sm_qn"), 1)
            moe_pool(pool)

        @block.scalar
        def _(act):
            def a(out, in_, f, **kw):
                return nc.scalar.activation(out, in_, f, **kw)

            act.wait_ge(s("ld_lam"), 16)
            a(prm[:, 0, :], lam[:, 2, :], ACT.Exp).then_inc(s("a_dt"), 1)
            act.wait_ge(s("d_z"), 1)
            for j, e in enumerate((1, 2, 3, 4, -1, -2, -3)):
                i = a(prm[:, 3 + j, :], prm[:, 1, :], ACT.Exp, scale=float(e))
            i.then_inc(s("a_pow"), 1)
            for n_, i in enumerate((0, 4, 1, 2, 3)):
                act.wait_ge(s("d_stat0"), 1)
                if n_:
                    act.wait_ge(s("a_ss"), n_)
                if i == 4:
                    act.wait_ge(s("ld_tok4"), 32)
                else:
                    act.wait_ge(s(f"ld_tok{i}"), 16)
                r = XR if i == TE else P
                a(xn_bufs[0:r, 0, :], x_tiles[0:r, i, :], ACT.Square, accum_out=stat[0:r, 0, i:i + 1]).then_inc(s("a_ss"), 1)
            act.wait_ge(s("a_ss"), NT)
            a(stat[:, 1, 0:NT], stat[:, 0, 0:NT], ACT.Sqrt, scale=1.0 / D, bias=stat[:, 7, 0:1]).then_inc(s("a_rt"), 1)
            act.wait_ge(s("d_th"), 1)
            a(prm[:, 12, :], prm[:, 11, :], ACT.Sin)
            a(prm[:, 13, :], prm[:, 11, :], ACT.Sin, scale=0.5).then_inc(s("a_sin"), 1)
            for n_, i in enumerate((4, 0, 1, 2, 3)):
                r = XR if i == TE else P
                for hf in range(2):
                    act.wait_ge(s("pe_xt"), 2 * n_ + hf + 1)
                    b = bank[2 * (n_ % 2) + hf]
                    nc.scalar.copy(hT[:, 4 * hf:4 * hf + 4, P * i:P * i + r],
                                   b[:, :].rearrange("p (k t) -> p k t", k=4)[:, :, 0:r]).then_inc(s("a_ht"), 1)
            for ft in range(4):
                act.wait_ge(s("pe_u"), ft + 1)
                nc.scalar.copy(u_feat[:, ft, NMETA:NMETA + SEQ], bank[4 + 2 * (ft % 2)][:, :])
                nc.scalar.copy(u_feat[:, ft, 0:NMETA], bank[5 + 2 * (ft % 2)][:, XM:XR])
                nc.scalar.copy(u_feat[:, ft, NMETA + SEQ:], bank[5 + 2 * (ft % 2)][:, 0:NS]).then_inc(s("a_u"), 1)
            act.wait_ge(s("a_u"), 4)
            act.wait_ge(s("d_uzero"), 1)
            u_shuffle(nc.scalar.copy, 1, s("a_uc"))

            def s5_evac(half):
                for n_ in range(4):
                    act.wait_ge(s("pe_vt"), 4 * half + n_ + 1)
                    nc.scalar.copy((v_re, v_im)[n_ // 2][:, 512 * (n_ % 2):512 * (n_ % 2 + 1)],
                                   bank[2 + n_][:, :]).then_inc(s("a_v"), 1)
                for n_ in range(6):
                    act.wait_ge(s("pe_s"), 6 * half + n_ + 1)
                    g0, g1 = 3 * (n_ % 3), min(3 * (n_ % 3) + 3, HG)
                    nc.scalar.copy((st_re, st_im)[n_ // 3][:, NCS * g0:NCS * g1],
                                   bank[2 + n_][:, 0:NCS * (g1 - g0)]).then_inc(s("a_s"), 1)

            def y_evac(half):
                for n_ in range(3):
                    act.wait_ge(s("pe_y"), 3 * half + n_ + 1)
                    g0, g1 = 3 * n_, min(3 * n_ + 3, HG)
                    i = nc.scalar.copy(st_re[:, NCS * g0:NCS * g1], bank[2 + n_][:, 0:NCS * (g1 - g0)])
                i.then_inc(s("a_y"), 1)
                act.wait_ge(s("a_y"), half + 1)
                y_shuffle(nc.scalar.copy, half, 1, s("a_yf"))

            n = [0]

            def aseq(i_):
                n[0] += 1
                i_.then_inc(s("act_seq"), 1)
                act.wait_ge(s("act_seq"), n[0])

            def rows(i_):
                return XR if i_ == TE else P

            s5_evac(0)
            for n_, i in enumerate(TILES):
                act.wait_ge(s("pe_v"), n_ + 1)
                if n_ == 0:
                    act.wait_ge(s("pe_xt"), 10)
                nc.scalar.copy(v_tok[0:rows(i), i, :], bank[n_ % 2][0:rows(i), :]).then_inc(s("a_v2"), 1)
            for c in range(4):
                act.wait_ge(s("pe_kt"), c + 1)
                nc.scalar.copy(kT[:, :, P * c:P * (c + 1)],
                               bank[6][:, :].rearrange("p (a t) -> p a t", a=4)).then_inc(s("a_kt"), 1)
            y_evac(0)
            s5_evac(1)
            for n_, i in enumerate(TILES):
                act.wait_ge(s("pe_g"), n_ + 1)
                a(gate_tok[0:rows(i), i, :], bank[n_ % 2][0:rows(i), :], ACT.Silu).then_inc(s("a_g"), 1)
            y_evac(1)
            act.wait_ge(s("a_yf"), 2)
            act.wait_ge(s("d_yf"), 2)
            a(y_feat, y_feat, ACT.Gelu_apprx_tanh).then_inc(s("a_gelu"), 1)

            def yr_evac(k_, c0, c1):
                act.wait_ge(s("pe_yrt"), k_ + 1)
                for a_ in range(4):
                    i_ = a(yr_feat[:, a_, c0:c1], bank[7][:, P * a_:P * a_ + c1 - c0], ACT.Copy,
                           scale=norms[:, 1, a_:a_ + 1])
                i_.then_inc(s("a_yr"), 1)

            act.wait_ge(s("ld_tri"), 16 * 4)
            for c in range(4):
                act.wait_ge(s("pe_qt"), c + 1)
                nc.scalar.copy(qT[:, c % 2], bank[6][:, :].rearrange("p (a t) -> p a t", a=4)).then_inc(s("a_qt"), 1)
                if c >= 1:
                    yr_evac(c - 1, P * (c - 1), P * c)
                act.wait_ge(s("d_var"), c + 1)
                a(hst[:, 2, :], hst[:, 1, :], ACT.Sqrt, scale=1.0 / HD, bias=stat[:, 7, 0:1]).then_inc(s("a_sd"), 1)
            yr_evac(3, P * 3, P * 4)
            for f in range(4):
                act.wait_ge(s("pe_glu"), f + 1)
                a(glu_t[:, f, 0:SEQ], bank[f][:, :], ACT.Tanh, scale=0.5)
                a(glu_t[:, f, SEQ:], bank[4 + f][:, 0:NS], ACT.Tanh, scale=0.5).then_inc(s("a_tanh"), 1)
            for f in range(4):
                act.wait_ge(s("d_glu"), f + 1)
                a(glu_sq[:, f, :], y_feat[:, f, :], ACT.Square).then_inc(s("a_sq"), 1)
            act.wait_ge(s("sm_var"), 1)
            a(hst[0:SR, 2, 0:1], hst[0:SR, 1, 0:1], ACT.Sqrt, scale=1.0 / HD, bias=stat[0:SR, 7, 0:1]).then_inc(s("a_sd"), 1)
            act.wait_ge(s("pe_ss"), 1)
            act.wait_ge(s("d_statz"), 1)
            a(stat[:, 4, 0:4], bank[7][:, 0:4], ACT.Sqrt, scale=1.0 / DS5, bias=stat[:, 7, 0:1])
            a(stat[0:NS, 4, TE:NT], bank[7][0:NS, TE:NT], ACT.Sqrt, scale=1.0 / DS5,
              bias=stat[0:NS, 7, 0:1]).then_inc(s("a_rs5"), 1)
            yr_evac(4, SEQ, TT)
            for n_, i in enumerate(TILES):
                r = NS if i == TE else P
                act.wait_ge(s("d_x2"), n_ + 1)
                if n_ >= 2:
                    act.wait_ge(s("pe_h2t"), 2 * (n_ - 1))
                    act.wait_ge(s(f"st_h2_{n_ % 2}"), 16 * (n_ // 2))
                a(h2p[0:r, n_ % 2, :], acc[0:r, i, :], ACT.Square, accum_out=stat[0:r, 8, i:i + 1]).then_inc(s("a_ss2"), 1)
                act.wait_ge(s("a_ss2"), n_ + 1)
                a(stat[0:r, 9, i:i + 1], stat[0:r, 8, i:i + 1], ACT.Sqrt, scale=1.0 / D,
                  bias=stat[0:r, 7, 0:1]).then_inc(s("a_rt2"), 1)
                if n_ >= 1:
                    h2t_evac(n_ - 1)
            h2t_evac(NT - 1)
            moe_act(act)

        @block.vector
        def _(dve):
            v = nc.vector
            n = [0]

            def seq(i):
                n[0] += 1
                i.then_inc(s("dve_seq"), 1)
                dve.wait_ge(s("dve_seq"), n[0])

            def tt(o, a_, b_, op):
                return v.tensor_tensor(o, a_, b_, op)

            v.memset(x_tiles[0:XR, TE, :], 0.0).then_inc(s("x4_zero"), 1)
            v.memset(ones_col[:], 1.0)
            v.memset(stat[:], EPS).then_inc(s("d_stat0"), 1)
            R = lambda i: prm[:, i, :]
            dve.wait_ge(s("a_dt"), 1)
            seq(tt(R(1), lam[:, 0, :], R(0), ALU.mult))
            seq(tt(R(2), lam[:, 1, :], R(0), ALU.mult))
            v.memset(u_chunk[:, :, NC_ALL:], 0.0).then_inc(s("d_uzero"), 1)
            v.tensor_copy(R(33), R(1)).then_inc(s("d_z"), 1)
            seq(v.tensor_scalar(R(10), R(2), 1.0 / (2 * np.pi), MAGIC, ALU.mult, ALU.add))
            seq(v.tensor_scalar(R(10), R(10), -MAGIC, None, ALU.add))
            seq(v.scalar_tensor_tensor(R(11), R(10), -C1, R(2), ALU.mult, ALU.add))
            seq(v.scalar_tensor_tensor(R(11), R(10), -C2, R(11), ALU.mult, ALU.add))
            seq(v.scalar_tensor_tensor(R(11), R(10), -C3, R(11), ALU.mult, ALU.add))
            v.tensor_scalar(R(11), R(11), 3.141592, -3.141592, ALU.min, ALU.max).then_inc(s("d_th"), 1)
            dve.wait_ge(s("a_rt"), 1)
            seq(v.reciprocal(stat[:, 2, 0:NT], stat[:, 1, 0:NT]))
            dve.wait_ge(s("ld_gain"), 16)
            for n_, i in enumerate((4, 0, 1, 2, 3)):
                r = XR if i == TE else P
                if n_ >= 2:
                    dve.wait_ge(s("pe_xt"), 2 * (n_ - 1))
                v.scalar_tensor_tensor(xn_bufs[0:r, n_ % 2, :], x_tiles[0:r, i, :], stat[0:r, 2, i:i + 1],
                                       gain1[0:r, :], ALU.mult, ALU.mult).then_inc(s("d_xn"), 1)
            dve.wait_ge(s("a_sin"), 1)
            dve.wait_ge(s("a_pow"), 1)
            seq(tt(R(14), R(13), R(13), ALU.mult))
            seq(v.tensor_scalar(R(14), R(14), -2.0, 1.0, ALU.mult, ALU.add))
            seq(tt(R(15), R(12), R(12), ALU.mult))
            seq(v.tensor_scalar(R(16), R(15), -2.0, 1.0, ALU.mult, ALU.add))
            seq(v.scalar_tensor_tensor(R(17), R(12), 2.0, R(14), ALU.mult, ALU.mult))
            seq(tt(R(15), R(17), R(17), ALU.mult))
            seq(v.tensor_scalar(R(20), R(15), -2.0, 1.0, ALU.mult, ALU.add))
            seq(v.scalar_tensor_tensor(R(21), R(17), 2.0, R(16), ALU.mult, ALU.mult))
            v.memset(over[:], 0.0).then_inc(s("prm_ready"), 1)
            seq(tt(R(15), R(17), R(12), ALU.mult))
            seq(tt(R(18), R(16), R(14), ALU.mult))
            seq(tt(R(18), R(18), R(15), ALU.subtract))
            seq(tt(R(15), R(16), R(12), ALU.mult))
            seq(tt(R(19), R(17), R(14), ALU.mult))
            seq(tt(R(19), R(19), R(15), ALU.add))
            cs = {1: (14, 12), 2: (16, 17), 3: (18, 19)}
            v.memset(pw[:, 0:4:2, :, 3], 1.0)
            v.memset(pw[:, 1:4:2, :, 3], 0.0)
            for j in (1, 2, 3):
                c_, s_ = cs[j]
                seq(tt(pw[:, 0, :, 3 - j], R(3 + j - 1), R(c_), ALU.mult))
                seq(tt(pw[:, 1, :, 3 - j], R(3 + j - 1), R(s_), ALU.mult))
                seq(tt(pw[:, 2, :, 3 - j], R(7 + j - 1), R(c_), ALU.mult))
                seq(v.scalar_tensor_tensor(pw[:, 3, :, 3 - j], R(7 + j - 1), -1.0, R(s_), ALU.mult, ALU.mult))
            seq(v.tensor_scalar(R(22), pw[:, 0, :, 2], -1.0, None, ALU.add))
            ni = pw[:, 1, :, 2]
            seq(tt(R(23), R(22), lam[:, 0, :], ALU.mult))
            seq(tt(R(24), ni, lam[:, 1, :], ALU.mult))
            seq(tt(R(23), R(23), R(24), ALU.add))
            seq(tt(R(24), ni, lam[:, 0, :], ALU.mult))
            seq(tt(R(25), R(22), lam[:, 1, :], ALU.mult))
            seq(tt(R(24), R(24), R(25), ALU.subtract))
            seq(tt(R(25), lam[:, 0, :], lam[:, 0, :], ALU.mult))
            seq(tt(R(26), lam[:, 1, :], lam[:, 1, :], ALU.mult))
            seq(tt(R(25), R(25), R(26), ALU.add))
            seq(v.reciprocal(R(26), R(25)))
            seq(tt(R(27), R(23), R(26), ALU.mult))
            seq(tt(R(28), R(24), R(26), ALU.mult))
            fr = bc(R(27).unsqueeze(2), [P, GP, 16])
            fi = bc(R(28).unsqueeze(2), [P, GP, 16])
            dve.wait_ge(s("ld_bc"), 16)
            seq(tt(bt[:, 0], pb[:, 0], fr, ALU.mult))
            seq(tt(bt[:, 1], pb[:, 1], fi, ALU.mult))
            seq(tt(bb[:, 0], bt[:, 0], bt[:, 1], ALU.subtract))
            seq(tt(bt[:, 0], pb[:, 1], fr, ALU.mult))
            seq(tt(bt[:, 1], pb[:, 0], fi, ALU.mult))
            seq(tt(bb[:, 1], bt[:, 0], bt[:, 1], ALU.add))
            seq(v.tensor_scalar(ncim[:], pb[:, 3], -1.0, None, ALU.mult))

            def blocks(w):
                return w.rearrange("p (g l b h) -> p g l b h", g=HG, l=L, b=2)

            def tell(i, name, value):
                i.then_inc(s(name), 1)
                dve.wait_ge(s(name), value)

            def tables(half):
                gs = slice(HG * half, HG * (half + 1))
                m1 = u_tmp[:, 0:512].rearrange("p (g l h) -> p g l h", g=HG, l=L)
                m2 = u_tmp[:, 512:1024].rearrange("p (g l h) -> p g l h", g=HG, l=L)
                for w in (vt_re, vt_im, wt_re, wt_im):
                    seq(v.memset(w, 0.0))
                sh = [P, HG, L, 16]
                for w, b0, p0, b1, p1, op in (
                        (vt_re, bb[:, 0], 0, bb[:, 1], 1, ALU.subtract), (vt_im, bb[:, 1], 0, bb[:, 0], 1, ALU.add),
                        (wt_re, pb[:, 2], 2, ncim[:], 3, ALU.add), (wt_im, ncim[:], 2, pb[:, 2], 3, ALU.subtract)):
                    seq(tt(m1, bc(b0[:, gs, :].unsqueeze(2), sh), bc(pw[:, p0, gs, :].unsqueeze(3), sh), ALU.mult))
                    seq(tt(m2, bc(b1[:, gs, :].unsqueeze(2), sh), bc(pw[:, p1, gs, :].unsqueeze(3), sh), ALU.mult))
                    for g2 in range(2):
                        r = slice(NST * g2, NST * (g2 + 1))
                        last = tt(blocks(w)[r, :, :, g2, :], m1[r], m2[r], op)
                        if not (w is wt_im and g2):
                            seq(last)
                tell(last, "d_tab", half + 1)

            def m_evac(half):
                for n_ in range(2):
                    dve.wait_ge(s("pe_m"), 2 * half + n_ + 1)
                    mm = m_mat[:, 512 * n_:512 * (n_ + 1)].rearrange("p (g t) -> p g t", g=4)
                    seq(tt(mm, bank[n_][:, :].rearrange("p (g t) -> p g t", g=4),
                           bc(mask_m[:].unsqueeze(1), [P, 4, P]), ALU.mult))
                for g in range(HG):
                    mm = m_mat[:, 128 * g:128 * (g + 1)]
                    last = v.scalar_tensor_tensor(mm, ident[:], dskip[:, HG * half + g:HG * half + g + 1], mm,
                                                  ALU.mult, ALU.add)
                tell(last, "d_m", half + 1)

            def scan(half):
                gs = slice(HG * half, HG * (half + 1))
                g3 = lambda w: w.rearrange("p (g c) -> p g c", g=HG)
                dve.wait_ge(s("a_s"), 6 * (half + 1))
                seq(v.tensor_copy(fin_s5[:, 0, gs, :], g3(st_re)[:, :, NC_ALL - 1:]))
                seq(v.tensor_copy(fin_s5[:, 1, gs, :], g3(st_im)[:, :, NC_ALL - 1:]))
                dve.wait_ge(s("phase_ready"), half + 1)
                seq(tt(rot_re, st_re, phase_re, ALU.mult))
                seq(tt(rot_im, st_im, phase_im, ALU.mult))
                seq(tt(rot_re, rot_re, rot_im, ALU.add))
                seq(tt(rot_im, st_im, phase_re, ALU.mult))
                seq(tt(st_re, st_re, phase_im, ALU.mult))
                seq(tt(rot_im, rot_im, st_re, ALU.subtract))
                for w, o in ((rot_re, st_re), (rot_im, st_im)):
                    for g in range(HG):
                        v.tensor_tensor_scan(o[:, NCS * g:NCS * g + NC_ALL], w[:, NCS * g:NCS * g + NC_ALL],
                                             bc(prm[:, 6, HG * half + g:HG * half + g + 1], [P, NC_ALL]),
                                             0.0, ALU.add, ALU.mult)
                o = e1 = slice(1, NC_ALL)
                zi = slice(0, NC_ALL - 1)
                seq(v.memset(over[:, 1:2], 0.0))
                seq(tt(g3(rot_re)[:, :, o], g3(st_re)[:, :, zi], g3(phase_re)[:, :, e1], ALU.mult))
                seq(tt(g3(rot_im)[:, :, o], g3(st_im)[:, :, zi], g3(phase_im)[:, :, e1], ALU.mult))
                seq(tt(g3(rot_re)[:, :, o], g3(rot_re)[:, :, o], g3(rot_im)[:, :, o], ALU.subtract))
                seq(tt(g3(rot_im)[:, :, o], g3(st_re)[:, :, zi], g3(phase_im)[:, :, e1], ALU.mult))
                seq(tt(g3(st_im)[:, :, zi], g3(st_im)[:, :, zi], g3(phase_re)[:, :, e1], ALU.mult))
                seq(tt(g3(rot_im)[:, :, o], g3(rot_im)[:, :, o], g3(st_im)[:, :, zi], ALU.add))
                seq(tt(fin_s5[:, 0, gs, 0:1], fin_s5[:, 0, gs, 0:1], g3(rot_re)[:, :, NC_ALL - 1:NC_ALL], ALU.add))
                seq(tt(fin_s5[:, 1, gs, 0:1], fin_s5[:, 1, gs, 0:1], g3(rot_im)[:, :, NC_ALL - 1:NC_ALL], ALU.add))
                seq(v.memset(g3(rot_re)[:, :, 0:1], 0.0))
                seq(v.memset(g3(rot_im)[:, :, 0:1], 0.0))
                ar = bc(pw[:, 0, gs, 2:3], [P, HG, NS])
                ai = bc(pw[:, 1, gs, 2:3], [P, HG, NS])
                smp = slice(NC_ALL, NCS)
                t1, t2 = g3(st_im)[:, :, 0:NS], g3(st_im)[:, :, NS:2 * NS]
                dve.wait_ge(s("ld_xs0"), 16)
                seq(tt(t1, xs0[:, 0, gs, :], ar, ALU.mult))
                seq(tt(t2, xs0[:, 1, gs, :], ai, ALU.mult))
                seq(tt(g3(rot_re)[:, :, smp], t1, t2, ALU.subtract))
                seq(tt(t1, xs0[:, 1, gs, :], ar, ALU.mult))
                seq(tt(t2, xs0[:, 0, gs, :], ai, ALU.mult))
                seq(tt(g3(rot_im)[:, :, smp], t1, t2, ALU.add))
                seq(tt(fin_s5[:, 0, gs, 1:], fin_s5[:, 0, gs, 1:], g3(rot_re)[:, :, smp], ALU.add))
                tell(tt(fin_s5[:, 1, gs, 1:], fin_s5[:, 1, gs, 1:], g3(rot_im)[:, :, smp], ALU.add), "z_ready", half + 1)

            u_tmp = rot_re

            def rows(i_):
                return XR if i_ == TE else P

            def rotate(dst, src, i_):
                r_ = rows(i_)
                h3 = lambda w: w[0:r_].rearrange("p (a d) -> p a d", d=HD // 2)
                h4 = lambda w: w[0:r_].rearrange("p (h b d) -> p h b d", b=2, d=HD // 2)
                co = bc(cosin[0:r_, 0, i_, :].unsqueeze(1), [r_, 2 * H, HD // 2])
                si = bc(cosin[0:r_, 1, i_, :].unsqueeze(1), [r_, 2 * H, HD // 2])
                seq(tt(h3(rt1), h3(src), co, ALU.mult))
                seq(tt(h3(rt2), h3(src), si, ALU.mult))
                seq(tt(h4(dst)[:, :, 0, :], h4(rt1)[:, :, 0, :], h4(rt2)[:, :, 1, :], ALU.subtract))
                return tt(h4(dst)[:, :, 1, :], h4(rt1)[:, :, 1, :], h4(rt2)[:, :, 0, :], ALU.add)

            def k_tile(n_, i_):
                r_ = rows(i_)
                dve.wait_ge(s("pe_k"), n_ + 1)
                if n_ == 0:
                    dve.wait_ge(s("ld_cos"), 16 * 4)
                if n_ >= 3:
                    dve.wait_ge(s("pe_kt"), n_ - 2)
                if n_ >= 2:
                    dve.wait_ge(s("pe_st"), n_ - 1)
                if n_ == 2:
                    dve.wait_ge(s("st_kv4"), 32)
                rot = rotd[n_ % 2]
                k_ = rotate(rot, bank[n_ % 2], i_)
                k_.then_inc(s("d_k"), 1)
                dve.wait_ge(s("d_k"), n_ + 1)
                hd = lambda w: w[0:r_].rearrange("p (h d) -> p h d", h=H)
                tt(hd(kdec[:, n_ % 2, :]), hd(rot),
                   bc(dec_cols[0:r_, 1 if i_ == TE else 0, :].unsqueeze(2), [r_, H, HD]), ALU.mult).then_inc(s("d_kd"), 1)
                dve.wait_ge(s("d_kd"), n_ + 1)

            def state_step(n_):
                dve.wait_ge(s("pe_st"), n_ + 1)
                for g in range(2):
                    r_ = slice(HD * g, HD * (g + 1))
                    ps = bank[7][r_, :].rearrange("p (a b v) -> p a b v", a=4, b=2)[:, :, g, :]
                    new = state_bd[r_, n_, :, HD * g:HD * (g + 1)] if n_ < 4 else state_new[r_, 0, :, :]
                    if n_ == 0:
                        last = v.tensor_copy(new, ps)
                        if g == 0:
                            seq(last)
                    else:
                        old = state_bd[r_, n_ - 1, :, HD * g:HD * (g + 1)]
                        seq(tt(state_new[r_, 1, :, :], old, bc(gam_pair[r_, :].unsqueeze(2), [HD, 4, HD]), ALU.mult))
                        last = tt(new, state_new[r_, 1, :, :], ps, ALU.add)
                        if g == 0:
                            seq(last)
                last.then_inc(s("d_st"), 1)
                dve.wait_ge(s("d_st"), n_ + 1)

            def head_norm(src, tmp, sq, cols, r_, nh):
                h_ = lambda w: w.rearrange("p (h d) -> p h d", h=nh)
                seq(v.tensor_reduce(hst[0:r_, 0, 0:nh], h_(src), AX.X, ALU.add))
                seq(v.tensor_scalar(hst[0:r_, 0, 0:nh], hst[0:r_, 0, 0:nh], 1.0 / HD, None, ALU.mult))
                seq(tt(h_(tmp), h_(src), bc(hst[0:r_, 0, 0:nh].unsqueeze(2), [r_, nh, HD]), ALU.subtract))
                seq(tt(sq, tmp, tmp, ALU.mult))
                return v.tensor_reduce(hst[0:r_, 1, 0:nh], h_(sq), AX.X, ALU.add)

            def q_tile(n_, i_):
                dve.wait_ge(s("pe_q"), n_ + 1)
                if n_ >= 3:
                    dve.wait_ge(s("pe_qt"), n_ - 2)
                if n_ == 2:
                    dve.wait_ge(s("st_q4"), 16)
                rotate(rotd[n_ % 2], bank[n_ % 2], i_).then_inc(s("d_q"), 1)
                dve.wait_ge(s("d_q"), n_ + 1)

            def attend(c):
                for hs in range(2):
                    dve.wait_ge(s("pe_sc"), 2 * c + hs + 1)
                    if c >= 1:
                        dve.wait_ge(s("pe_o"), c)
                    tt(probs[:, hs, :], bank[2 + hs][:, :], mask_dec[:, 512 * hs:512 * (hs + 1)],
                       ALU.mult).then_inc(s("d_pr"), 1)
                    dve.wait_ge(s("d_pr"), 2 * c + hs + 1)
                dve.wait_ge(s("pe_o"), c + 1)
                if c >= 1:
                    dve.wait_ge(s("pe_yrt"), c)
                seq(tt(on1.rearrange("p (h d) -> p h d", h=H), bank[4 + c % 2][:, :].rearrange("p (h d) -> p h d", h=H),
                       bc(dec_cols[:, 2, :].unsqueeze(2), [P, H, HD]), ALU.mult))
                head_norm(on1, on2, on3, None, P, H).then_inc(s("d_var"), 1)
                dve.wait_ge(s("a_sd"), c + 1)
                seq(v.reciprocal(hst[:, 3, :], hst[:, 2, :]))
                seq(tt(on2, on2, gate_tok[:, c, :], ALU.mult))
                tt(on1.rearrange("p (h d) -> p h d", h=H), on2.rearrange("p (h d) -> p h d", h=H),
                   bc(hst[:, 3, :].unsqueeze(2), [P, H, HD]), ALU.mult).then_inc(s("d_yr"), 1)
                dve.wait_ge(s("d_yr"), c + 1)

            tables(0)
            dve.wait_ge(s("a_u"), 4)
            dve.wait_ge(s("d_uzero"), 1)
            u_shuffle(v.tensor_copy, 0, s("d_uc"))
            dve.wait_ge(s("ld_mm"), 32)
            dve.wait_ge(s("ld_id"), 16)
            m_evac(0)
            scan(0)
            seq(v.memset(state_bd[:], 0.0))
            seq(v.memset(state_new[:], 0.0))
            for n_, i in enumerate(TILES):
                k_tile(n_, i)
                if n_ >= 1:
                    state_step(n_ - 1)
            state_step(NT - 1)
            tell(v.memset(over[:, 2:3], 0.0), "ret_state_ready", 1)
            dve.wait_ge(s("a_y"), 1)
            y_shuffle(v.tensor_copy, 0, 0, s("d_yf"))
            dve.wait_ge(s("a_yf"), 1)
            dve.wait_ge(s("d_yf"), 1)
            tables(1)
            m_evac(1)
            scan(1)
            tell(v.memset(over[:, 2:3], 0.0), "s5_state_ready", 1)
            dve.wait_ge(s("a_y"), 2)
            y_shuffle(v.tensor_copy, 1, 0, s("d_yf"))
            dve.wait_ge(s("a_g"), NT)
            q_tile(0, TE)
            for c in range(4):
                q_tile(c + 1, c)
                attend(c)

            dve.wait_ge(s("ld_smst"), 16 * 4)
            for c in range(4):
                dve.wait_ge(s("sm_kv"), c + 1)
                v.scalar_tensor_tensor(sm_st[c], sm_st[c], dec_cols[0:SR, 3, 0:1], sm_kv[c],
                                       ALU.mult, ALU.add).then_inc(s("sm_new"), 1)
            for f in range(4):
                dve.wait_ge(s("a_tanh"), f + 1)
                seq(v.tensor_scalar(glu_t[:, f, :], glu_t[:, f, :], 0.5, 0.5, ALU.mult, ALU.add))
                if f == 0:
                    dve.wait_ge(s("pe_glu"), 4)
                tt(y_feat[:, f, :], y_feat[:, f, :], glu_t[:, f, :], ALU.mult).then_inc(s("d_glu"), 1)
            for c in range(4):
                dve.wait_ge(s("sm_qn"), c + 1)
                last = v.tensor_reduce(sm_o[:, c, :], sm_kv[c].rearrange("p (d v) -> p v d", v=HD), AX.X, ALU.add)
            seq(last)
            seq(v.tensor_reduce(sm_x[:, 1, :], sm_o.rearrange("p c v -> p v c"), AX.X, ALU.add))
            head_norm(sm_x[:, 1, :], sm_x[:, 2, :], sm_x[:, 3, :], None, SR, 1).then_inc(s("sm_var"), 1)
            for f in range(4):
                dve.wait_ge(s("a_sq"), f + 1)
                v.tensor_scalar(y_feat[:, f, :], y_feat[:, f, :], norms[:, 0, f:f + 1], None, ALU.mult).then_inc(s("d_yn"), 1)
            v.memset(stat[:, 4, :], 1.0).then_inc(s("d_statz"), 1)
            dve.wait_ge(s("a_sd"), 5)
            seq(v.reciprocal(hst[0:SR, 3, 0:1], hst[0:SR, 2, 0:1]))
            v.tensor_scalar(sm_x[:, 0, :], sm_x[:, 2, :], hst[0:SR, 3, 0:1], None, ALU.mult).then_inc(s("sm_on"), 1)
            dve.wait_ge(s("ld_oex"), 16)
            dve.wait_ge(s("pe_yrt"), 4)
            tt(on1[0:NS, :], o_ex, gate_tok[0:NS, TE, :], ALU.mult).then_inc(s("d_yr"), 1)
            dve.wait_ge(s("a_rs5"), 1)
            seq(v.reciprocal(stat[:, 5, 0:NT], stat[:, 4, 0:NT]))
            v.memset(over[:, 2:3], 0.0).then_inc(s("d_y2"), NT)
            for n_, i in enumerate(TILES):
                r_ = NS if i == TE else P
                b = 4 * (n_ % 2)
                dve.wait_ge(s("pe_out"), n_ + 1)
                dve.wait_ge(s(f"ld_tok{i}"), 48 if i == TE else 32)
                for hf in range(2):
                    cl = slice(512 * hf, 512 * hf + 512)
                    seq(tt(acc[0:r_, i, cl], acc[0:r_, i, cl], bank[b + 2 + hf][0:r_, :], ALU.add))
                    last = v.scalar_tensor_tensor(acc[0:r_, i, cl], bank[b + hf][0:r_, :], stat[0:r_, 5, i:i + 1],
                                                  acc[0:r_, i, cl], ALU.mult, ALU.add)
                    if hf == 0:
                        seq(last)
                last.then_inc(s("d_x2"), 1)
                dve.wait_ge(s("a_rt2"), n_ + 1)
                if n_ == 0:
                    dve.wait_ge(s("ld_gain"), 32)
                seq(v.reciprocal(stat[0:r_, 10, i:i + 1], stat[0:r_, 9, i:i + 1]))
                v.scalar_tensor_tensor(h2p[0:r_, n_ % 2, :].rearrange("t (k p) -> t p k", k=KD),
                                       acc[0:r_, i, :].rearrange("t (p k) -> t p k", k=KD), stat[0:r_, 10, i:i + 1],
                                       gain2[0:r_, :].rearrange("t (p k) -> t p k", k=KD),
                                       ALU.mult, ALU.mult).then_inc(s("d_h2"), 1)
            moe_dve(dve)

        @block.tensor
        def _(pe):
            def mm(o, l, r, start, stop, **kw):
                return nc.tensor.matmul(o, l, r, start=start, stop=stop, skip_group_check=True, **kw)

            pe.wait_ge(s("ld_id"), 16)
            for n_, i in enumerate((4, 0, 1, 2, 3)):
                r = XR if i == TE else P
                pe.wait_ge(s("d_xn"), n_ + 1)
                for hf in range(2):
                    if n_ >= 2:
                        pe.wait_ge(s("a_ht"), 2 * (n_ - 2) + hf + 1)
                    for k in range(4):
                        kk = 4 * hf + k
                        t = nc.tensor.transpose(bank[2 * (n_ % 2) + hf][:, P * k:P * k + r],
                                                xn_bufs[0:r, n_ % 2, P * kk:P * kk + P], ident[0:r, 0:r])
                    t.then_inc(s("pe_xt"), 1)
            pe.wait_ge(s("a_ht"), 10)
            w = lambda buf: wbuf[:, 4096 * buf:4096 * (buf + 1)].rearrange("p (k n) -> p k n", k=KD)
            pe.wait_ge(s("ld_wbuf0"), 16)
            for ft in range(4):
                if ft >= 2:
                    pe.wait_ge(s("a_u"), ft - 1)
                for c0, c1, b in ((0, SEQ, 4), (SEQ, TC, 5)):
                    for k in range(KD):
                        t = mm(bank[b + 2 * (ft % 2)][:, 0:c1 - c0], w(0)[:, k, P * ft:P * ft + P],
                               hT[:, k, c0:c1], k == 0, k == KD - 1)
                t.then_inc(s("pe_u"), 1)

            def proj(name, load, buf, evac, after=None):
                pe.wait_ge(s(f"ld_wbuf{buf}"), 16 * load)
                for n_, i_ in enumerate(TILES):
                    if n_ >= 2:
                        pe.wait_ge(s(evac), n_ - 1)
                    r_ = XR if i_ == TE else P
                    for k_ in range(KD):
                        t_ = mm(bank[n_ % 2][0:r_, :], hT[:, k_, P * i_:P * i_ + r_], w(buf)[:, k_, :],
                                k_ == 0, k_ == KD - 1)
                    t_.then_inc(s(name), 1)
                    if after and n_ >= 1:
                        after(n_ - 1)
                if after:
                    after(NT - 1)

            def k_after(n_):
                i_ = TILES[n_]
                rot, kd = rotd[n_ % 2], kdec[:, n_ % 2, :]
                pe.wait_ge(s("d_k"), n_ + 1)
                if i_ != TE:
                    if n_ >= 2:
                        pe.wait_ge(s("a_kt"), n_ - 1)
                    for a_ in range(4):
                        t_ = nc.tensor.transpose(bank[6][:, P * a_:P * a_ + P], rot[:, P * a_:P * a_ + P], ident[:])
                    t_.then_inc(s("pe_kt"), 1)
                pe.wait_ge(s("d_kd"), n_ + 1)
                if n_ == 0:
                    pe.wait_ge(s("a_v2"), NT)
                if n_ >= 1:
                    pe.wait_ge(s("d_st"), n_)
                r_ = slice(XM, XR) if i_ == TE else slice(0, P)
                for a_ in range(4):
                    t_ = mm(bank[7][:, P * a_:P * a_ + P], kd[r_, P * a_:P * a_ + P],
                            v_tok[r_, i_, P * a_:P * a_ + P], True, True)
                t_.then_inc(s("pe_st"), 1)

            def q_after(n_):
                if n_ == 0:
                    return
                c = n_ - 1
                pe.wait_ge(s("d_q"), n_ + 1)
                if c >= 1:
                    pe.wait_ge(s("a_qt"), c)
                for a_ in range(4):
                    t_ = nc.tensor.transpose(bank[6][:, P * a_:P * a_ + P], rotd[n_ % 2][:, P * a_:P * a_ + P], ident[:])
                t_.then_inc(s("pe_qt"), 1)
                pe.wait_ge(s("a_qt"), c + 1)
                q_ = qT[:, c % 2]
                for hs in range(2):
                    if c >= 1:
                        pe.wait_ge(s("d_pr"), 2 * (c - 1) + hs + 1)
                    r_ = slice(HD * hs, HD * hs + HD)
                    for j_ in range(4):
                        t_ = mm(bank[2 + hs][:, P * j_:P * j_ + P], kT[r_, j_, P * c:P * c + P],
                                q_[r_, j_, :], True, True)
                    t_.then_inc(s("pe_sc"), 1)
                if c >= 1:
                    yr_transposes(c - 1)
                o = bank[4 + c % 2]
                for a_ in range(4):
                    mm(o[:, P * a_:P * a_ + P], q_[:, a_, :], state_bd[:, c, a_, :], a_ == 0, False)
                for hs in range(2):
                    pe.wait_ge(s("d_pr"), 2 * c + hs + 1)
                    for j_ in range(4):
                        h = 2 * j_ + hs
                        t_ = mm(o[:, HD * h:HD * h + HD], probs[:, hs, P * j_:P * j_ + P],
                                v_tok[:, c, HD * h:HD * h + HD], False, h == H - 1)
                t_.then_inc(s("pe_o"), 1)

            def yr_transposes(k_):
                r_ = NS if k_ == 4 else P
                pe.wait_ge(s("d_yr"), k_ + 1)
                if k_ >= 1:
                    pe.wait_ge(s("a_yr"), k_)
                for a_ in range(4):
                    t_ = nc.tensor.transpose(bank[7][:, P * a_:P * a_ + r_], on1[0:r_, P * a_:P * a_ + P],
                                             ident[0:r_, 0:r_])
                t_.then_inc(s("pe_yrt"), 1)

            def s5_prep(half):
                pe.wait_ge(s("d_tab"), half + 1)
                for n_ in range(2):
                    for g in range(4 * n_, 4 * n_ + 4):
                        o = bank[n_][:, 128 * (g - 4 * n_):128 * (g - 4 * n_) + 128]
                        c = slice(128 * g, 128 * g + 128)
                        mm(o, vt_re[:, c], wt_re[:, c], True, False)
                        t = mm(o, vt_im[:, c], wt_im[:, c], False, True)
                    t.then_inc(s("pe_m"), 1)
                for n_ in range(4):
                    for g in range(4):
                        c = 512 * (n_ % 2) + 128 * g
                        t = nc.tensor.transpose(bank[2 + n_][:, 128 * g:128 * g + 128],
                                                (vt_re, vt_im)[n_ // 2][:, c:c + 128], ident[:])
                    t.then_inc(s("pe_vt"), 1)
                pe.wait_ge(s("a_v"), 4 * (half + 1))
                pe.wait_ge(s("a_uc"), 1)
                pe.wait_ge(s("d_uc"), 1)
                for n_ in range(6):
                    g0, g1 = 3 * (n_ % 3), min(3 * (n_ % 3) + 3, HG)
                    for g in range(g0, g1):
                        t = mm(bank[2 + n_][:, NCS * (g - g0):NCS * (g - g0 + 1)],
                               (v_re, v_im)[n_ // 3][:, 128 * g:128 * g + 128], u_chunk[:, HG * half + g, :], True, True)
                    t.then_inc(s("pe_s"), 1)

            def s5_out(half):
                pe.wait_ge(s("z_ready"), half + 1)
                pe.wait_ge(s("d_m"), half + 1)
                for n_ in range(3):
                    g0, g1 = 3 * n_, min(3 * n_ + 3, HG)
                    for g in range(g0, g1):
                        o = bank[2 + n_][:, NCS * (g - g0):NCS * (g - g0 + 1)]
                        c = slice(128 * g, 128 * g + 128)
                        z = slice(NCS * g, NCS * g + NCS)
                        mm(o, m_mat[:, c], u_chunk[:, HG * half + g, :], True, False)
                        mm(o, wt_re[:, c], rot_re[:, z], False, False)
                        t = mm(o, wt_im[:, c], rot_im[:, z], False, True)
                    t.then_inc(s("pe_y"), 1)

            pe.wait_ge(s("a_u"), 4)
            s5_prep(0)
            pe.wait_ge(s("d_m"), 1)
            proj("pe_v", 1, 1, "a_v2")
            pe.wait_ge(s("a_s"), 6)
            pe.wait_ge(s("a_v2"), NT)
            proj("pe_k", 2, 0, "d_k", k_after)
            s5_out(0)
            pe.wait_ge(s("a_y"), 1)
            pe.wait_ge(s("d_k"), NT)
            pe.wait_ge(s("a_kt"), 4)
            pe.wait_ge(s("d_st"), NT)
            s5_prep(1)
            pe.wait_ge(s("d_m"), 2)
            proj("pe_g", 2, 1, "a_g")
            pe.wait_ge(s("a_s"), 12)
            s5_out(1)
            pe.wait_ge(s("a_y"), 2)
            pe.wait_ge(s("a_g"), NT)
            proj("pe_q", 3, 0, "d_q", q_after)
            yr_transposes(3)
            pe.wait_ge(s("ld_glu"), 16)
            pe.wait_ge(s("a_gelu"), 1)
            pe.wait_ge(s("d_q"), NT)
            pe.wait_ge(s("d_pr"), 8)
            pe.wait_ge(s("a_qt"), 4)
            pe.wait_ge(s("d_yr"), 4)
            pe.wait_ge(s("a_yr"), 4)
            for f in range(4):
                for c0, c1, b in ((0, SEQ, bank[f]), (SEQ, TT, bank[4 + f])):
                    for k in range(4):
                        t = mm(b[:, 0:c1 - c0], w_glu[:, k, P * f:P * f + P], y_feat[:, k, c0:c1], k == 0, k == 3)
                t.then_inc(s("pe_glu"), 1)
            pe.wait_ge(s("a_sq"), 4)
            pe.wait_ge(s("a_tanh"), 4)
            for n_, i in enumerate(TILES):
                r = NS if i == TE else P
                for f in range(4):
                    t = mm(bank[7][0:r, i:i + 1], glu_sq[:, f, P * i:P * i + r], ones_col[:, 0:1], f == 0, f == 3)
            t.then_inc(s("pe_ss"), 1)
            pe.wait_ge(s("a_rs5"), 1)
            yr_transposes(4)
            pe.wait_ge(s("a_yr"), NT)
            pe.wait_ge(s("d_yn"), 4)
            pe.wait_ge(s("ld_wbuf1"), 48)
            pe.wait_ge(s("ld_wbuf0"), 64)
            pe.wait_ge(s("a_rs5"), 1)

            def h2_transposes(n_):
                i_ = TILES[n_]
                r_ = NS if i_ == TE else P
                pe.wait_ge(s("d_h2"), n_ + 1)
                for hf_ in range(2):
                    for k_ in range(4):
                        kk = 4 * hf_ + k_
                        t_ = nc.tensor.transpose(bank[4 * (n_ % 2) + hf_][:, P * k_:P * k_ + r_],
                                                 h2p[0:r_, n_ % 2, P * kk:P * kk + P], ident[0:r_, 0:r_])
                    t_.then_inc(s("pe_h2t"), 1)

            wo = [wbuf[:, 4096:].rearrange("p (k n) -> p k n", k=4), wbuf[:, 0:4096].rearrange("p (k n) -> p k n", k=4)]
            for n_, i in enumerate(TILES):
                r = NS if i == TE else P
                for part, y in ((1, yr_feat), (0, y_feat)):
                    if n_ >= 2 and part == 0:
                        pe.wait_ge(s("a_h2t"), 2 * (n_ - 1))
                    for k in range(4):
                        for hf in range(2):
                            t = mm(bank[4 * (n_ % 2) + 2 * part + hf][0:r, :], y[:, k, P * i:P * i + r],
                                   wo[part][:, k, 512 * hf:512 * hf + 512], k == 0, k == 3)
                t.then_inc(s("pe_out"), 1)
                if n_ >= 1:
                    h2_transposes(n_ - 1)
            h2_transposes(NT - 1)
            moe_pe(pe)


_INS = ["x_prompt", "x_sample", "meta_tokens", "norm1", "w_in", "w_router", "router_bias", "w_gate_e", "w_up_e",
        "w_down_e", "w_gate_sh", "w_up_sh", "w_down_sh", "s5_w_glu", "w_out", "norm2", "final_norm", "state_ret"]


def shape_constants():
    c = {}
    c["c_ident"] = np.eye(P, dtype=np.float32)
    t = np.arange(P)
    c["c_mask_m"] = (t[None, :] // 32 >= t[:, None] // 32).astype(np.float32)
    bf16_bits = lambda w: (np.ascontiguousarray(w, np.float32).view(np.uint32) >> 16).astype(np.uint16)
    tri = np.zeros((P, 2, P), np.float32)
    tri[:, 0] = (t[:, None] < t[None, :])
    tri[:, 1] = 1
    c["c_tri"] = bf16_bits(tri)
    c["c_iota"] = bf16_bits(np.broadcast_to(np.arange(P, dtype=np.float32), (P, P)))
    half = HD // 2
    inv = np.float32(10000.0) ** (-np.arange(half, dtype=np.float32) / np.float32(half))
    pos = np.zeros((P, NT), np.float32)
    for i in range(4):
        pos[:, i] = NMETA + i * P + t
    pos[0:NS, TE] = PAST
    pos[XM:XR, TE] = np.arange(NMETA)
    ang = (pos[:, :, None] * inv[None, None, :]).astype(np.float32)
    co, si = np.cos(ang), np.sin(ang)
    c["c_cosin"] = np.ascontiguousarray(np.stack([co, si], 1)
                                        ).astype(np.float32)
    lg = np.log1p(-np.exp2(-5.0 - np.arange(H)))
    sc = HD ** -0.5
    m = (t[None, None, :] >= t[:, None, None]) * np.exp(-lg[None, :, None] * (t[:, None, None] + 1.0)) * sc
    c["c_mask_dec"] = m.reshape(P, 4, 2, P).swapaxes(1, 2).reshape(P, H * P).astype(np.float32)
    dec = np.zeros((P, 4, H))
    dec[:, 0] = np.exp(lg[None] * (P - 1.0 - t[:, None])) * sc
    dec[XM:XR, 1] = np.exp(lg[None] * (NMETA - 1.0 - np.arange(NMETA)[:, None])) * sc
    dec[:, 2] = np.exp(lg[None] * (t[:, None] + 1.0))
    dec[0:NS * H, 3, 0] = np.tile(np.exp(lg), NS)
    dec[0:NS * H, 3, 1] = sc
    c["c_dec"] = dec.astype(np.float32)
    c["c_gam"] = np.exp(P * lg).reshape(4, 2).repeat(HD, 1).T.astype(np.float32)
    r = np.zeros((P, 16), np.float32)
    r[:, 0] = TT + t
    r[:, 1:5] = 1
    r[0:NS, 5] = 1
    r[:, 6] = t
    c["c_route"] = r
    i8 = np.arange(8)
    c["c_tri8"] = np.broadcast_to((i8[None, :] < i8[:, None]).astype(np.float32).reshape(64), (P, 64)).copy()
    return c


_OUTS = {
    "y_prompt": (1, SEQ, D), "y_sample": (NS, 1, D), "s5_states": (P, 2, GP, 1 + NS), "ret_prompt": (2, HD, 4, HD),
    "ret_sample": (NS * H, HD * HD),
}


def kernel(**inputs):
    import concourse.bacc as _bacc
    from concourse.bass_utils import run_bass_kernel_spmd as _run

    a = {k: np.asarray(v) for k, v in inputs.items()}
    feed = {k: a[k] for k in _INS}
    pair = lambda w: np.ascontiguousarray(w.reshape((GP, 2) + w.shape[1:]).swapaxes(0, 1))
    lamT = [pair(w[0]).transpose(0, 2, 1).reshape(P, GP) for w in (a["s5_lam_re"], a["s5_lam_im"])]
    ldt = np.broadcast_to(a["s5_log_dt"][0].reshape(GP, 2).T[:, None, :], (2, NST, GP)).reshape(P, GP)
    feed["lam"] = np.stack(lamT + [ldt], 1)
    bs = [pair(w[0]).transpose(0, 2, 1, 3).reshape(P, GP, 16) for w in (a["s5_b_re"], a["s5_b_im"])]
    cs = [pair(w[0]).transpose(0, 3, 1, 2).reshape(P, GP, 16) for w in (a["s5_c_re"], a["s5_c_im"])]
    feed["bc"] = np.stack(bs + cs, 1)
    d = a["s5_d"][0].reshape(GP, 2 * 16).T
    feed["dskip"] = np.tile(d, (L, 1))
    xs = [w[0].reshape(NS, GP, 2, NST).transpose(2, 3, 1, 0).reshape(P, GP, NS)
          for w in (a["state_s5_re"], a["state_s5_im"])]
    feed["xs0"] = np.stack(xs, 1)
    feed["norms"] = np.stack([a["s5_norm"][0].reshape(4, P).T, a["ret_norm"][0].reshape(4, P).T,
                              a["ret_norm"][0].reshape(4, P).T], 1)
    feed.update(shape_constants())
    nc = _bacc.Bacc("TRN2", target_bir_lowering=False, num_devices=1)
    arrays, ins, outs = {}, {}, {}
    for k, w in feed.items():
        w = np.ascontiguousarray(w)
        arrays[f"in_{k}"] = w
        ins[k] = nc.dram_tensor(f"in_{k}", w.shape, mybir.dt.from_np(w.dtype), kind="ExternalInput").ap()
    for k, shape in _OUTS.items():
        outs[k] = nc.dram_tensor(f"out_{k}", shape, F32, kind="ExternalOutput").ap()
    kernel_program(nc, ins, outs)
    r = _run(nc, [arrays], core_ids=[0]).results[0]
    g = {k: np.asarray(r[f"out_{k}"]) for k in _OUTS}
    s5 = lambda w: w.reshape(2, NST, GP, -1).transpose(3, 2, 0, 1).reshape(1, -1, NG, NST)
    fin = g["s5_states"]
    return (g["y_prompt"], g["y_sample"], s5(fin[:, 0, :, 0:1]), s5(fin[:, 1, :, 0:1]),
            g["ret_prompt"].transpose(2, 0, 1, 3).reshape(1, 1, H, HD, HD),
            s5(fin[:, 0, :, 1:]), s5(fin[:, 1, :, 1:]), g["ret_sample"].reshape(1, NS, H, HD, HD))
```

```python
from contextlib import ExitStack

import numpy as np

import concourse.bass as bass
from concourse import mybir

ALU = mybir.AluOpType
ACT = mybir.ActivationFunctionType
AX = mybir.AxisListType
F32 = mybir.dt.float32
BF16 = mybir.dt.bfloat16
I32 = mybir.dt.int32
U32 = mybir.dt.uint32
U16 = mybir.dt.uint16

P = 128
D = 1024
KD = D // P
SEQ = 512
NMETA = 16
NS = 8
PAST = 4096
DS5 = 512
NG = 32
NST = 64
H = 8
HD = 64
NE = 64
TOPG = 4
TOPK = 8
FE = 256
SCALE_ROUTED = 2.5
EPS = 1e-6

L = 4
GP = NG // 2
HG = GP // 2
NC_META = NMETA // L
NC_ALL = (NMETA + SEQ) // L
NCS = NC_ALL + NS
TE = 4
XM = 32
XR = XM + NMETA
TC = SEQ + XR
TT = SEQ + NS
NT = 5
SLOTS = 128
MORE = -(-TT // SLOTS) - 1
JOBS = TT * TOPK // SLOTS // 4 * 4
MAGIC = 12582912.0
C1, C2 = 6.28125, 0.0019350051879882812
C3 = float(2 * np.pi - C1 - C2)


def kernel_program(nc, ins, outs):
    ctx = ExitStack()
    with ctx:
        arena = ctx.enter_context(nc.sbuf_tensor("arena", [P, 49920], F32))

        def at(off, n):
            return arena[:, off:off + n]

        def sb(name, shape, dt=F32):
            return ctx.enter_context(nc.sbuf_tensor(name, shape, dt))

        def sem(name):
            return ctx.enter_context(nc.semaphore(name))

        bank = [ctx.enter_context(nc.psum_tensor(f"bank{i}", [P, 512], F32)) for i in range(8)]

        HC = HG * NCS
        phase_re, phase_im = at(0, HC), at(1120, HC)
        rot_re, rot_im = at(2240, HC), at(3360, HC)
        st_re, st_im = at(4480, HC), at(5600, HC)
        vt_re, vt_im = at(4480, 1024), at(5600, 1024)
        wt_re, wt_im = at(6720, 1024), at(7744, 1024)
        m_mat = at(8768, 1024)
        v_re, v_im = at(9792, 1024), at(10816, 1024)
        u_chunk = at(11840, GP * NCS).rearrange("p (g c) -> p g c", g=GP)
        x_tiles = at(14080, NT * D).rearrange("p (t d) -> p t d", t=NT)
        xn_bufs = at(19200, 2 * D).rearrange("p (b d) -> p b d", b=2)
        gain1 = at(26880, D)
        v_tok = at(14080, NT * 512).rearrange("p (t f) -> p t f", t=NT)
        gate_tok = at(16640, NT * 512).rearrange("p (t f) -> p t f", t=NT)
        kT = at(19200, 4 * 512).rearrange("p (a t) -> p a t", a=4)
        qT = at(21248, 2 * 512).rearrange("p (b a t) -> p b a t", b=2, a=4)
        kdec = at(22272, 2 * 512).rearrange("p (b f) -> p b f", b=2)
        rt1, rt2 = at(23296, 512), at(23808, 512)
        rotd = [at(24320, 512), at(26880, 512)]
        probs = at(24832, 2 * 512).rearrange("p (b f) -> p b f", b=2)
        on1, on2, on3 = at(25856, 512), at(26368, 512), at(27904, 512)
        state_bd = at(28416, 4 * 512).rearrange("p (c a v) -> p c a v", c=4, a=4)
        state_new = at(30464, 512).rearrange("p (b a v) -> p b a v", b=2, a=4)
        u_feat = at(30976, 4 * 536).rearrange("p (f t) -> p f t", f=4)
        y_feat = at(30976, 4 * TT).rearrange("p (f t) -> p f t", f=4)
        yr_feat = at(33120, 4 * TT).rearrange("p (f t) -> p f t", f=4)
        wbuf = at(35200, 8192)
        w_glu = at(8704, 2048).rearrange("p (k n) -> p k n", k=4)
        hT = at(45440, KD * TC).rearrange("p (k t) -> p k t", k=KD)
        SR = NS * H
        sm_qkv = arena[0:SR, 0:192].rearrange("p (c d) -> p c d", c=3)
        sm_st = [arena[0:SR, 256 + D * b:256 + D * b + D] for b in range(4)]
        sm_kv = [arena[0:SR, 4352 + D * b:4352 + D * b + D] for b in range(4)]
        sm_o = arena[0:SR, 8448:8448 + 256].rearrange("p (c v) -> p c v", c=4)
        sm_x = arena[0:SR, 10752:10752 + 256].rearrange("p (c v) -> p c v", c=4)
        o_ex = arena[0:NS, 11008:11520]
        WSLOT = 6144
        wexp = [at(WSLOT * s, WSLOT) for s in range(4)]
        acc = at(24576, NT * D).rearrange("p (t d) -> p t d", t=NT)
        h2p = at(22272, 2 * D).rearrange("p (b d) -> p b d", b=2)
        glu_t = at(14080, 4 * TT).rearrange("p (f t) -> p f t", f=4)
        glu_sq = at(16160, 4 * TT).rearrange("p (f t) -> p f t", f=4)
        xg = [at(29696 + D * b, D) for b in range(2)]
        xgT = [at(31744 + D * b, D).rearrange("p (k t) -> p k t", k=KD) for b in range(2)]
        ys = [at(33792 + D * b, D) for b in range(2)]
        sil = [at(35840 + 256 * b, 256) for b in range(2)]
        actg = [at(36352 + 256 * b, 256) for b in range(2)]
        actT = [at(36864 + 256 * b, 256).rearrange("p (k t) -> p k t", k=2) for b in range(2)]
        TB = 37376
        small = [at(TB + 320 * i, 320).rearrange("p (t e) -> p t e", t=NT) for i in range(12)]
        hot = [at(TB + 3840 + 320 * b, 320).bitcast(BF16).rearrange("p (t s) -> p t s", t=NT) for b in range(2)]
        info_v = at(TB + 4480, 1280).bitcast(BF16).rearrange("p (t e c) -> p t e c", t=NT, c=8)
        h2T = at(45440, KD * TT).rearrange("p (k t) -> p k t", k=KD)
        gain2 = at(19200, D)
        gain_f = at(43392, D)

        ident = sb("ident", [P, P])
        identb_tri = sb("tri_ones", [P, 2, P], BF16)
        ones_col = sb("ones_col", [P, 2])
        cosin = sb("cosin", [P, 2, NT, HD // 2])
        mask_dec = at(43392, 1024)
        mask_m = sb("mask_m", [P, P])
        dec_cols = sb("dec_cols", [P, 4, H])
        gam_pair = sb("gam_pair", [P, 4])
        lam = sb("lam", [P, 3, GP])
        pb = at(44416, 1024).rearrange("p (a g h) -> p a g h", a=4, g=GP)
        bb = sb("bb", [P, 2, GP, 16])
        bt = at(4480, 512).rearrange("p (a g h) -> p a g h", a=2, g=GP)
        ncim = sb("ncim", [P, GP, 16])
        dskip = sb("dskip", [P, GP])
        pw = sb("pw", [P, 4, GP, L])
        prm = sb("prm", [P, 34, GP])
        xs0 = sb("xs0", [P, 2, GP, NS])
        fin_s5 = sb("fin_s5", [P, 2, GP, 1 + NS])
        stat = sb("stat", [P, 12, 8])
        norms = sb("norms", [P, 3, 4])
        hst = sb("hst", [P, 4, H])
        w_rt = at(20224, KD * NE).rearrange("p (k n) -> p k n", k=KD)
        bias_b = at(43136, NE)
        rconst = sb("rconst", [P, 16])
        iota_b = sb("iota_b", [P, P], BF16)
        tri8 = at(43200, NE)
        idx_all = at(43264, NE).bitcast(I32)
        gate_all = at(43328, NE)
        idx_buf = sb("idx_buf", [P, 4], I32)
        gate_buf = sb("gate_buf", [P, 4])
        marks = sb("marks", [P, 6])
        JT = JOBS + 4
        job_e, job_shift = small[0][:, 0, 0:JT], small[0][:, 1, 0:JT]
        job_ei = small[0][:, 2, 0:JT].bitcast(I32)
        n_more_i = small[0][0:1, 2, NE - 1:NE].bitcast(I32)
        idx_more, gate_more = small[0][:, 3, 0:JT].bitcast(I32), small[0][:, 4, 0:JT]
        done_mark, info_mark = marks[:, 2:3], marks[:, 3:4]
        INFO_OPS = 7

        h2_dram = nc.dram_tensor("h2_rows", [TT, D], F32, kind="Internal").ap()
        sum_dram = nc.dram_tensor("sum_rows", [TT + SLOTS, D], F32, kind="Internal").ap()
        qkv_dram = nc.dram_tensor("qkv_samples", [3, NS, 512], F32, kind="Internal").ap()
        o_dram = nc.dram_tensor("o_samples", [NS * H, HD], F32, kind="Internal").ap()

        S = {}

        def s(name):
            if name not in S:
                S[name] = sem(name)
            return S[name]

        block = ctx.enter_context(nc.Block())
        TILES = (TE, 0, 1, 2, 3)
        EARLY = (0, TE, 1, 2, 3)
        LATE = (0, 1, 2, 3, TE)

        def bc(ap, shape):
            return ap.to_broadcast(shape)

        def h2t_evac(n_):
            i_ = LATE[n_]
            r_ = NS if i_ == TE else P
            for hf in range(2):
                nc.scalar.wait_ge(s("pe_h2t"), 2 * n_ + hf + 1)
                nc.scalar.copy(h2T[:, 4 * hf:4 * hf + 4, P * i_:P * i_ + r_],
                               bank[4 * (n_ % 2) + hf][:, :].rearrange("p (k t) -> p k t", k=4)[:, :, 0:r_]
                               ).then_inc(s("a_h2t"), 1)

        def weights(slot, kind):
            return wexp[slot][:, 2048 * kind:2048 * (kind + 1)]

        def load_expert(sp, q, j, e, first):
            if not first:
                sp.wait_ge(s("pe_down"), 4 * q + j - 3)
            for kind, nm in enumerate(("w_gate_e", "w_up_e")):
                if not first and kind == 1:
                    sp.wait_ge(s("pe_half"), 4 * q + j - 1)
                sp.dma_start(weights(j, kind), ins[nm][0, bass.ds(e, 1)].rearrange("a (p k) f -> p (a k f)", p=P)
                             ).then_inc(s(f"w_slot{j}"), 16)
            if not first:
                sp.wait_ge(s("pe_gu"), 4 * q + j - 1)
            sp.dma_start(weights(j, 2), ins["w_down_e"][0, bass.ds(e, 1)].rearrange("a (p k) d -> p (a k d)", p=P)
                         ).then_inc(s(f"w_slot{j}"), 16)

        def moe_sync(sp):
            sp.dma_start(gain_f, ins["final_norm"].partition_broadcast(P)).then_inc(s("ld_gain"), 16)
            for j in range(2):
                load_expert(sp, 0, j, j, True)
            sp.wait_ge(s("pe_rt"), NT)
            sp.wait_ge(s("st_h2_0"), 16 * 3)
            sp.wait_ge(s("st_h2_1"), 16 * 2)
            load_expert(sp, 0, 3, 3, True)
            sp.wait_ge(s("pe_shared"), NT)
            load_expert(sp, 0, 2, 2, True)
            for n_, i in enumerate(LATE):
                r_ = NS if i == TE else P
                sp.wait_ge(s("d_sh"), n_ + 1)
                sp.dma_start(sum_dram[P * i:P * i + r_, :], acc[0:r_, i, :]).then_inc(s("st_sum"), 16)
            with sp.Fori(1, NE // 4) as q:
                for j in range(4):
                    load_expert(sp, q, j, 4 * q + j, False)
            overflow(sp, sync_more)
            sp.wait_ge(s("all_added"), 1)
            for n_, i in enumerate(LATE):
                r_ = NS if i == TE else P
                sp.dma_start(acc[0:r_, i, :], sum_dram[P * i:P * i + r_, :]).then_inc(s(f"ld_tok{i}"), 16)
            for n_, i in enumerate(LATE):
                sp.wait_ge(s("d_out"), n_ + 1)
                if i == TE:
                    sp.dma_start(outs["y_sample"][:, 0, :], acc[0:NS, TE, :]).then_inc(s("st_fin"), 16)
                else:
                    sp.dma_start(outs["y_prompt"][0, P * i:P * (i + 1), :], acc[:, i, :]).then_inc(s("st_fin"), 16)
            sp.wait_ge(s("st_fin"), 16 * 5)

        def sync_more(sp, k):
            for j in range(4):
                e = sp.value_load(job_ei[0:1, bass.ds(4 * k + j, 1)], min_val=0, max_val=NE - 1)
                load_expert(sp, NE // 4 + k, j, e, False)

        def overflow(eng, body):
            eng.wait_ge(s("jobs_ready"), 1)
            n_more = eng.value_load(n_more_i, min_val=0, max_val=JOBS)
            with eng.If(n_more > 0):
                body(eng, 0)
            with eng.If(n_more > 4):
                with eng.Fori(1, JOBS // 4) as k:
                    with eng.If(n_more > 4 * k):
                        body(eng, k)

        def settle(pool, kind, n):
            if not isinstance(n, int) or n:
                pool.wait_ge(s(f"settled{kind}"), n)
            mark = marks[0:1, kind:kind + 1]
            pool.tensor_tensor(mark, mark, mark, ALU.mult).then_inc(s(f"settled{kind}"), 1)

        def pool_step(pool, q, j, gate, idx):
            first = isinstance(q, int) and q == 0
            if not first:
                pool.wait_ge(s("scattered"), 16 * (4 * q + j - 3))
                pool.wait_ge(s("act_done"), 4 * q + j - 3)
            pool.tensor_copy(gate_buf[:, j:j + 1], gate).then_inc(s("gate_copied"), 1)
            pool.tensor_copy(idx_buf[:, j:j + 1], idx).then_inc(s("idx_copied"), 1)
            pool.wait_ge(s("idx_copied"), 4 * q + j + 1)
            if not first or j >= 2:
                pool.wait_ge(s("pe_xgt"), 4 * q + j - 1)
            settle(pool, 0, 4 * q + j)
            pool.indirect_dma_start(xg[j % 2], None, h2_dram, bass.IndirectOffsetOnAxis(idx_buf[:, j:j + 1].bitcast(U32), axis=0),
                                    bounds_check=TT - 1, oob_is_err=False).then_inc(s(f"gathered{j % 2}"), 16)

        def pool_scatter(pool, q, j):
            first = isinstance(q, int) and q == 0
            pool.wait_ge(s("a_ys"), 4 * q + j + 1)
            pool.wait_ge(s("d_ys"), 4 * q + j + 1)
            if not first or j >= 1:
                pool.wait_ge(s("scattered"), 16 * (4 * q + j))
            settle(pool, 1, 4 * q + j)
            pool.indirect_dma_start(sum_dram, bass.IndirectOffsetOnAxis(idx_buf[:, j:j + 1].bitcast(U32), axis=0),
                                    ys[j % 2], None, bounds_check=TT + SLOTS - 1, compute_op=ALU.add
                                    ).then_inc(s("scattered"), 16)

        def pool_first(pool):
            for j in range(4):
                pool_step(pool, 0, j, gate_all[:, j:j + 1], idx_all[:, j:j + 1])
                if j == 3:
                    pool.wait_ge(s("st_sum"), 16 * NT)
                    pool.wait_ge(s("st_dump"), 16)
                    pool_scatter(pool, 0, 0)
            with pool.Fori(1, NE // 4) as q:
                pool.wait_ge(s("info_ready"), q)
                for j in range(4):
                    e = bass.ds(4 * q + j, 1)
                    pool_step(pool, q, j, gate_all[:, e], idx_all[:, e])
                    pool_scatter(pool, q + ((j + 1) // 4 - 1), (j + 1) % 4)
            pool.wait_ge(s("info_ready"), NE // 4)
            for j in (0, 1):
                pool_step(pool, NE // 4, j, gate_more[:, j:j + 1], idx_more[:, j:j + 1])
                pool_scatter(pool, NE // 4 - 1, j + 1)
            pool_scatter(pool, NE // 4 - 1, 3)

        def pool_more(pool, k):
            q = NE // 4 + k
            for j in (2, 3):
                n_ = bass.ds(4 * k + j, 1)
                pool_step(pool, q, j, gate_more[:, n_], idx_more[:, n_])
                pool_scatter(pool, q, j - 2)
            pool.wait_ge(s("info_ready"), NE // 4 + k + 1)
            for j in (0, 1):
                n_ = bass.ds(4 * (k + 1) + j, 1)
                pool_step(pool, q + 1, j, gate_more[:, n_], idx_more[:, n_])
                pool_scatter(pool, q, j + 2)
            pool.wait_ge(s("scattered"), 16 * (4 * q + 4))
            mark = marks[0:1, 2:3]
            pool.wait_ge(s("group_done"), k + 1)
            pool.tensor_tensor(mark, mark, mark, ALU.mult).then_inc(s("group_done"), 1)

        def moe_pool(pool):
            pool.wait_ge(s("info_ready"), 1)
            pool.wait_ge(s("st_h2_0"), 16 * 3)
            pool.wait_ge(s("st_h2_1"), 16 * 2)
            pool.wait_ge(s("xg_zero"), 1)
            pool.memset(marks[:, 5:6], 0.0).then_inc(s("group_done"), 1)
            pool_first(pool)
            pool.wait_ge(s("scattered"), 16 * NE)
            overflow(pool, pool_more)
            pool.memset(marks[:, 4:5], 0.0).then_inc(s("all_added"), 1)

        def act_rows(act, q, j):
            first = isinstance(q, int) and q == 0
            n = 4 * q + j
            act.wait_ge(s("pe_xgt"), n + 1)
            if not first or j >= 2:
                act.wait_ge(s("pe_gu"), n - 1)
            nc.scalar.copy(xgT[j % 2][:, 0:4, :], bank[0][:, :].rearrange("p (k t) -> p k t", k=4)).then_inc(s("a_xgt"), 1)

        def act_step(act, q, j, last=False, alone=False):
            first = isinstance(q, int) and q == 0
            n = 4 * q + j
            act.wait_ge(s("pe_gu"), n + 1)
            if not first or j >= 2:
                act.wait_ge(s("act_done"), n - 1)
            nc.scalar.activation(sil[j % 2], bank[(2, 6)[j % 2]][:, 0:FE], ACT.Silu).then_inc(s("silu_done"), 1)
            if not last:
                act_rows(act, q + (j + 1) // 4, (j + 1) % 4)
            if (not first or j >= 1) and not (alone and j == 0):
                act_down(act, q if j else q - 1, (j - 1) % 4)

        def act_down(act, q, j):
            first = isinstance(q, int) and q == 0
            n = 4 * q + j
            act.wait_ge(s("pe_down"), n + 1)
            if not first or j >= 2:
                act.wait_ge(s("scattered"), 16 * (n - 1))
            nc.scalar.copy(ys[j % 2][:, 0:512], bank[4][:, :]).then_inc(s("a_ys"), 1)

        def act_first(act):
            act_rows(act, 0, 0)
            for j in range(4):
                act_step(act, 0, j)
            with act.Fori(1, NE // 4 - 1) as q:
                for j in range(4):
                    act_step(act, q, j)
            for j in range(4):
                act_step(act, NE // 4 - 1, j, last=j == 3)
            act_down(act, NE // 4 - 1, 3)

        def act_more(act, k):
            act_rows(act, NE // 4 + k, 0)
            for j in range(4):
                act_step(act, NE // 4 + k, j, j == 3, True)
            act_down(act, NE // 4 + k, 3)

        def moe_act(act):
            def a(out, in_, f, **kw):
                return nc.scalar.activation(out, in_, f, **kw)
            def shared_silu(n_):
                i = LATE[n_]
                r_ = NS if i == TE else P
                act.wait_ge(s("pe_shgu"), n_ + 1)
                if n_ >= 2:
                    act.wait_ge(s("d_shact"), n_ - 1)
                a(sil[n_ % 2][0:r_, :], bank[(6, 2)[n_ % 2]][0:r_, 0:FE], ACT.Silu).then_inc(s("a_shsil"), 1)

            shared_silu(0)
            act.wait_ge(s("pe_rt"), NT)
            act.wait_ge(s("lg_zero"), 1)
            a(small[0][:, 0:4, :], bank[0][:, 0:4 * NE].rearrange("p (t e) -> p t e", e=NE), ACT.Tanh, scale=0.5
              ).then_inc(s("a_lg"), 1)
            a(small[0][0:NS, TE, :], bank[0][0:NS, TE * NE:NT * NE], ACT.Tanh, scale=0.5).then_inc(s("a_lg"), 1)
            for n_ in range(1, NT):
                shared_silu(n_)
            act_first(act)
            overflow(act, act_more)
            a(stat[:, 11, 0:1], stat[:, 7, 0:1], ACT.Sqrt)
            for n_, i in enumerate(LATE):
                r_ = NS if i == TE else P
                act.wait_ge(s(f"ld_tok{i}"), 64 if i == TE else 48)
                a(h2p[0:r_, n_ % 2, :], acc[0:r_, i, :], ACT.Square, accum_out=stat[0:r_, 8, i:i + 1]).then_inc(s("a_ss2"), 1)
                act.wait_ge(s("a_ss2"), NT + n_ + 1)
                a(stat[0:r_, 9, i:i + 1], stat[0:r_, 8, i:i + 1], ACT.Sqrt, scale=1.0 / D,
                  bias=stat[0:r_, 7, 0:1]).then_inc(s("a_rt2"), 1)

        def dve_rows(dve, q, j):
            first = isinstance(q, int) and q == 0
            n = 4 * q + j
            dve.wait_ge(s("pe_xgt"), n + 1)
            if not first or j >= 2:
                dve.wait_ge(s("pe_gu"), n - 1)
            nc.vector.tensor_copy(xgT[j % 2][:, 4:8, :], bank[1][:, :].rearrange("p (k t) -> p k t", k=4)
                                  ).then_inc(s("d_xgt"), 1)

        def dve_step(dve, q, j, last=False, alone=False):
            first = isinstance(q, int) and q == 0
            n = 4 * q + j
            v = nc.vector
            dve.wait_ge(s("silu_done"), n + 1)
            dve.wait_ge(s("gate_copied"), n + 1)
            if not first or j >= 2:
                dve.wait_ge(s("pe_at"), n - 1)
            v.scalar_tensor_tensor(actg[j % 2].rearrange("t (k p) -> t p k", k=2), sil[j % 2].rearrange("t (p k) -> t p k", k=2),
                                   gate_buf[:, j:j + 1], bank[(2, 6)[j % 2]][:, FE:].rearrange("t (p k) -> t p k", k=2),
                                   ALU.mult, ALU.mult).then_inc(s("act_done"), 1)
            if not last:
                dve_rows(dve, q + (j + 1) // 4, (j + 1) % 4)
            if (not first or j >= 1) and not (alone and j == 0):
                dve_down(dve, q if j else q - 1, (j - 1) % 4)
            dve.wait_ge(s("pe_at"), n + 1)
            if not first or j >= 2:
                dve.wait_ge(s("pe_down"), n - 1)
            v.tensor_copy(actT[j % 2], bank[3][:, 0:256].rearrange("p (k t) -> p k t", k=2)).then_inc(s("d_at"), 1)

        def dve_down(dve, q, j):
            first = isinstance(q, int) and q == 0
            n = 4 * q + j
            dve.wait_ge(s("pe_down"), n + 1)
            if not first or j >= 2:
                dve.wait_ge(s("scattered"), 16 * (n - 1))
            nc.vector.tensor_copy(ys[j % 2][:, 512:1024], bank[5][:, :]).then_inc(s("d_ys"), 1)

        def hot_rows(half, ranks):
            for i in range(NT):
                last = nc.vector.tensor_scalar(hot[half][:, i, :], iota_b[:], ranks(i), None, ALU.is_equal)
            last.then_inc(s("hot_ready"), 1)

        def dve_info(dve):
            for e in range(2 * 4):
                if e >= 2:
                    dve.wait_ge(s("pe_info"), e - 1)
                hot_rows(e % 2, lambda i: small[1][:, i, e:e + 1])
            dve.wait_ge(s("pe_info"), 8)
            slot_info(dve, 8, 0, idx_all[:, 0:8], gate_all[:, 0:8])

        def dve_ahead(dve, q, j):
            for j2 in {0: (0,), 1: (1,), 2: (2, 3), 3: ()}[j]:
                n = 4 * (q + 2) + j2
                dve.wait_ge(s("pe_info"), n - 1)
                hot_rows(j2 % 2, lambda i: small[1][:, i, bass.ds(n, 1)])
            if j == 3:
                g = bass.ds(4 * (q + 2), 4)
                dve.wait_ge(s("pe_info"), 4 * (q + 2) + 4)
                slot_info(dve, 4, INFO_OPS * (q + 1), idx_all[:, g], gate_all[:, g])

        def slot_info(dve, ne, base, idx, gate):
            v = nc.vector
            ps = bank[7][:, 0:8 * ne].rearrange("p (e c) -> p e c", c=8)
            flat = small[3].rearrange("p t e -> p (t e)")
            col = lambda c: flat[:, ne * c:ne * (c + 1)]
            t0, t1 = small[2][:, 0, 0:ne], small[2][:, 1, 0:ne]
            v.tensor_copy(flat[:, 0:4 * ne].rearrange("p (c e) -> p e c", c=4), ps[:, :, 0:4]).then_inc(s("d_info"), 1)
            dve.wait_ge(s("d_info"), base + 1)
            v.scalar_tensor_tensor(t0, col(0), float(P), col(1), ALU.mult, ALU.add).then_inc(s("d_info"), 1)
            v.tensor_scalar(t1, col(2), -1.0, 1.0, ALU.mult, ALU.add).then_inc(s("d_info"), 1)
            dve.wait_ge(s("d_info"), base + 3)
            v.scalar_tensor_tensor(t0, t1, rconst[:, 0:1], t0, ALU.mult, ALU.add).then_inc(s("d_info"), 1)
            dve.wait_ge(s("d_info"), base + 4)
            v.tensor_tensor(t1, col(3), ps[:, :, 4], ALU.add).then_inc(s("d_info"), 1)
            dve.wait_ge(s("d_info"), base + 5)
            v.tensor_copy(idx, t0).then_inc(s("d_info"), 1)
            v.tensor_tensor(gate, t1, ps[:, :, 5], ALU.add).then_inc(s("d_info"), 1)
            dve.wait_ge(s("d_info"), base + INFO_OPS)
            v.memset(info_mark, 0.0).then_inc(s("info_ready"), 1)

        def dve_first(dve, seq):
            dve_rows(dve, 0, 0)
            for j in range(4):
                dve_step(dve, 0, j)
                dve_ahead(dve, 0, j)
                job_table(seq, j)
            with dve.Fori(1, NE // 4 - 2) as q:
                for j in range(4):
                    dve_step(dve, q, j)
                    dve_ahead(dve, q, j)
            for q in (NE // 4 - 2, NE // 4 - 1):
                for j in range(4):
                    dve_step(dve, q, j, last=q == NE // 4 - 1 and j == 3)
                    if q == NE // 4 - 2:
                        dve_ahead_more(dve, 0, j)
            dve_down(dve, NE // 4 - 1, 3)

        def job_table(seq, part):
            v = nc.vector
            cnt, xb, cum, js = (small[11][:, i_, :] for i_ in range(4))
            js, inval = js[:, 0:JOBS], small[11][:, 4, 0:JOBS]
            cmp = at(TB + 4 * 320, JOBS * NE).rearrange("p (j e) -> p j e", e=NE)
            sh = [P, JOBS, NE]
            je, jsh = job_e[:, 0:JOBS], job_shift[:, 0:JOBS]
            if part == 0:
                v.tensor_copy(js, iota_b[:, 0:JOBS])
                seq(v.tensor_scalar(xb, cnt, float(SLOTS), None, ALU.is_gt))
                for m in range(2, MORE + 1):
                    seq(v.scalar_tensor_tensor(xb, cnt, float(SLOTS * m), xb, ALU.is_gt, ALU.add))
                seq(v.tensor_tensor_scan(cum, xb, bc(ones_col[:, 0:1], [P, NE]), 0.0, ALU.add, ALU.mult))
                seq(v.tensor_tensor(cmp, bc(cum.unsqueeze(1), sh), bc(js.unsqueeze(2), sh), ALU.is_le))
            elif part == 1:
                seq(v.memset(job_e[:, JOBS:], 0.0))
                seq(v.tensor_reduce(je, cmp, AX.X, ALU.add))
                seq(v.tensor_tensor(cmp, cmp, bc(xb.unsqueeze(1), sh), ALU.mult))
            elif part == 2:
                seq(v.memset(job_shift[:, JOBS:], float(SLOTS * TT)))
                seq(v.tensor_reduce(jsh, cmp, AX.X, ALU.add))
                seq(v.tensor_tensor(jsh, js, jsh, ALU.subtract))
                seq(v.tensor_scalar(inval, js, cum[:, NE - 1:NE], float(TT), ALU.is_ge, ALU.mult))
                seq(v.tensor_tensor(jsh, jsh, inval, ALU.add))
                seq(v.tensor_scalar(jsh, jsh, 1.0, float(SLOTS), ALU.add, ALU.mult))
            else:
                seq(v.tensor_scalar(job_e, job_e, float(NE - 1), None, ALU.min))
                seq(v.tensor_copy(job_ei, job_e))
                seq(v.tensor_copy(n_more_i, cum[0:1, NE - 1:NE]))
                v.memset(done_mark, 0.0).then_inc(s("jobs_ready"), 1)

        def dve_ahead_more(dve, k, j):
            n = NE + 4 * k
            for j2 in {0: (0,), 1: (1,), 2: (2, 3), 3: ()}[j]:
                if isinstance(k, int):
                    e = dve.value_load(job_ei[0:1, 4 * k + j2:4 * k + j2 + 1], min_val=0, max_val=NE - 1)
                else:
                    e = dve.value_load(job_ei[0:1, bass.ds(4 * k + j2, 1)], min_val=0, max_val=NE - 1)
                nc.vector.tensor_tensor(small[2][:, :, j2:j2 + 1], small[1][:, :, bass.ds(e, 1)],
                                        bc(job_shift[:, bass.ds(4 * k + j2, 1)].unsqueeze(1), [P, NT, 1]), ALU.subtract
                                        ).then_inc(s("rank_shift"), 1)
                dve.wait_ge(s("rank_shift"), 4 * k + j2 + 1)
                dve.wait_ge(s("pe_info"), n + j2 - 1)
                hot_rows(j2 % 2, lambda i: small[2][:, i, j2:j2 + 1])
            if j == 3:
                g = bass.ds(4 * k, 4)
                dve.wait_ge(s("pe_info"), n + 4)
                slot_info(dve, 4, INFO_OPS * (NE // 4 - 1 + k), idx_more[:, g], gate_more[:, g])

        def dve_more(dve, k):
            dve_rows(dve, NE // 4 + k, 0)
            for j in range(4):
                dve_step(dve, NE // 4 + k, j, j == 3, True)
                dve_ahead_more(dve, k + 1, j)
            dve_down(dve, NE // 4 + k, 3)

        def moe_dve(dve):
            v = nc.vector
            n = [0]

            def seq(i):
                n[0] += 1
                i.then_inc(s("moe_seq"), 1)
                dve.wait_ge(s("moe_seq"), n[0])

            def tt(o, a_, b_, op):
                return v.tensor_tensor(o, a_, b_, op)

            def rows_of(n_):
                return NS if LATE[n_] == TE else P

            def shared_product(n_):
                r_ = rows_of(n_)
                dve.wait_ge(s("a_shsil"), n_ + 1)
                if n_ >= 2:
                    dve.wait_ge(s("pe_shat"), n_ - 1)
                tt(actg[n_ % 2][0:r_].rearrange("t (k p) -> t p k", k=2), sil[n_ % 2][0:r_].rearrange("t (p k) -> t p k", k=2),
                   bank[(6, 2)[n_ % 2]][0:r_, FE:].rearrange("t (p k) -> t p k", k=2), ALU.mult).then_inc(s("d_shact"), 1)

            def shared_act(n_):
                r_ = rows_of(n_)
                dve.wait_ge(s("pe_shat"), n_ + 1)
                v.tensor_copy(actT[n_ % 2][:, :, 0:r_], bank[3][:, 0:256].rearrange("p (k t) -> p k t", k=2)[:, :, 0:r_]
                              ).then_inc(s("d_shat"), 1)

            def shared_add(n_):
                r_, i = rows_of(n_), LATE[n_]
                dve.wait_ge(s("pe_shared"), n_ + 1)
                for hf in range(2):
                    last = tt(acc[0:r_, i, 512 * hf:512 * hf + 512], acc[0:r_, i, 512 * hf:512 * hf + 512],
                              bank[4 + hf][0:r_, :], ALU.add)
                last.then_inc(s("d_sh"), 1)

            dve.wait_ge(s("ld_bt"), 32)
            seq(v.memset(small[0], 0.0))
            for b in range(2):
                seq(v.memset(xg[b], 0.0))
            v.memset(ys[0], 0.0).then_inc(s("xg_zero"), 1)
            dve.wait_ge(s("xg_zero"), 1)
            v.memset(done_mark, 0.0).then_inc(s("lg_zero"), 1)
            dve.wait_ge(s("lg_zero"), 1)
            seq(v.memset(info_v.rearrange("p t e c -> p (t e c)"), 0.0))
            for i in range(NT):
                v.memset(info_v[:, i, :, 0], float(i))
            v.tensor_copy(info_v[:, :, :, 1], bc(rconst[:, 6:7].unsqueeze(2), [P, NT, NE]))
            seq(v.memset(info_v[:, :, :, 2], 1.0))
            shared_product(0)
            dve.wait_ge(s("a_lg"), 2)
            sc, sel = small[2], small[3]
            t4, t5, t6, t7 = small[4], small[5], small[6], small[7]
            seq(v.tensor_scalar(sc, small[0], 0.5, 0.5, ALU.mult, ALU.add))
            seq(tt(sel, sc, bc(bias_b.unsqueeze(1), [P, NT, NE]), ALU.add))
            g8 = lambda w: w.rearrange("p t (g m) -> p (t g) m", m=8)
            for k in (1, 2, 3, 4):
                o = t4 if k == 1 else t5
                tt(g8(o)[:, :, 0:8 - k], g8(sel)[:, :, 0:8 - k], g8(sel)[:, :, k:8], ALU.add)
                seq(tt(g8(o)[:, :, 8 - k:8], g8(sel)[:, :, 8 - k:8], g8(sel)[:, :, 0:k], ALU.add))
                if k > 1:
                    seq(tt(t4, t4, t5, ALU.max))
            gs = t5.rearrange("p t e -> p (t e)")[:, 0:NT * 8].rearrange("p (t g) -> p t g", g=8)
            seq(v.tensor_reduce(gs, g8(t4).rearrange("p (t g) m -> p t g m", g=8), AX.X, ALU.max))
            shared_act(0)
            shared_product(1)
            a4 = lambda w: w.rearrange("p t (i j) -> p t i j", j=8)
            for i in range(NT):
                gi = bc(gs[:, i, :].unsqueeze(2), [P, 8, 8])
                gj = bc(gs[:, i, :].unsqueeze(1), [P, 8, 8])
                tt(a4(t6)[:, i], gj, gi, ALU.is_gt)
                last = tt(a4(t7)[:, i], gj, gi, ALU.is_equal)
            seq(last)
            seq(tt(t7, t7, bc(tri8.unsqueeze(1), [P, NT, 64]), ALU.mult))
            seq(tt(t6, t6, t7, ALU.add))
            rk = t4.rearrange("p t e -> p (t e)")[:, 0:NT * 8]
            seq(v.tensor_reduce(rk, t6.rearrange("p t (i j) -> p (t i) j", j=8), AX.X, ALU.add))
            seq(v.tensor_scalar(rk, rk, float(TOPG) - 0.5, None, ALU.is_lt))
            gm = bc(rk.unsqueeze(2), [P, NT * 8, 8])
            seq(v.tensor_scalar(t5.rearrange("p t e -> p (t e)")[:, 0:NT * 8], rk, -1.0, 1e30, ALU.add, ALU.mult))
            lo = bc(t5.rearrange("p t e -> p (t e)")[:, 0:NT * 8].unsqueeze(2), [P, NT * 8, 8])
            seq(tt(g8(t6), g8(sel), gm, ALU.mult))
            seq(tt(g8(t6), g8(t6), lo, ALU.add))
            best = [small[9][:, i, 0:8] for i in range(NT)]
            for i in range(NT):
                last = v.max(best[i], t6[:, i, :])
            seq(last)
            for i in range(NT):
                last = v.match_replace(t7[:, i, :], best[i], t6[:, i, :], -3e38)
            seq(last)
            seq(tt(t4, t6, t7, ALU.not_equal))
            seq(tt(t4, t4, bc(rconst[:, 1:6].unsqueeze(2), [P, NT, NE]), ALU.mult))
            shared_add(0)
            v.tensor_copy(small[8].rearrange("p t e -> p (t e)").bitcast(BF16)[:, 0:NT * NE], t4.rearrange("p t e -> p (t e)")
                          ).then_inc(s("mask_ready"), 1)
            seq(tt(t5, sc, t4, ALU.mult))
            sm = stat[:, 6, 0:NT]
            seq(v.tensor_reduce(sm, t5, AX.X, ALU.add))
            seq(v.tensor_scalar(sm, sm, 1e-37, None, ALU.max))
            seq(v.reciprocal(sm, sm))
            seq(v.scalar_tensor_tensor(t5, t5, SCALE_ROUTED, bc(sm.unsqueeze(2), [P, NT, NE]), ALU.mult, ALU.mult))
            shared_act(1)
            seq(v.tensor_copy(info_v[:, :, :, 3], t5))
            seq(tt(t6, t5, info_v[:, :, :, 3], ALU.subtract))
            seq(v.tensor_copy(info_v[:, :, :, 4], t6))
            seq(tt(t6, t6, info_v[:, :, :, 4], ALU.subtract))
            seq(v.tensor_copy(info_v[:, :, :, 5], t6))
            dve.wait_ge(s("pe_rank"), 1)
            ps = bank[1][:, 0:NT * NE].rearrange("p (t e) -> p t e", e=NE)
            seq(v.tensor_scalar(t6, ps, 1.0, None, ALU.add))
            seq(tt(t6, t6, t4, ALU.mult))
            seq(v.tensor_scalar(small[1], t6, -1.0, None, ALU.add))
            seq(v.tensor_copy(small[11][:, 0, :], bank[1][:, 384:448]))
            dve_info(dve)
            shared_add(1)
            for n_ in range(2, NT):
                shared_product(n_)
                shared_act(n_)
                shared_add(n_)
            dve_first(dve, seq)
            overflow(dve, dve_more)
            dve.wait_ge(s("ld_gain"), 48)
            for n_, i in enumerate(LATE):
                r_ = NS if i == TE else P
                dve.wait_ge(s("a_rt2"), NT + n_ + 1)
                seq(v.reciprocal(stat[0:r_, 10, i:i + 1], stat[0:r_, 9, i:i + 1]))
                v.scalar_tensor_tensor(acc[0:r_, i, :], acc[0:r_, i, :], stat[0:r_, 10, i:i + 1], gain_f[0:r_, :],
                                       ALU.mult, ALU.mult).then_inc(s("d_out"), 1)

        def mmul(o, l, r, start, stop):
            return nc.tensor.matmul(o, l, r, start=start, stop=stop, skip_group_check=True)

        def w_gu(slot):
            return wexp[slot][:, 0:4096].rearrange("p (a k f) -> p k a f", a=2, k=KD)

        def pe_rows(pe, q, j):
            first = isinstance(q, int) and q == 0
            n = 4 * q + j
            pe.wait_ge(s(f"gathered{j % 2}"), 16 * (2 * q + j // 2 + 1))
            if not first or j >= 1:
                pe.wait_ge(s("a_xgt"), n)
                pe.wait_ge(s("d_xgt"), n)
            for k in range(KD):
                t = nc.tensor.transpose(bank[k // 4][:, P * (k % 4):P * (k % 4) + P], xg[j % 2][:, P * k:P * k + P], ident[:])
            t.then_inc(s("pe_xgt"), 1)

        def pe_up(pe, q, j):
            first = isinstance(q, int) and q == 0
            n = 4 * q + j
            pe.wait_ge(s(f"w_slot{j}"), 48 * (q + 1))
            pe.wait_ge(s("a_xgt"), n + 1)
            pe.wait_ge(s("d_xgt"), n + 1)
            if not first or j >= 2:
                pe.wait_ge(s("act_done"), n - 1)
            for k in range(KD):
                t = mmul(bank[(2, 6)[j % 2]][:, :].rearrange("p (a f) -> p a f", a=2), xgT[j % 2][:, k, :],
                         w_gu(j)[:, k], k == 0, k == KD - 1)
                if k == KD // 2 - 1:
                    t.then_inc(s("pe_half"), 1)
            t.then_inc(s("pe_gu"), 1)

        def pe_act(pe, q, j):
            first = isinstance(q, int) and q == 0
            n = 4 * q + j
            pe.wait_ge(s("act_done"), n + 1)
            if not first or j >= 1:
                pe.wait_ge(s("d_at"), n)
            for k in range(2):
                t = nc.tensor.transpose(bank[3][:, P * k:P * k + P], actg[j % 2][:, P * k:P * k + P], ident[:])
            t.then_inc(s("pe_at"), 1)

        def pe_down(pe, q, j):
            first = isinstance(q, int) and q == 0
            n = 4 * q + j
            pe.wait_ge(s("d_at"), n + 1)
            if not first or j >= 1:
                pe.wait_ge(s("a_ys"), n)
                pe.wait_ge(s("d_ys"), n)
            wd = weights(j, 2).rearrange("p (k d) -> p k d", k=2)
            for hf in range(2):
                for k in range(2):
                    t = mmul(bank[4 + hf][:, :], actT[j % 2][:, k, :], wd[:, k, 512 * hf:512 * hf + 512], k == 0, k == 1)
            t.then_inc(s("pe_down"), 1)

        def pe_step(pe, q, j, last=False, ahead=False, more=None):
            pe_up(pe, q, j)
            if ahead:
                pe_ahead(pe, q, j)
            if more is not None:
                if j == 0:
                    pe.wait_ge(s("jobs_ready"), 1)
                pe_ahead_more(pe, more, j)
            if not last:
                pe_rows(pe, q + (j + 1) // 4, (j + 1) % 4)
            if not (isinstance(q, int) and q == 0 and j == 0):
                pe_down(pe, q if j else q - 1, (j - 1) % 4)
            pe_act(pe, q, j)

        def pe_info(pe):
            for e in range(2 * 4):
                info_block(pe, e % 2, e, e, e)

        def pe_ahead(pe, q, j):
            if j == 0:
                pe.wait_ge(s("info_ready"), q + 1)
            for j2 in {0: (), 1: (0,), 2: (1,), 3: (2, 3)}[j]:
                info_block(pe, j2 % 2, j2, 4 * (q + 2) + j2, 4 * (q + 2) + j2)

        def pe_ahead_more(pe, k, j):
            if j == 0:
                pe.wait_ge(s("info_ready"), NE // 4 - 1 + k)
            for j2 in {0: (), 1: (0,), 2: (1,), 3: (2, 3)}[j]:
                if isinstance(k, int):
                    e = pe.value_load(job_ei[0:1, 4 * k + j2:4 * k + j2 + 1], min_val=0, max_val=NE - 1)
                else:
                    e = pe.value_load(job_ei[0:1, bass.ds(4 * k + j2, 1)], min_val=0, max_val=NE - 1)
                info_block(pe, j2 % 2, j2, e, NE + 4 * k + j2)

        def info_block(pe, half, col, e, n):
            pe.wait_ge(s("hot_ready"), n + 1)
            for i in range(NT):
                t = mmul(bank[7][:, bass.ds(8 * col, 8)], hot[half][:, i, :], info_v[:, i, bass.ds(e, 1), :],
                         i == 0, i == NT - 1)
            t.then_inc(s("pe_info"), 1)

        def pe_first(pe):
            pe_rows(pe, 0, 0)
            for j in range(4):
                pe_step(pe, 0, j, ahead=True)
            with pe.Fori(1, NE // 4 - 2) as q:
                for j in range(4):
                    pe_step(pe, q, j, ahead=True)
            for q in (NE // 4 - 2, NE // 4 - 1):
                for j in range(4):
                    pe_step(pe, q, j, last=q == NE // 4 - 1 and j == 3, more=0 if q == NE // 4 - 2 else None)
            pe_down(pe, NE // 4 - 1, 3)

        def pe_more(pe, k):
            q = NE // 4 + k
            pe_rows(pe, q, 0)
            for j in range(4):
                pe_up(pe, q, j)
                pe_ahead_more(pe, k + 1, j)
                if j < 3:
                    pe_rows(pe, q, j + 1)
                if j > 0:
                    pe_down(pe, q, j - 1)
                pe_act(pe, q, j)
            pe_down(pe, q, 3)

        def shared_pe(pe):
            wd = weights(2, 2).rearrange("p (k d) -> p k d", k=2)

            def sh_up(n_):
                i = LATE[n_]
                r_ = NS if i == TE else P
                if n_ >= 2:
                    pe.wait_ge(s("d_shact"), n_ - 1)
                for k in range(KD):
                    t = mmul(bank[(6, 2)[n_ % 2]][0:r_, :].rearrange("p (a f) -> p a f", a=2), h2T[:, k, P * i:P * i + r_],
                             w_gu(2)[:, k], k == 0, k == KD - 1)
                t.then_inc(s("pe_shgu"), 1)

            def sh_down(n_):
                r_ = NS if LATE[n_] == TE else P
                pe.wait_ge(s("d_shact"), n_ + 1)
                if n_ >= 1:
                    pe.wait_ge(s("d_shat"), n_)
                for k in range(2):
                    t = nc.tensor.transpose(bank[3][:, P * k:P * k + r_], actg[n_ % 2][0:r_, P * k:P * k + P], ident[0:r_, 0:r_])
                t.then_inc(s("pe_shat"), 1)
                pe.wait_ge(s("d_shat"), n_ + 1)
                if n_ >= 1:
                    pe.wait_ge(s("d_sh"), n_)
                for hf in range(2):
                    for k in range(2):
                        t = mmul(bank[4 + hf][0:r_, :], actT[n_ % 2][:, k, 0:r_], wd[:, k, 512 * hf:512 * hf + 512], k == 0, k == 1)
                t.then_inc(s("pe_shared"), 1)

            return sh_up, sh_down

        def moe_pe(pe, sh_up, sh_down):
            pe.wait_ge(s("a_h2t"), 10)
            pe.wait_ge(s("ld_rt"), 16)
            for n_, i in enumerate(LATE):
                r_ = NS if i == TE else P
                for k in range(KD):
                    t = mmul(bank[0][0:r_, NE * i:NE * (i + 1)], h2T[:, k, P * i:P * i + r_], w_rt[:, k, :], k == 0, k == KD - 1)
                t.then_inc(s("pe_rt"), 1)
            sh_up(1)
            sh_down(0)
            sh_up(2)
            sh_down(1)
            pe.wait_ge(s("mask_ready"), 1)
            mb = small[8].rearrange("p t e -> p (t e)").bitcast(BF16)[:, 0:NT * NE].rearrange("p (t e) -> p t e", e=NE)
            for i in range(NT):
                for i2 in range(i + 1):
                    t = mmul(bank[1][:, NE * i:NE * (i + 1)], identb_tri[:, 0 if i2 == i else 1, :], mb[:, i2, :], i2 == 0, i2 == i)
            for i in range(NT):
                t = mmul(bank[1][:, 384:448], identb_tri[:, 1, :], mb[:, i, :], i == 0, i == NT - 1)
            t.then_inc(s("pe_rank"), 1)
            pe_info(pe)
            for n_ in range(2, NT):
                if n_ < NT - 1:
                    sh_up(n_ + 1)
                sh_down(n_)
            pe.wait_ge(s("d_sh"), NT)
            pe_first(pe)
            overflow(pe, pe_more)

        def u_shuffle(copy, odd, done):
            uf = u_feat.rearrange("p f (c l) -> p f c l", l=L)
            for a_ in range(4):
                for t in range(4):
                    if (t % 2) != odd:
                        continue
                    dst = u_chunk[32 * t:32 * t + 32, :, 0:NC_ALL].rearrange("p (f a) c -> p f a c", a=4)[:, :, a_, :]
                    src = uf[32 * a_:32 * a_ + 32, :, 0:NC_ALL, t]
                    i = copy(dst, src)
                if odd:
                    dst = u_chunk[96:128, :, NC_ALL:].rearrange("p (f a) c -> p f a c", a=4)[:, :, a_, :]
                    i = copy(dst, u_feat[32 * a_:32 * a_ + 32, :, NMETA + SEQ:])
            i.then_inc(done, 1)

        def y_shuffle(copy, half, odd, done):
            ysb = st_re.rearrange("p (f a c) -> p f a c", f=2, a=4)
            yf = y_feat[:, 2 * half:2 * half + 2, 0:SEQ].rearrange("p f (c l) -> p f c l", l=L)
            for a_ in range(4):
                for t in range(4):
                    if (t % 2) != odd:
                        continue
                    i = copy(yf[32 * a_:32 * a_ + 32, :, :, t], ysb[32 * t:32 * t + 32, :, a_, NC_META:NC_ALL])
                if odd:
                    i = copy(y_feat[32 * a_:32 * a_ + 32, 2 * half:2 * half + 2, SEQ:],
                             ysb[96:128, :, a_, NC_ALL:])
            i.then_inc(done, 1)

        @block.sync
        def _(sp):
            def load(dst, src, name):
                sp.dma_start(dst, src).then_inc(s(name), 16)

            load(lam[:], ins["lam"], "ld_lam")
            load(x_tiles[:, 0, :], ins["x_prompt"][0, 0:P, :], "ld_tok0")
            sp.wait_ge(s("x4_zero"), 1)
            load(x_tiles[0:NS, TE, :], ins["x_sample"][:, 0, :], "ld_tok4")
            load(x_tiles[XM:XR, TE, :], ins["meta_tokens"], "ld_tok4")
            load(gain1, ins["norm1"].rearrange("a d -> (a d)").partition_broadcast(P), "ld_gain")
            load(ident[:], ins["c_ident"], "ld_id")
            for i in range(1, 4):
                load(x_tiles[:, i, :], ins["x_prompt"][0, i * P:(i + 1) * P, :], f"ld_tok{i}")
            w_in = ins["w_in"][0].rearrange("(k p) n -> p k n", p=P)

            def wblock(b, buf):
                dst = wbuf[:, 4096 * buf:4096 * (buf + 1)].rearrange("p (k n) -> p k n", k=KD)
                load(dst, w_in[:, :, 512 * b:512 * (b + 1)], f"ld_wbuf{buf}")

            wblock(0, 0)
            load(pb[:], ins["bc"], "ld_bc")
            load(mask_m[:], ins["c_mask_m"], "ld_mm")
            load(dskip[:], ins["dskip"], "ld_mm")
            wblock(3, 1)
            load(xs0[:], ins["xs0"], "ld_xs0")
            load(cosin[:], ins["c_cosin"], "ld_cos")
            load(mask_dec, ins["c_mask_dec"], "ld_cos")
            load(dec_cols[:], ins["c_dec"], "ld_cos")
            load(gam_pair[:], ins["c_gam"], "ld_cos")
            load(identb_tri[:].bitcast(U16), ins["c_tri"], "ld_tri")
            load(rconst[:], ins["c_route"], "ld_tri")
            load(iota_b[:].bitcast(U16), ins["c_iota"], "ld_tri")
            load(norms[:], ins["norms"], "ld_tri")
            sp.wait_ge(s("pe_u"), 4)
            wblock(2, 0)
            sp.wait_ge(s("pe_v"), NT)
            wblock(4, 1)
            for c, nm in ((2, "v"), (1, "k")):
                sp.wait_ge(s("a_v2" if nm == "v" else "d_k"), 1)
                src = v_tok[0:NS, TE, :] if nm == "v" else rotd[0][0:NS, :]
                sp.dma_start(qkv_dram[c], src).then_inc(s("st_kv4"), 16)
            sp.wait_ge(s("pe_k"), NT)
            wblock(1, 0)
            w_out = ins["w_out"][0].rearrange("(k p) n -> p k n", p=P)
            sp.wait_ge(s("pe_g"), NT)
            load(wbuf[:, 4096:].rearrange("p (k n) -> p k n", k=4), w_out[:, 0:4, :], "ld_wbuf1")
            sp.wait_ge(s("s5_state_ready"), 1)
            sp.dma_start(outs["s5_states"], fin_s5[:]).then_inc(s("st_out"), 16)
            sp.wait_ge(s("ret_state_ready"), 1)
            for g in range(2):
                sp.dma_start(outs["ret_prompt"][g], state_new[HD * g:HD * (g + 1), 0, :, :]).then_inc(s("st_out"), 16)
            sp.wait_ge(s("a_y"), 2)
            sp.wait_ge(s("a_yf"), 2)
            sp.wait_ge(s("d_yf"), 2)
            load(w_glu, ins["s5_w_glu"][0].rearrange("(k p) n -> p k n", p=P), "ld_glu")
            st_in = ins["state_ret"].rearrange("a b h d v -> (a b h) (d v)")
            for c in range(4):
                load(sm_st[c], st_in[:, D * c:D * (c + 1)], "ld_smst")
            sp.wait_ge(s("d_q"), 1)
            sp.dma_start(qkv_dram[0], rotd[0][0:NS, :]).then_inc(s("st_q4"), 16)
            sp.wait_ge(s("st_kv4"), 32)
            sp.wait_ge(s("st_q4"), 16)
            load(sm_qkv, qkv_dram.rearrange("c b (h d) -> (b h) c d", h=H), "ld_smq")
            sp.wait_ge(s("pe_q"), NT)
            load(wbuf[:, 0:4096].rearrange("p (k n) -> p k n", k=4), w_out[:, 4:8, :], "ld_wbuf0")
            for c in range(4):
                sp.wait_ge(s("sm_new"), c + 1)
                sp.dma_start(outs["ret_sample"][:, D * c:D * (c + 1)], sm_st[c]).then_inc(s("st_out"), 16)
            sp.wait_ge(s("pe_o"), 4)
            sp.wait_ge(s("d_yr"), 4)
            for i in (0, 3):
                load(acc[:, i, :], ins["x_prompt"][0, i * P:(i + 1) * P, :], f"ld_tok{i}")
            load(acc[0:NS, TE, :], ins["x_sample"][:, 0, :], "ld_tok4")
            load(gain2, ins["norm2"].rearrange("a d -> (a d)").partition_broadcast(P), "ld_gain")
            load(w_rt, ins["w_router"][0].rearrange("(p k) n -> p k n", k=KD), "ld_rt")
            sp.wait_ge(s("sm_on"), 1)
            sp.dma_start(o_dram, sm_x[:, 0, :]).then_inc(s("st_o"), 16)
            sp.wait_ge(s("st_o"), 16)
            load(o_ex, o_dram.rearrange("(b h) d -> b (h d)", h=H), "ld_oex")
            sp.wait_ge(s("a_yr"), NT)
            for i in (1, 2):
                load(acc[:, i, :], ins["x_prompt"][0, i * P:(i + 1) * P, :], f"ld_tok{i}")
            sp.wait_ge(s("pe_ss"), 1)
            for kind, nm in enumerate(("w_gate_sh", "w_up_sh")):
                sp.dma_start(weights(2, kind), ins[nm][0].rearrange("(p k) f -> p (k f)", p=P)).then_inc(s("w_shared"), 16)
            sp.dma_start(weights(2, 2), ins["w_down_sh"][0].rearrange("(p k) d -> p (k d)", p=P)).then_inc(s("w_shared"), 16)
            for n_, i in enumerate(LATE):
                r_ = NS if i == TE else P
                sp.wait_ge(s("d_h2"), n_ + 1)
                if n_ == NT - 1:
                    load(bias_b, ins["router_bias"].rearrange("a d -> (a d)").partition_broadcast(P), "ld_bt")
                    load(tri8, ins["c_tri8"], "ld_bt")
                sp.dma_start(h2_dram[P * i:P * i + r_, :], h2p[0:r_, n_ % 2, :]).then_inc(s(f"st_h2_{n_ % 2}"), 16)
            sp.wait_ge(s("xg_zero"), 1)
            sp.dma_start(sum_dram[TT:TT + SLOTS, :], ys[0]).then_inc(s("st_dump"), 16)
            sp.wait_ge(s("st_out"), 16 * 7)
            moe_sync(sp)

        @block.gpsimd
        def _(pool):
            n = [0]

            def seq(i):
                n[0] += 1
                i.then_inc(s("pool_seq"), 1)
                pool.wait_ge(s("pool_seq"), n[0])

            for half in range(2):
                gs = slice(HG * half, HG * (half + 1))
                er = phase_re.rearrange("p (g c) -> p g c", g=HG)
                ei = phase_im.rearrange("p (g c) -> p g c", g=HG)
                if half == 0:
                    pool.wait_ge(s("prm_ready"), 1)
                else:
                    pool.wait_ge(s("z_ready"), 1)
                    pool.wait_ge(s("pe_y"), 3)
                sc = prm[:, 29:33, gs]
                seq(pool.tensor_copy(sc[:, 0, :], prm[:, 20, gs]))
                seq(pool.tensor_copy(sc[:, 1, :], prm[:, 21, gs]))
                seq(pool.memset(er[:, :, 0:1], 1.0))
                seq(pool.memset(ei[:, :, 0:1], 0.0))
                w = 1
                while w < NCS:
                    m = min(w, NCS - w)
                    cr = bc(sc[:, 0, :].unsqueeze(2), [P, HG, m])
                    ci = bc(sc[:, 1, :].unsqueeze(2), [P, HG, m])
                    t1 = rot_im[:, 0:HG * m].rearrange("p (g c) -> p g c", g=HG)
                    t2 = rot_im[:, 512:512 + HG * m].rearrange("p (g c) -> p g c", g=HG)
                    pool.tensor_tensor(t1, er[:, :, 0:m], cr, ALU.mult)
                    seq(pool.tensor_tensor(t2, ei[:, :, 0:m], ci, ALU.mult))
                    seq(pool.tensor_tensor(er[:, :, w:w + m], t1, t2, ALU.subtract))
                    pool.tensor_tensor(t1, er[:, :, 0:m], ci, ALU.mult)
                    seq(pool.tensor_tensor(t2, ei[:, :, 0:m], cr, ALU.mult))
                    seq(pool.tensor_tensor(ei[:, :, w:w + m], t1, t2, ALU.add))
                    w *= 2
                    if w < NCS:
                        pool.tensor_tensor(sc[:, 2, :], sc[:, 0, :], sc[:, 1, :], ALU.mult)
                        seq(pool.tensor_tensor(sc[:, 3, :], sc[:, 1, :], sc[:, 1, :], ALU.mult))
                        pool.tensor_scalar(sc[:, 0, :], sc[:, 3, :], -2.0, 1.0, ALU.mult, ALU.add)
                        seq(pool.tensor_scalar(sc[:, 1, :], sc[:, 2, :], 2.0, None, ALU.mult))
                pool.memset(rot_im[:, 0:1], 0.0).then_inc(s("phase_ready"), 1)

            pool.wait_ge(s("ld_smq"), 16)
            seq(pool.tensor_scalar(sm_x[:, 0, :], sm_qkv[:, 1, :], float(HD ** -0.5), None, ALU.mult))
            part = lambda w: w.rearrange("p (d v) -> p d v", v=HD)
            for c in range(4):
                pool.tensor_tensor(part(sm_kv[c]), bc(sm_x[:, 0, 16 * c:16 * c + 16].unsqueeze(2), [SR, 16, HD]),
                                   bc(sm_qkv[:, 2, :].unsqueeze(1), [SR, 16, HD]), ALU.mult).then_inc(s("sm_kv"), 1)
            for c in range(4):
                pool.wait_ge(s("sm_new"), c + 1)
                pool.tensor_tensor(part(sm_kv[c]), part(sm_st[c]),
                                   bc(sm_qkv[:, 0, 16 * c:16 * c + 16].unsqueeze(2), [SR, 16, HD]),
                                   ALU.mult).then_inc(s("sm_qn"), 1)
            moe_pool(pool)

        @block.scalar
        def _(act):
            def a(out, in_, f, **kw):
                return nc.scalar.activation(out, in_, f, **kw)

            act.wait_ge(s("ld_lam"), 16)
            a(prm[:, 0, :], lam[:, 2, :], ACT.Exp).then_inc(s("a_dt"), 1)
            act.wait_ge(s("d_z"), 1)
            for j, e in enumerate((1, 2, 3, 4, -1, -2, -3)):
                i = a(prm[:, 3 + j, :], prm[:, 1, :], ACT.Exp, scale=float(e))
            i.then_inc(s("a_pow"), 1)
            for n_, i in enumerate(EARLY):
                act.wait_ge(s("d_stat0"), 1)
                if n_:
                    act.wait_ge(s("a_ss"), n_)
                if i == 4:
                    act.wait_ge(s("ld_tok4"), 32)
                else:
                    act.wait_ge(s(f"ld_tok{i}"), 16)
                r = XR if i == TE else P
                a(at(45440, D)[0:r, :], x_tiles[0:r, i, :], ACT.Square, accum_out=stat[0:r, 0, i:i + 1]).then_inc(s("a_ss"), 1)
                act.wait_ge(s("a_ss"), n_ + 1)
                a(stat[0:r, 1, i:i + 1], stat[0:r, 0, i:i + 1], ACT.Sqrt, scale=1.0 / D,
                  bias=stat[0:r, 7, 0:1]).then_inc(s("a_rt"), 1)
            act.wait_ge(s("d_th"), 1)
            a(prm[:, 12, :], prm[:, 11, :], ACT.Sin)
            a(prm[:, 13, :], prm[:, 11, :], ACT.Sin, scale=0.5).then_inc(s("a_sin"), 1)
            for n_, i in enumerate(EARLY):
                r = XR if i == TE else P
                for hf in range(2):
                    act.wait_ge(s("pe_xt"), 2 * n_ + hf + 1)
                    b = bank[2 * (n_ % 2) + hf]
                    nc.scalar.copy(hT[:, 4 * hf:4 * hf + 4, P * i:P * i + r],
                                   b[:, :].rearrange("p (k t) -> p k t", k=4)[:, :, 0:r]).then_inc(s("a_ht"), 1)
            for ft in range(4):
                act.wait_ge(s("pe_u"), ft + 1)
                nc.scalar.copy(u_feat[:, ft, NMETA:NMETA + SEQ], bank[4 + 2 * (ft % 2)][:, :])
                nc.scalar.copy(u_feat[:, ft, 0:NMETA], bank[5 + 2 * (ft % 2)][:, XM:XR])
                nc.scalar.copy(u_feat[:, ft, NMETA + SEQ:], bank[5 + 2 * (ft % 2)][:, 0:NS]).then_inc(s("a_u"), 1)
            act.wait_ge(s("a_u"), 4)
            act.wait_ge(s("d_uzero"), 1)
            u_shuffle(nc.scalar.copy, 1, s("a_uc"))

            def s5_evac(half):
                for n_ in range(4):
                    act.wait_ge(s("pe_vt"), 4 * half + n_ + 1)
                    nc.scalar.copy((v_re, v_im)[n_ // 2][:, 512 * (n_ % 2):512 * (n_ % 2 + 1)],
                                   bank[2 + n_][:, :]).then_inc(s("a_v"), 1)
                for n_ in range(6):
                    act.wait_ge(s("pe_s"), 6 * half + n_ + 1)
                    g0, g1 = 3 * (n_ % 3), min(3 * (n_ % 3) + 3, HG)
                    nc.scalar.copy((st_re, st_im)[n_ // 3][:, NCS * g0:NCS * g1],
                                   bank[2 + n_][:, 0:NCS * (g1 - g0)]).then_inc(s("a_s"), 1)

            def y_evac(half):
                for n_ in range(3):
                    act.wait_ge(s("pe_y"), 3 * half + n_ + 1)
                    g0, g1 = 3 * n_, min(3 * n_ + 3, HG)
                    i = nc.scalar.copy(st_re[:, NCS * g0:NCS * g1], bank[2 + n_][:, 0:NCS * (g1 - g0)])
                i.then_inc(s("a_y"), 1)
                act.wait_ge(s("a_y"), half + 1)
                y_shuffle(nc.scalar.copy, half, 1, s("a_yf"))

            def rows(i_):
                return XR if i_ == TE else P

            s5_evac(0)
            for n_, i in enumerate(TILES):
                act.wait_ge(s("pe_v"), n_ + 1)
                if n_ == 0:
                    act.wait_ge(s("pe_xt"), 10)
                nc.scalar.copy(v_tok[0:rows(i), i, :], bank[n_ % 2][0:rows(i), :]).then_inc(s("a_v2"), 1)
            for c in range(4):
                act.wait_ge(s("pe_kt"), c + 1)
                nc.scalar.copy(kT[:, :, P * c:P * (c + 1)],
                               bank[6][:, :].rearrange("p (a t) -> p a t", a=4)).then_inc(s("a_kt"), 1)
            y_evac(0)
            for n_, i in enumerate(TILES):
                if n_ == 3:
                    s5_evac(1)
                act.wait_ge(s("pe_g"), n_ + 1)
                a(gate_tok[0:rows(i), i, :], bank[n_ % 2][0:rows(i), :], ACT.Silu).then_inc(s("a_g"), 1)
            y_evac(1)
            act.wait_ge(s("a_yf"), 2)
            act.wait_ge(s("d_yf"), 2)
            a(y_feat, y_feat, ACT.Gelu_apprx_tanh).then_inc(s("a_gelu"), 1)

            def yr_evac(k_, c0, c1):
                act.wait_ge(s("pe_yrt"), k_ + 1)
                for a_ in range(4):
                    i_ = a(yr_feat[:, a_, c0:c1], bank[7][:, P * a_:P * a_ + c1 - c0], ACT.Copy,
                           scale=norms[:, 1, a_:a_ + 1])
                i_.then_inc(s("a_yr"), 1)

            act.wait_ge(s("ld_tri"), 16 * 4)

            def qt_evac(c):
                act.wait_ge(s("pe_qt"), c + 1)
                nc.scalar.copy(qT[:, c % 2], bank[6][:, :].rearrange("p (a t) -> p a t", a=4)).then_inc(s("a_qt"), 1)

            for c in range(4):
                if c < 3:
                    qt_evac(c)
                if c >= 1:
                    yr_evac(c - 1, P * (c - 1), P * c)
                if c == 2:
                    qt_evac(3)
                act.wait_ge(s("d_var"), c + 1)
                a(hst[:, 2, :], hst[:, 1, :], ACT.Sqrt, scale=1.0 / HD, bias=stat[:, 7, 0:1]).then_inc(s("a_sd"), 1)
            for f in range(4):
                act.wait_ge(s("pe_glu"), f + 1)
                a(glu_t[:, f, 0:SEQ], bank[f][:, :], ACT.Tanh, scale=0.5).then_inc(s("a_tanh"), 1)
            a(glu_t[:, :, SEQ:], bank[6][:, 0:4 * NS].rearrange("p (f t) -> p f t", f=4), ACT.Tanh, scale=0.5
              ).then_inc(s("a_tanh"), 1)
            yr_evac(3, P * 3, P * 4)
            for f in range(4):
                act.wait_ge(s("d_glu"), f + 1)
                a(glu_sq[:, f, 0:SEQ], y_feat[:, f, 0:SEQ], ACT.Square).then_inc(s("a_sq"), 1)
            act.wait_ge(s("d_glu"), 5)
            a(glu_sq[:, :, SEQ:], y_feat[:, :, SEQ:], ACT.Square).then_inc(s("a_sq"), 1)
            act.wait_ge(s("sm_var"), 1)
            a(hst[0:SR, 2, 0:1], hst[0:SR, 1, 0:1], ACT.Sqrt, scale=1.0 / HD, bias=stat[0:SR, 7, 0:1]).then_inc(s("a_sd"), 1)
            act.wait_ge(s("pe_ss"), 1)
            act.wait_ge(s("d_statz"), 1)
            a(stat[:, 4, 0:4], bank[4][:, 0:4], ACT.Sqrt, scale=1.0 / DS5, bias=stat[:, 7, 0:1])
            a(stat[0:NS, 4, TE:NT], bank[4][0:NS, TE:NT], ACT.Sqrt, scale=1.0 / DS5,
              bias=stat[0:NS, 7, 0:1]).then_inc(s("a_rs5"), 1)
            yr_evac(4, SEQ, TT)
            for n_, i in enumerate(LATE):
                r = NS if i == TE else P
                act.wait_ge(s("d_x2"), n_ + 1)
                if n_ >= 2:
                    act.wait_ge(s("pe_h2t"), 2 * (n_ - 1))
                    act.wait_ge(s(f"st_h2_{n_ % 2}"), 16 * (n_ // 2))
                a(h2p[0:r, n_ % 2, :], acc[0:r, i, :], ACT.Square, accum_out=stat[0:r, 8, i:i + 1]).then_inc(s("a_ss2"), 1)
                act.wait_ge(s("a_ss2"), n_ + 1)
                a(stat[0:r, 9, i:i + 1], stat[0:r, 8, i:i + 1], ACT.Sqrt, scale=1.0 / D,
                  bias=stat[0:r, 7, 0:1]).then_inc(s("a_rt2"), 1)
                if n_ >= 1:
                    h2t_evac(n_ - 1)
            h2t_evac(NT - 1)
            moe_act(act)

        @block.vector
        def _(dve):
            v = nc.vector
            n = [0]

            def seq(i):
                n[0] += 1
                i.then_inc(s("dve_seq"), 1)
                dve.wait_ge(s("dve_seq"), n[0])

            def tt(o, a_, b_, op):
                return v.tensor_tensor(o, a_, b_, op)

            v.memset(x_tiles[0:XR, TE, :], 0.0).then_inc(s("x4_zero"), 1)
            v.memset(ones_col[:], 1.0)
            v.memset(stat[:], EPS).then_inc(s("d_stat0"), 1)
            R = lambda i: prm[:, i, :]
            dve.wait_ge(s("a_dt"), 1)
            seq(tt(R(1), lam[:, 0, :], R(0), ALU.mult))
            seq(tt(R(2), lam[:, 1, :], R(0), ALU.mult))
            v.memset(u_chunk[:, :, NC_ALL:], 0.0).then_inc(s("d_uzero"), 1)
            v.tensor_copy(R(33), R(1)).then_inc(s("d_z"), 1)
            seq(v.tensor_scalar(R(10), R(2), 1.0 / (2 * np.pi), MAGIC, ALU.mult, ALU.add))
            seq(v.tensor_scalar(R(10), R(10), -MAGIC, None, ALU.add))
            seq(v.scalar_tensor_tensor(R(11), R(10), -C1, R(2), ALU.mult, ALU.add))
            seq(v.scalar_tensor_tensor(R(11), R(10), -C2, R(11), ALU.mult, ALU.add))
            seq(v.scalar_tensor_tensor(R(11), R(10), -C3, R(11), ALU.mult, ALU.add))
            v.tensor_scalar(R(11), R(11), 3.141592, -3.141592, ALU.min, ALU.max).then_inc(s("d_th"), 1)
            dve.wait_ge(s("ld_gain"), 16)
            for n_, i in enumerate(EARLY):
                r = XR if i == TE else P
                dve.wait_ge(s("a_rt"), n_ + 1)
                seq(v.reciprocal(stat[0:r, 2, i:i + 1], stat[0:r, 1, i:i + 1]))
                if n_ >= 2:
                    dve.wait_ge(s("pe_xt"), 2 * (n_ - 1))
                v.scalar_tensor_tensor(xn_bufs[0:r, n_ % 2, :], x_tiles[0:r, i, :], stat[0:r, 2, i:i + 1],
                                       gain1[0:r, :], ALU.mult, ALU.mult).then_inc(s("d_xn"), 1)
            dve.wait_ge(s("a_sin"), 1)
            dve.wait_ge(s("a_pow"), 1)
            seq(tt(R(14), R(13), R(13), ALU.mult))
            seq(v.tensor_scalar(R(14), R(14), -2.0, 1.0, ALU.mult, ALU.add))
            seq(tt(R(15), R(12), R(12), ALU.mult))
            seq(v.tensor_scalar(R(16), R(15), -2.0, 1.0, ALU.mult, ALU.add))
            seq(v.scalar_tensor_tensor(R(17), R(12), 2.0, R(14), ALU.mult, ALU.mult))
            seq(tt(R(15), R(17), R(17), ALU.mult))
            seq(v.tensor_scalar(R(20), R(15), -2.0, 1.0, ALU.mult, ALU.add))
            seq(v.scalar_tensor_tensor(R(21), R(17), 2.0, R(16), ALU.mult, ALU.mult))
            v.memset(marks[:], 0.0).then_inc(s("prm_ready"), 1)
            seq(tt(R(15), R(17), R(12), ALU.mult))
            seq(tt(R(18), R(16), R(14), ALU.mult))
            seq(tt(R(18), R(18), R(15), ALU.subtract))
            seq(tt(R(15), R(16), R(12), ALU.mult))
            seq(tt(R(19), R(17), R(14), ALU.mult))
            seq(tt(R(19), R(19), R(15), ALU.add))
            cs = {1: (14, 12), 2: (16, 17), 3: (18, 19)}
            v.memset(pw[:, 0:4:2, :, 3], 1.0)
            v.memset(pw[:, 1:4:2, :, 3], 0.0)
            for j in (1, 2, 3):
                c_, s_ = cs[j]
                seq(tt(pw[:, 0, :, 3 - j], R(3 + j - 1), R(c_), ALU.mult))
                seq(tt(pw[:, 1, :, 3 - j], R(3 + j - 1), R(s_), ALU.mult))
                seq(tt(pw[:, 2, :, 3 - j], R(7 + j - 1), R(c_), ALU.mult))
                seq(v.scalar_tensor_tensor(pw[:, 3, :, 3 - j], R(7 + j - 1), -1.0, R(s_), ALU.mult, ALU.mult))
            seq(v.tensor_scalar(R(22), pw[:, 0, :, 2], -1.0, None, ALU.add))
            ni = pw[:, 1, :, 2]
            seq(tt(R(23), R(22), lam[:, 0, :], ALU.mult))
            seq(tt(R(24), ni, lam[:, 1, :], ALU.mult))
            seq(tt(R(23), R(23), R(24), ALU.add))
            seq(tt(R(24), ni, lam[:, 0, :], ALU.mult))
            seq(tt(R(25), R(22), lam[:, 1, :], ALU.mult))
            seq(tt(R(24), R(24), R(25), ALU.subtract))
            seq(tt(R(25), lam[:, 0, :], lam[:, 0, :], ALU.mult))
            seq(tt(R(26), lam[:, 1, :], lam[:, 1, :], ALU.mult))
            seq(tt(R(25), R(25), R(26), ALU.add))
            seq(v.reciprocal(R(26), R(25)))
            seq(tt(R(27), R(23), R(26), ALU.mult))
            seq(tt(R(28), R(24), R(26), ALU.mult))
            fr = bc(R(27).unsqueeze(2), [P, GP, 16])
            fi = bc(R(28).unsqueeze(2), [P, GP, 16])
            dve.wait_ge(s("ld_bc"), 16)
            seq(tt(bt[:, 0], pb[:, 0], fr, ALU.mult))
            seq(tt(bt[:, 1], pb[:, 1], fi, ALU.mult))
            seq(tt(bb[:, 0], bt[:, 0], bt[:, 1], ALU.subtract))
            seq(tt(bt[:, 0], pb[:, 1], fr, ALU.mult))
            seq(tt(bt[:, 1], pb[:, 0], fi, ALU.mult))
            seq(tt(bb[:, 1], bt[:, 0], bt[:, 1], ALU.add))
            seq(v.tensor_scalar(ncim[:], pb[:, 3], -1.0, None, ALU.mult))

            def blocks(w):
                return w.rearrange("p (g l b h) -> p g l b h", g=HG, l=L, b=2)

            def tell(i, name, value):
                i.then_inc(s(name), 1)
                dve.wait_ge(s(name), value)

            def tables(half):
                gs = slice(HG * half, HG * (half + 1))
                m1 = u_tmp[:, 0:512].rearrange("p (g l h) -> p g l h", g=HG, l=L)
                m2 = u_tmp[:, 512:1024].rearrange("p (g l h) -> p g l h", g=HG, l=L)
                for w in (vt_re, vt_im, wt_re, wt_im):
                    seq(v.memset(w, 0.0))
                sh = [P, HG, L, 16]
                for w, b0, p0, b1, p1, op in (
                        (vt_re, bb[:, 0], 0, bb[:, 1], 1, ALU.subtract), (vt_im, bb[:, 1], 0, bb[:, 0], 1, ALU.add),
                        (wt_re, pb[:, 2], 2, ncim[:], 3, ALU.add), (wt_im, ncim[:], 2, pb[:, 2], 3, ALU.subtract)):
                    seq(tt(m1, bc(b0[:, gs, :].unsqueeze(2), sh), bc(pw[:, p0, gs, :].unsqueeze(3), sh), ALU.mult))
                    seq(tt(m2, bc(b1[:, gs, :].unsqueeze(2), sh), bc(pw[:, p1, gs, :].unsqueeze(3), sh), ALU.mult))
                    for g2 in range(2):
                        r = slice(NST * g2, NST * (g2 + 1))
                        last = tt(blocks(w)[r, :, :, g2, :], m1[r], m2[r], op)
                        if not (w is wt_im and g2):
                            seq(last)
                tell(last, "d_tab", half + 1)

            def m_evac(half):
                for n_ in range(2):
                    dve.wait_ge(s("pe_m"), 2 * half + n_ + 1)
                    mm = m_mat[:, 512 * n_:512 * (n_ + 1)].rearrange("p (g t) -> p g t", g=4)
                    seq(tt(mm, bank[n_][:, :].rearrange("p (g t) -> p g t", g=4),
                           bc(mask_m[:].unsqueeze(1), [P, 4, P]), ALU.mult))
                for g in range(HG):
                    mm = m_mat[:, 128 * g:128 * (g + 1)]
                    last = v.scalar_tensor_tensor(mm, ident[:], dskip[:, HG * half + g:HG * half + g + 1], mm,
                                                  ALU.mult, ALU.add)
                tell(last, "d_m", half + 1)

            def scan(half):
                gs = slice(HG * half, HG * (half + 1))
                g3 = lambda w: w.rearrange("p (g c) -> p g c", g=HG)
                dve.wait_ge(s("a_s"), 6 * (half + 1))
                seq(v.tensor_copy(fin_s5[:, 0, gs, :], g3(st_re)[:, :, NC_ALL - 1:]))
                seq(v.tensor_copy(fin_s5[:, 1, gs, :], g3(st_im)[:, :, NC_ALL - 1:]))
                dve.wait_ge(s("phase_ready"), half + 1)
                seq(tt(rot_re, st_re, phase_re, ALU.mult))
                seq(tt(rot_im, st_im, phase_im, ALU.mult))
                seq(tt(rot_re, rot_re, rot_im, ALU.add))
                seq(tt(rot_im, st_im, phase_re, ALU.mult))
                seq(tt(st_re, st_re, phase_im, ALU.mult))
                seq(tt(rot_im, rot_im, st_re, ALU.subtract))
                for w, o in ((rot_re, st_re), (rot_im, st_im)):
                    for g in range(HG):
                        v.tensor_tensor_scan(o[:, NCS * g:NCS * g + NC_ALL], w[:, NCS * g:NCS * g + NC_ALL],
                                             bc(prm[:, 6, HG * half + g:HG * half + g + 1], [P, NC_ALL]),
                                             0.0, ALU.add, ALU.mult)
                o = e1 = slice(1, NC_ALL)
                zi = slice(0, NC_ALL - 1)
                seq(v.memset(marks[:, 1:2], 0.0))
                seq(tt(g3(rot_re)[:, :, o], g3(st_re)[:, :, zi], g3(phase_re)[:, :, e1], ALU.mult))
                seq(tt(g3(rot_im)[:, :, o], g3(st_im)[:, :, zi], g3(phase_im)[:, :, e1], ALU.mult))
                seq(tt(g3(rot_re)[:, :, o], g3(rot_re)[:, :, o], g3(rot_im)[:, :, o], ALU.subtract))
                seq(tt(g3(rot_im)[:, :, o], g3(st_re)[:, :, zi], g3(phase_im)[:, :, e1], ALU.mult))
                seq(tt(g3(st_im)[:, :, zi], g3(st_im)[:, :, zi], g3(phase_re)[:, :, e1], ALU.mult))
                seq(tt(g3(rot_im)[:, :, o], g3(rot_im)[:, :, o], g3(st_im)[:, :, zi], ALU.add))
                seq(tt(fin_s5[:, 0, gs, 0:1], fin_s5[:, 0, gs, 0:1], g3(rot_re)[:, :, NC_ALL - 1:NC_ALL], ALU.add))
                seq(tt(fin_s5[:, 1, gs, 0:1], fin_s5[:, 1, gs, 0:1], g3(rot_im)[:, :, NC_ALL - 1:NC_ALL], ALU.add))
                seq(v.memset(g3(rot_re)[:, :, 0:1], 0.0))
                seq(v.memset(g3(rot_im)[:, :, 0:1], 0.0))
                ar = bc(pw[:, 0, gs, 2:3], [P, HG, NS])
                ai = bc(pw[:, 1, gs, 2:3], [P, HG, NS])
                smp = slice(NC_ALL, NCS)
                t1, t2 = g3(st_im)[:, :, 0:NS], g3(st_im)[:, :, NS:2 * NS]
                dve.wait_ge(s("ld_xs0"), 16)
                seq(tt(t1, xs0[:, 0, gs, :], ar, ALU.mult))
                seq(tt(t2, xs0[:, 1, gs, :], ai, ALU.mult))
                seq(tt(g3(rot_re)[:, :, smp], t1, t2, ALU.subtract))
                seq(tt(t1, xs0[:, 1, gs, :], ar, ALU.mult))
                seq(tt(t2, xs0[:, 0, gs, :], ai, ALU.mult))
                seq(tt(g3(rot_im)[:, :, smp], t1, t2, ALU.add))
                seq(tt(fin_s5[:, 0, gs, 1:], fin_s5[:, 0, gs, 1:], g3(rot_re)[:, :, smp], ALU.add))
                tell(tt(fin_s5[:, 1, gs, 1:], fin_s5[:, 1, gs, 1:], g3(rot_im)[:, :, smp], ALU.add), "z_ready", half + 1)

            u_tmp = rot_re

            def rows(i_):
                return XR if i_ == TE else P

            def rotate(dst, src, i_):
                r_ = rows(i_)
                h3 = lambda w: w[0:r_].rearrange("p (a d) -> p a d", d=HD // 2)
                h4 = lambda w: w[0:r_].rearrange("p (h b d) -> p h b d", b=2, d=HD // 2)
                co = bc(cosin[0:r_, 0, i_, :].unsqueeze(1), [r_, 2 * H, HD // 2])
                si = bc(cosin[0:r_, 1, i_, :].unsqueeze(1), [r_, 2 * H, HD // 2])
                seq(tt(h3(rt1), h3(src), co, ALU.mult))
                seq(tt(h3(rt2), h3(src), si, ALU.mult))
                seq(tt(h4(dst)[:, :, 0, :], h4(rt1)[:, :, 0, :], h4(rt2)[:, :, 1, :], ALU.subtract))
                return tt(h4(dst)[:, :, 1, :], h4(rt1)[:, :, 1, :], h4(rt2)[:, :, 0, :], ALU.add)

            def k_tile(n_, i_):
                r_ = rows(i_)
                dve.wait_ge(s("pe_k"), n_ + 1)
                if n_ == 0:
                    dve.wait_ge(s("ld_cos"), 16 * 4)
                if n_ >= 3:
                    dve.wait_ge(s("pe_kt"), n_ - 2)
                if n_ >= 2:
                    dve.wait_ge(s("pe_st"), n_ - 1)
                if n_ == 2:
                    dve.wait_ge(s("st_kv4"), 32)
                rot = rotd[n_ % 2]
                k_ = rotate(rot, bank[n_ % 2], i_)
                k_.then_inc(s("d_k"), 1)
                dve.wait_ge(s("d_k"), n_ + 1)
                hd = lambda w: w[0:r_].rearrange("p (h d) -> p h d", h=H)
                tt(hd(kdec[:, n_ % 2, :]), hd(rot),
                   bc(dec_cols[0:r_, 1 if i_ == TE else 0, :].unsqueeze(2), [r_, H, HD]), ALU.mult).then_inc(s("d_kd"), 1)
                dve.wait_ge(s("d_kd"), n_ + 1)

            def state_step(n_):
                dve.wait_ge(s("pe_st"), n_ + 1)
                for g in range(2):
                    r_ = slice(HD * g, HD * (g + 1))
                    ps = bank[7][r_, :].rearrange("p (a b v) -> p a b v", a=4, b=2)[:, :, g, :]
                    new = state_bd[r_, n_, :, HD * g:HD * (g + 1)] if n_ < 4 else state_new[r_, 0, :, :]
                    if n_ == 0:
                        last = v.tensor_copy(new, ps)
                        if g == 0:
                            seq(last)
                    else:
                        old = state_bd[r_, n_ - 1, :, HD * g:HD * (g + 1)]
                        seq(tt(state_new[r_, 1, :, :], old, bc(gam_pair[r_, :].unsqueeze(2), [HD, 4, HD]), ALU.mult))
                        last = tt(new, state_new[r_, 1, :, :], ps, ALU.add)
                        if g == 0:
                            seq(last)
                last.then_inc(s("d_st"), 1)
                dve.wait_ge(s("d_st"), n_ + 1)

            def head_norm(src, tmp, sq, r_, nh):
                h_ = lambda w: w.rearrange("p (h d) -> p h d", h=nh)
                seq(v.tensor_reduce(hst[0:r_, 0, 0:nh], h_(src), AX.X, ALU.add))
                seq(v.tensor_scalar(hst[0:r_, 0, 0:nh], hst[0:r_, 0, 0:nh], 1.0 / HD, None, ALU.mult))
                seq(tt(h_(tmp), h_(src), bc(hst[0:r_, 0, 0:nh].unsqueeze(2), [r_, nh, HD]), ALU.subtract))
                seq(tt(sq, tmp, tmp, ALU.mult))
                return v.tensor_reduce(hst[0:r_, 1, 0:nh], h_(sq), AX.X, ALU.add)

            def q_tile(n_, i_):
                dve.wait_ge(s("pe_q"), n_ + 1)
                if n_ >= 3:
                    dve.wait_ge(s("pe_qt"), n_ - 2)
                if n_ == 2:
                    dve.wait_ge(s("st_q4"), 16)
                rotate(rotd[n_ % 2], bank[n_ % 2], i_).then_inc(s("d_q"), 1)
                dve.wait_ge(s("d_q"), n_ + 1)

            def attend_probs(c):
                for hs in range(2):
                    dve.wait_ge(s("pe_sc"), 2 * c + hs + 1)
                    if c >= 1:
                        dve.wait_ge(s("pe_o"), c)
                    tt(probs[:, hs, :], bank[2 + hs][:, :], mask_dec[:, 512 * hs:512 * (hs + 1)],
                       ALU.mult).then_inc(s("d_pr"), 1)
                    dve.wait_ge(s("d_pr"), 2 * c + hs + 1)

            def attend_out(c):
                dve.wait_ge(s("pe_o"), c + 1)
                if c >= 1:
                    dve.wait_ge(s("pe_yrt"), c)
                seq(tt(on1.rearrange("p (h d) -> p h d", h=H), bank[4 + c % 2][:, :].rearrange("p (h d) -> p h d", h=H),
                       bc(dec_cols[:, 2, :].unsqueeze(2), [P, H, HD]), ALU.mult))
                head_norm(on1, on2, on3, P, H).then_inc(s("d_var"), 1)
                dve.wait_ge(s("a_sd"), c + 1)
                seq(v.reciprocal(hst[:, 3, :], hst[:, 2, :]))
                seq(tt(on2, on2, gate_tok[:, c, :], ALU.mult))
                tt(on1.rearrange("p (h d) -> p h d", h=H), on2.rearrange("p (h d) -> p h d", h=H),
                   bc(hst[:, 3, :].unsqueeze(2), [P, H, HD]), ALU.mult).then_inc(s("d_yr"), 1)
                dve.wait_ge(s("d_yr"), c + 1)

            tables(0)
            dve.wait_ge(s("a_u"), 4)
            dve.wait_ge(s("d_uzero"), 1)
            u_shuffle(v.tensor_copy, 0, s("d_uc"))
            dve.wait_ge(s("ld_mm"), 32)
            dve.wait_ge(s("ld_id"), 16)
            m_evac(0)
            scan(0)
            seq(v.memset(state_bd[:], 0.0))
            seq(v.memset(state_new[:], 0.0))
            for n_, i in enumerate(TILES):
                k_tile(n_, i)
                if n_ >= 1:
                    state_step(n_ - 1)
            state_step(NT - 1)
            tell(v.memset(marks[:, 2:3], 0.0), "ret_state_ready", 1)
            dve.wait_ge(s("a_y"), 1)
            y_shuffle(v.tensor_copy, 0, 0, s("d_yf"))
            dve.wait_ge(s("a_yf"), 1)
            dve.wait_ge(s("d_yf"), 1)
            tables(1)
            m_evac(1)
            scan(1)
            tell(v.memset(marks[:, 2:3], 0.0), "s5_state_ready", 1)
            q_tile(0, TE)
            q_tile(1, 0)
            dve.wait_ge(s("a_y"), 2)
            y_shuffle(v.tensor_copy, 1, 0, s("d_yf"))
            dve.wait_ge(s("a_g"), NT)
            attend_probs(0)
            for c in range(4):
                if c < 3:
                    q_tile(c + 2, c + 1)
                attend_out(c)
                if c < 3:
                    attend_probs(c + 1)

            dve.wait_ge(s("ld_smst"), 16 * 4)
            for c in range(4):
                dve.wait_ge(s("sm_kv"), c + 1)
                v.scalar_tensor_tensor(sm_st[c], sm_st[c], dec_cols[0:SR, 3, 0:1], sm_kv[c],
                                       ALU.mult, ALU.add).then_inc(s("sm_new"), 1)
            def glu_gate(f, cols, n_):
                seq(v.tensor_scalar(glu_t[:, f, cols], glu_t[:, f, cols], 0.5, 0.5, ALU.mult, ALU.add))
                if n_ == 0:
                    dve.wait_ge(s("pe_glu"), 4)
                tt(y_feat[:, f, cols], y_feat[:, f, cols], glu_t[:, f, cols], ALU.mult).then_inc(s("d_glu"), 1)

            for f in range(4):
                dve.wait_ge(s("a_tanh"), f + 1)
                glu_gate(f, slice(0, SEQ), f)
            dve.wait_ge(s("a_tanh"), 5)
            glu_gate(slice(0, 4), slice(SEQ, TT), 4)
            for c in range(4):
                dve.wait_ge(s("sm_qn"), c + 1)
                last = v.tensor_reduce(sm_o[:, c, :], sm_kv[c].rearrange("p (d v) -> p v d", v=HD), AX.X, ALU.add)
            seq(last)
            seq(v.tensor_reduce(sm_x[:, 1, :], sm_o.rearrange("p c v -> p v c"), AX.X, ALU.add))
            head_norm(sm_x[:, 1, :], sm_x[:, 2, :], sm_x[:, 3, :], SR, 1).then_inc(s("sm_var"), 1)
            dve.wait_ge(s("a_sq"), 5)
            for f in range(4):
                v.tensor_scalar(y_feat[:, f, :], y_feat[:, f, :], norms[:, 0, f:f + 1], None, ALU.mult).then_inc(s("d_yn"), 1)
            v.memset(stat[:, 4, :], 1.0).then_inc(s("d_statz"), 1)
            dve.wait_ge(s("a_sd"), 5)
            seq(v.reciprocal(hst[0:SR, 3, 0:1], hst[0:SR, 2, 0:1]))
            v.tensor_scalar(sm_x[:, 0, :], sm_x[:, 2, :], hst[0:SR, 3, 0:1], None, ALU.mult).then_inc(s("sm_on"), 1)
            dve.wait_ge(s("ld_oex"), 16)
            dve.wait_ge(s("pe_yrt"), 4)
            tt(on1[0:NS, :], o_ex, gate_tok[0:NS, TE, :], ALU.mult).then_inc(s("d_yr"), 1)
            dve.wait_ge(s("a_rs5"), 1)
            seq(v.reciprocal(stat[:, 5, 0:NT], stat[:, 4, 0:NT]))
            for n_, i in enumerate(LATE):
                r_ = NS if i == TE else P
                b = 4 * (n_ % 2)
                dve.wait_ge(s("pe_out"), n_ + 1)
                dve.wait_ge(s(f"ld_tok{i}"), 48 if i == TE else 32)
                for hf in range(2):
                    cl = slice(512 * hf, 512 * hf + 512)
                    seq(tt(acc[0:r_, i, cl], acc[0:r_, i, cl], bank[b + 2 + hf][0:r_, :], ALU.add))
                    last = v.scalar_tensor_tensor(acc[0:r_, i, cl], bank[b + hf][0:r_, :], stat[0:r_, 5, i:i + 1],
                                                  acc[0:r_, i, cl], ALU.mult, ALU.add)
                    if hf == 0:
                        seq(last)
                last.then_inc(s("d_x2"), 1)
                dve.wait_ge(s("a_rt2"), n_ + 1)
                if n_ == 0:
                    dve.wait_ge(s("ld_gain"), 32)
                seq(v.reciprocal(stat[0:r_, 10, i:i + 1], stat[0:r_, 9, i:i + 1]))
                v.scalar_tensor_tensor(h2p[0:r_, n_ % 2, :].rearrange("t (k p) -> t p k", k=KD),
                                       acc[0:r_, i, :].rearrange("t (p k) -> t p k", k=KD), stat[0:r_, 10, i:i + 1],
                                       gain2[0:r_, :].rearrange("t (p k) -> t p k", k=KD),
                                       ALU.mult, ALU.mult).then_inc(s("d_h2"), 1)
            moe_dve(dve)

        @block.tensor
        def _(pe):
            def mm(o, l, r, start, stop, **kw):
                return nc.tensor.matmul(o, l, r, start=start, stop=stop, skip_group_check=True, **kw)

            pe.wait_ge(s("ld_id"), 16)
            for n_, i in enumerate(EARLY):
                r = XR if i == TE else P
                pe.wait_ge(s("d_xn"), n_ + 1)
                for hf in range(2):
                    if n_ >= 2:
                        pe.wait_ge(s("a_ht"), 2 * (n_ - 2) + hf + 1)
                    for k in range(4):
                        kk = 4 * hf + k
                        t = nc.tensor.transpose(bank[2 * (n_ % 2) + hf][:, P * k:P * k + r],
                                                xn_bufs[0:r, n_ % 2, P * kk:P * kk + P], ident[0:r, 0:r])
                    t.then_inc(s("pe_xt"), 1)
            pe.wait_ge(s("a_ht"), 10)
            w = lambda buf: wbuf[:, 4096 * buf:4096 * (buf + 1)].rearrange("p (k n) -> p k n", k=KD)
            pe.wait_ge(s("ld_wbuf0"), 16)
            for ft in range(4):
                if ft >= 2:
                    pe.wait_ge(s("a_u"), ft - 1)
                for c0, c1, b in ((0, SEQ, 4), (SEQ, TC, 5)):
                    for k in range(KD):
                        t = mm(bank[b + 2 * (ft % 2)][:, 0:c1 - c0], w(0)[:, k, P * ft:P * ft + P],
                               hT[:, k, c0:c1], k == 0, k == KD - 1)
                t.then_inc(s("pe_u"), 1)

            def proj_tile(name, load, buf, evac, n_):
                if n_ == 0:
                    pe.wait_ge(s(f"ld_wbuf{buf}"), 16 * load)
                if n_ >= 2:
                    pe.wait_ge(s(evac), n_ - 1)
                i_ = TILES[n_]
                r_ = XR if i_ == TE else P
                for k_ in range(KD):
                    t_ = mm(bank[n_ % 2][0:r_, :], hT[:, k_, P * i_:P * i_ + r_], w(buf)[:, k_, :],
                            k_ == 0, k_ == KD - 1)
                t_.then_inc(s(name), 1)

            def k_after(n_):
                i_ = TILES[n_]
                rot, kd = rotd[n_ % 2], kdec[:, n_ % 2, :]
                pe.wait_ge(s("d_k"), n_ + 1)
                if i_ != TE:
                    if n_ >= 2:
                        pe.wait_ge(s("a_kt"), n_ - 1)
                    for a_ in range(4):
                        t_ = nc.tensor.transpose(bank[6][:, P * a_:P * a_ + P], rot[:, P * a_:P * a_ + P], ident[:])
                    t_.then_inc(s("pe_kt"), 1)
                pe.wait_ge(s("d_kd"), n_ + 1)
                if n_ == 0:
                    pe.wait_ge(s("a_v2"), NT)
                if n_ >= 1:
                    pe.wait_ge(s("d_st"), n_)
                r_ = slice(XM, XR) if i_ == TE else slice(0, P)
                for a_ in range(4):
                    t_ = mm(bank[7][:, P * a_:P * a_ + P], kd[r_, P * a_:P * a_ + P],
                            v_tok[r_, i_, P * a_:P * a_ + P], True, True)
                t_.then_inc(s("pe_st"), 1)

            def q_after(n_):
                if n_ == 0:
                    return
                c = n_ - 1
                pe.wait_ge(s("d_q"), n_ + 1)
                if c >= 1:
                    pe.wait_ge(s("a_qt"), c)
                for a_ in range(4):
                    t_ = nc.tensor.transpose(bank[6][:, P * a_:P * a_ + P], rotd[n_ % 2][:, P * a_:P * a_ + P], ident[:])
                t_.then_inc(s("pe_qt"), 1)
                pe.wait_ge(s("a_qt"), c + 1)
                if c == 3:
                    pe.wait_ge(s("ld_glu"), 16)
                    pe.wait_ge(s("a_gelu"), 1)
                    glu_tile(0)
                q_ = qT[:, c % 2]
                for hs in range(2):
                    if c >= 1:
                        pe.wait_ge(s("d_pr"), 2 * (c - 1) + hs + 1)
                    r_ = slice(HD * hs, HD * hs + HD)
                    for j_ in range(4):
                        t_ = mm(bank[2 + hs][:, P * j_:P * j_ + P], kT[r_, j_, P * c:P * c + P],
                                q_[r_, j_, :], True, True)
                    t_.then_inc(s("pe_sc"), 1)
                if c >= 1:
                    yr_transposes(c - 1)
                o = bank[4 + c % 2]
                for a_ in range(4):
                    mm(o[:, P * a_:P * a_ + P], q_[:, a_, :], state_bd[:, c, a_, :], a_ == 0, False)
                for hs in range(2):
                    pe.wait_ge(s("d_pr"), 2 * c + hs + 1)
                    for j_ in range(4):
                        h = 2 * j_ + hs
                        t_ = mm(o[:, HD * h:HD * h + HD], probs[:, hs, P * j_:P * j_ + P],
                                v_tok[:, c, HD * h:HD * h + HD], False, h == H - 1)
                t_.then_inc(s("pe_o"), 1)

            def glu_tile(f):
                for c0, c1, o_ in ((0, SEQ, bank[f][:, :]), (SEQ, TT, bank[6][:, NS * f:NS * f + NS])):
                    for k_ in range(4):
                        t_ = mm(o_, w_glu[:, k_, P * f:P * f + P], y_feat[:, k_, c0:c1], k_ == 0, k_ == 3)
                t_.then_inc(s("pe_glu"), 1)

            def yr_transposes(k_):
                r_ = NS if k_ == 4 else P
                pe.wait_ge(s("d_yr"), k_ + 1)
                if k_ >= 1:
                    pe.wait_ge(s("a_yr"), k_)
                for a_ in range(4):
                    t_ = nc.tensor.transpose(bank[7][:, P * a_:P * a_ + r_], on1[0:r_, P * a_:P * a_ + P],
                                             ident[0:r_, 0:r_])
                t_.then_inc(s("pe_yrt"), 1)

            def s5_prep(half):
                pe.wait_ge(s("d_tab"), half + 1)
                for n_ in range(2):
                    for g in range(4 * n_, 4 * n_ + 4):
                        o = bank[n_][:, 128 * (g - 4 * n_):128 * (g - 4 * n_) + 128]
                        c = slice(128 * g, 128 * g + 128)
                        mm(o, vt_re[:, c], wt_re[:, c], True, False)
                        t = mm(o, vt_im[:, c], wt_im[:, c], False, True)
                    t.then_inc(s("pe_m"), 1)
                for n_ in range(4):
                    for g in range(4):
                        c = 512 * (n_ % 2) + 128 * g
                        t = nc.tensor.transpose(bank[2 + n_][:, 128 * g:128 * g + 128],
                                                (vt_re, vt_im)[n_ // 2][:, c:c + 128], ident[:])
                    t.then_inc(s("pe_vt"), 1)
                pe.wait_ge(s("a_v"), 4 * (half + 1))
                pe.wait_ge(s("a_uc"), 1)
                pe.wait_ge(s("d_uc"), 1)
                for n_ in range(6):
                    g0, g1 = 3 * (n_ % 3), min(3 * (n_ % 3) + 3, HG)
                    for g in range(g0, g1):
                        t = mm(bank[2 + n_][:, NCS * (g - g0):NCS * (g - g0 + 1)],
                               (v_re, v_im)[n_ // 3][:, 128 * g:128 * g + 128], u_chunk[:, HG * half + g, :], True, True)
                    t.then_inc(s("pe_s"), 1)

            def s5_out(half):
                pe.wait_ge(s("z_ready"), half + 1)
                pe.wait_ge(s("d_m"), half + 1)
                for n_ in range(3):
                    g0, g1 = 3 * n_, min(3 * n_ + 3, HG)
                    for g in range(g0, g1):
                        o = bank[2 + n_][:, NCS * (g - g0):NCS * (g - g0 + 1)]
                        c = slice(128 * g, 128 * g + 128)
                        z = slice(NCS * g, NCS * g + NCS)
                        mm(o, m_mat[:, c], u_chunk[:, HG * half + g, :], True, False)
                        mm(o, wt_re[:, c], rot_re[:, z], False, False)
                        t = mm(o, wt_im[:, c], rot_im[:, z], False, True)
                    t.then_inc(s("pe_y"), 1)

            pe.wait_ge(s("a_u"), 4)
            s5_prep(0)
            pe.wait_ge(s("d_m"), 1)
            for n_ in range(NT):
                proj_tile("pe_v", 1, 1, "a_v2", n_)
            pe.wait_ge(s("a_s"), 6)
            pe.wait_ge(s("a_v2"), NT)
            for n_ in range(NT):
                proj_tile("pe_k", 2, 0, "d_k", n_)
                if n_ >= 1:
                    k_after(n_ - 1)
            k_after(NT - 1)
            s5_out(0)
            pe.wait_ge(s("a_y"), 1)
            pe.wait_ge(s("d_k"), NT)
            for n_ in range(3):
                proj_tile("pe_g", 2, 1, "a_g", n_)
            pe.wait_ge(s("a_g"), 3)
            pe.wait_ge(s("a_kt"), 4)
            pe.wait_ge(s("d_st"), NT)
            s5_prep(1)
            pe.wait_ge(s("d_m"), 2)
            for n_ in range(3, NT):
                proj_tile("pe_g", 2, 1, "a_g", n_)
            pe.wait_ge(s("a_g"), NT)
            for n_ in range(2):
                proj_tile("pe_q", 3, 0, "d_q", n_)
            pe.wait_ge(s("a_s"), 12)
            s5_out(1)
            pe.wait_ge(s("a_y"), 2)
            for n_ in range(2, NT):
                proj_tile("pe_q", 3, 0, "d_q", n_)
                q_after(n_ - 1)
            q_after(NT - 1)
            pe.wait_ge(s("d_pr"), 8)
            for f in range(1, 4):
                glu_tile(f)
            yr_transposes(3)
            pe.wait_ge(s("a_yr"), 4)
            pe.wait_ge(s("ld_wbuf0"), 64)
            pe.wait_ge(s("a_tanh"), 5)
            wo = [wbuf[:, 4096:].rearrange("p (k n) -> p k n", k=4), wbuf[:, 0:4096].rearrange("p (k n) -> p k n", k=4)]

            def out_part(n_, part):
                i_ = LATE[n_]
                r_ = NS if i_ == TE else P
                y = (y_feat, yr_feat)[part]
                for k in range(4):
                    for hf in range(2):
                        t_ = mm(bank[4 * (n_ % 2) + 2 * part + hf][0:r_, :], y[:, k, P * i_:P * i_ + r_],
                                wo[part][:, k, 512 * hf:512 * hf + 512], k == 0, k == 3)
                return t_

            out_part(0, 1)
            pe.wait_ge(s("a_sq"), 5)
            pe.wait_ge(s("d_yr"), 4)
            for n_, i in enumerate(TILES):
                r = NS if i == TE else P
                for f in range(4):
                    t = mm(bank[4][0:r, i:i + 1], glu_sq[:, f, P * i:P * i + r], ones_col[:, 0:1], f == 0, f == 3)
            t.then_inc(s("pe_ss"), 1)
            pe.wait_ge(s("d_yn"), 4)
            pe.wait_ge(s("ld_wbuf1"), 48)
            out_part(0, 0).then_inc(s("pe_out"), 1)
            yr_transposes(4)
            pe.wait_ge(s("a_rs5"), 1)
            pe.wait_ge(s("a_yr"), NT)

            def h2_transposes(n_):
                i_ = LATE[n_]
                r_ = NS if i_ == TE else P
                pe.wait_ge(s("d_h2"), n_ + 1)
                for hf_ in range(2):
                    for k_ in range(4):
                        kk = 4 * hf_ + k_
                        t_ = nc.tensor.transpose(bank[4 * (n_ % 2) + hf_][:, P * k_:P * k_ + r_],
                                                 h2p[0:r_, n_ % 2, P * kk:P * kk + P], ident[0:r_, 0:r_])
                    t_.then_inc(s("pe_h2t"), 1)

            for n_ in range(1, NT):
                out_part(n_, 1)
                if n_ >= 2:
                    pe.wait_ge(s("a_h2t"), 2 * (n_ - 1))
                out_part(n_, 0).then_inc(s("pe_out"), 1)
                h2_transposes(n_ - 1)
            sh_up, sh_down = shared_pe(pe)
            pe.wait_ge(s("w_shared"), 48)
            pe.wait_ge(s("a_h2t"), 2)
            sh_up(0)
            h2_transposes(NT - 1)
            moe_pe(pe, sh_up, sh_down)


_INS = ["x_prompt", "x_sample", "meta_tokens", "norm1", "w_in", "w_router", "router_bias", "w_gate_e", "w_up_e",
        "w_down_e", "w_gate_sh", "w_up_sh", "w_down_sh", "s5_w_glu", "w_out", "norm2", "final_norm", "state_ret"]


def shape_constants():
    c = {}
    c["c_ident"] = np.eye(P, dtype=np.float32)
    t = np.arange(P)
    c["c_mask_m"] = (t[None, :] // 32 >= t[:, None] // 32).astype(np.float32)
    bf16_bits = lambda w: (np.ascontiguousarray(w, np.float32).view(np.uint32) >> 16).astype(np.uint16)
    tri = np.zeros((P, 2, P), np.float32)
    tri[:, 0] = (t[:, None] < t[None, :])
    tri[:, 1] = 1
    c["c_tri"] = bf16_bits(tri)
    c["c_iota"] = bf16_bits(np.broadcast_to(np.arange(P, dtype=np.float32), (P, P)))
    half = HD // 2
    inv = np.float32(10000.0) ** (-np.arange(half, dtype=np.float32) / np.float32(half))
    pos = np.zeros((P, NT), np.float32)
    for i in range(4):
        pos[:, i] = NMETA + i * P + t
    pos[0:NS, TE] = PAST
    pos[XM:XR, TE] = np.arange(NMETA)
    ang = (pos[:, :, None] * inv[None, None, :]).astype(np.float32)
    co, si = np.cos(ang), np.sin(ang)
    c["c_cosin"] = np.ascontiguousarray(np.stack([co, si], 1)
                                        ).astype(np.float32)
    lg = np.log1p(-np.exp2(-5.0 - np.arange(H)))
    sc = HD ** -0.5
    m = (t[None, None, :] >= t[:, None, None]) * np.exp(-lg[None, :, None] * (t[:, None, None] + 1.0)) * sc
    c["c_mask_dec"] = m.reshape(P, 4, 2, P).swapaxes(1, 2).reshape(P, H * P).astype(np.float32)
    dec = np.zeros((P, 4, H))
    dec[:, 0] = np.exp(lg[None] * (P - 1.0 - t[:, None])) * sc
    dec[XM:XR, 1] = np.exp(lg[None] * (NMETA - 1.0 - np.arange(NMETA)[:, None])) * sc
    dec[:, 2] = np.exp(lg[None] * (t[:, None] + 1.0))
    dec[0:NS * H, 3, 0] = np.tile(np.exp(lg), NS)
    dec[0:NS * H, 3, 1] = sc
    c["c_dec"] = dec.astype(np.float32)
    c["c_gam"] = np.exp(P * lg).reshape(4, 2).repeat(HD, 1).T.astype(np.float32)
    r = np.zeros((P, 16), np.float32)
    r[:, 0] = TT + t
    r[:, 1:5] = 1
    r[0:NS, 5] = 1
    r[:, 6] = t
    c["c_route"] = r
    i8 = np.arange(8)
    c["c_tri8"] = np.broadcast_to((i8[None, :] < i8[:, None]).astype(np.float32).reshape(64), (P, 64)).copy()
    return c


_OUTS = {
    "y_prompt": (1, SEQ, D), "y_sample": (NS, 1, D), "s5_states": (P, 2, GP, 1 + NS), "ret_prompt": (2, HD, 4, HD),
    "ret_sample": (NS * H, HD * HD),
}


def kernel(**inputs):
    import concourse.bacc as _bacc
    from concourse.bass_utils import run_bass_kernel_spmd as _run

    a = {k: np.asarray(v) for k, v in inputs.items()}
    feed = {k: a[k] for k in _INS}
    pair = lambda w: np.ascontiguousarray(w.reshape((GP, 2) + w.shape[1:]).swapaxes(0, 1))
    lamT = [pair(w[0]).transpose(0, 2, 1).reshape(P, GP) for w in (a["s5_lam_re"], a["s5_lam_im"])]
    ldt = np.broadcast_to(a["s5_log_dt"][0].reshape(GP, 2).T[:, None, :], (2, NST, GP)).reshape(P, GP)
    feed["lam"] = np.stack(lamT + [ldt], 1)
    bs = [pair(w[0]).transpose(0, 2, 1, 3).reshape(P, GP, 16) for w in (a["s5_b_re"], a["s5_b_im"])]
    cs = [pair(w[0]).transpose(0, 3, 1, 2).reshape(P, GP, 16) for w in (a["s5_c_re"], a["s5_c_im"])]
    feed["bc"] = np.stack(bs + cs, 1)
    d = a["s5_d"][0].reshape(GP, 2 * 16).T
    feed["dskip"] = np.tile(d, (L, 1))
    xs = [w[0].reshape(NS, GP, 2, NST).transpose(2, 3, 1, 0).reshape(P, GP, NS)
          for w in (a["state_s5_re"], a["state_s5_im"])]
    feed["xs0"] = np.stack(xs, 1)
    feed["norms"] = np.stack([a["s5_norm"][0].reshape(4, P).T, a["ret_norm"][0].reshape(4, P).T,
                              a["ret_norm"][0].reshape(4, P).T], 1)
    feed.update(shape_constants())
    nc = _bacc.Bacc("TRN2", target_bir_lowering=False, num_devices=1)
    arrays, ins, outs = {}, {}, {}
    for k, w in feed.items():
        w = np.ascontiguousarray(w)
        arrays[f"in_{k}"] = w
        ins[k] = nc.dram_tensor(f"in_{k}", w.shape, mybir.dt.from_np(w.dtype), kind="ExternalInput").ap()
    for k, shape in _OUTS.items():
        outs[k] = nc.dram_tensor(f"out_{k}", shape, F32, kind="ExternalOutput").ap()
    kernel_program(nc, ins, outs)
    r = _run(nc, [arrays], core_ids=[0]).results[0]
    g = {k: np.asarray(r[f"out_{k}"]) for k in _OUTS}
    s5 = lambda w: w.reshape(2, NST, GP, -1).transpose(3, 2, 0, 1).reshape(1, -1, NG, NST)
    fin = g["s5_states"]
    return (g["y_prompt"], g["y_sample"], s5(fin[:, 0, :, 0:1]), s5(fin[:, 1, :, 0:1]),
            g["ret_prompt"].transpose(2, 0, 1, 3).reshape(1, 1, H, HD, HD),
            s5(fin[:, 0, :, 1:]), s5(fin[:, 1, :, 1:]), g["ret_sample"].reshape(1, NS, H, HD, HD))
```
